# Optimizing a Trainium2 kernel written in Bass

```python
import math
import jax, jax.numpy as jnp
from jax import lax
import numpy as np

D_MODEL = 1024
BATCH = 1
SEQ = 1024
DEPTH = 1

HEAD_DIM = 64
ATT_GROUPS = ((128, 1), (512, 4), (2048, 16))
HEADS_PER_GROUP = 4
N_ATT_HEADS = HEADS_PER_GROUP * len(ATT_GROUPS)
ATT_WIDTH = N_ATT_HEADS * HEAD_DIM
ATT_MERGED = HEADS_PER_GROUP * HEAD_DIM
BLK = 128
POOL_WINDOWS = (2, 4, 8, 16)
POOL_GROUP_WIDTH = 3 * D_MODEL // 16
POOL_WIDTH = POOL_GROUP_WIDTH * len(POOL_WINDOWS)
D_FF = 4 * D_MODEL
N_IN = 3 * ATT_WIDTH + POOL_WIDTH + 2 * D_MODEL
NORM_EPS = 1e-6
ALIBI_MAX_BIAS = 8.0


def _rmsnorm(x, g):
    xf = x.astype(jnp.float32)
    y = xf * lax.rsqrt(jnp.mean(xf * xf, axis=-1, keepdims=True) + NORM_EPS)
    return (y * g.astype(jnp.float32)).astype(x.dtype)

def _dilated_window_attention(q, k, v, dilation, n_steps, slopes):
    B, S, H, Dh = q.shape
    L = S // dilation
    nb = -(-L // BLK)
    Lp = nb * BLK
    Z = B * dilation

    def to_sub(t):
        t = t.reshape(B, L, dilation, H, Dh).transpose(0, 2, 1, 3, 4).reshape(Z, L, H, Dh)
        return jnp.pad(t, ((0, 0), (0, Lp - L), (0, 0), (0, 0)))

    def band(t):
        prev = jnp.pad(t, ((0, 0), (BLK, 0), (0, 0), (0, 0)))[:, :Lp]
        return jnp.concatenate([prev.reshape(Z, nb, BLK, H, Dh),
                                t.reshape(Z, nb, BLK, H, Dh)], axis=2)

    qb = to_sub(q).reshape(Z, nb, BLK, H, Dh).astype(jnp.float32)
    kb = band(to_sub(k)).astype(jnp.float32)
    vb = band(to_sub(v)).astype(jnp.float32)

    s = jnp.einsum('znqhd,znkhd->znhqk', qb, kb) * (Dh ** -0.5)
    steps = BLK + jnp.arange(BLK)[:, None] - jnp.arange(2 * BLK)[None, :]
    key_idx = (jnp.arange(nb)[:, None, None] * BLK
               + jnp.arange(2 * BLK)[None, None, :] - BLK)
    valid = (steps >= 0) & (steps <= n_steps) & (key_idx >= 0)
    bias = -(slopes[:, None, None] * (steps * dilation).astype(jnp.float32))
    s = jnp.where(valid[None, :, None], s + bias[None, None], -jnp.inf)
    lse = jax.nn.logsumexp(s, axis=-1)
    p = jnp.exp(s - lse[..., None])
    o = jnp.einsum('znhqk,znkhd->znqhd', p, vb).reshape(Z, Lp, H, Dh)[:, :L]
    lse = lse.transpose(0, 1, 3, 2).reshape(Z, Lp, H)[:, :L]
    o = o.reshape(B, dilation, L, H, Dh).transpose(0, 2, 1, 3, 4).reshape(B, S, H, Dh)
    lse = lse.reshape(B, dilation, L, H).transpose(0, 2, 1, 3).reshape(B, S, H)
    return o, lse

def _attention_branch(q, k, v):
    B, S, _ = q.shape
    q = q.reshape(B, S, N_ATT_HEADS, HEAD_DIM)
    k = k.reshape(B, S, N_ATT_HEADS, HEAD_DIM)
    v = v.reshape(B, S, N_ATT_HEADS, HEAD_DIM)
    slopes = 2.0 ** (-ALIBI_MAX_BIAS * (jnp.arange(N_ATT_HEADS, dtype=jnp.float32) + 1.0)
                     / N_ATT_HEADS)
    outs, lses = [], []
    for g, (window, dilation) in enumerate(ATT_GROUPS):
        hs = slice(g * HEADS_PER_GROUP, (g + 1) * HEADS_PER_GROUP)
        o, l = _dilated_window_attention(q[:, :, hs], k[:, :, hs], v[:, :, hs],
                                         dilation, window // dilation, slopes[hs])
        outs.append(o)
        lses.append(l)
    outs = jnp.stack(outs, axis=0)
    wts = jax.nn.softmax(jnp.stack(lses, axis=0), axis=0)
    merged = jnp.sum(wts[..., None] * outs, axis=0)
    return merged.reshape(B, S, ATT_MERGED)

def _pool_branch(pz, w_grp, scale):
    B, S, _ = pz.shape
    pf = pz.astype(jnp.float32).reshape(B, S, len(POOL_WINDOWS), POOL_GROUP_WIDTH)
    c0 = jnp.pad(jnp.cumsum(pf, axis=1), ((0, 0), (1, 0), (0, 0), (0, 0)))
    t = jnp.arange(S)
    pooled = []
    for g, w in enumerate(POOL_WINDOWS):
        lower = jnp.take(c0[:, :, g], jnp.maximum(t + 1 - w, 0), axis=1)
        count = jnp.minimum(t + 1, w).astype(jnp.float32)[None, :, None]
        pooled.append((c0[:, 1:, g] - lower) / count)
    pooled = jnp.stack(pooled, axis=2) - pf
    mixed = jnp.einsum('bsgc,gcd->bsgd', pooled, w_grp.astype(jnp.float32))
    return mixed.reshape(B, S, POOL_WIDTH) * scale.astype(jnp.float32)

def first_inputs(seed: int = 0) -> dict:
    key = jax.random.key(seed)
    ks = jax.random.split(key, 12)
    f32 = jnp.float32

    def nrm(k, shape, fan_in):
        return jax.random.normal(k, shape, f32) * (fan_in ** -0.5)

    def gain(k, shape):
        return 1.0 + 0.02 * jax.random.normal(k, shape, f32)

    return {
        "x": jax.random.normal(ks[0], (BATCH, SEQ, D_MODEL), f32),
        "norm_mix_g": gain(ks[1], (DEPTH, D_MODEL)),
        "w_in": nrm(ks[2], (DEPTH, D_MODEL, N_IN), D_MODEL),
        "w_att_out": nrm(ks[3], (DEPTH, ATT_MERGED, D_MODEL), ATT_MERGED),
        "w_pool_grp": nrm(ks[4], (DEPTH, len(POOL_WINDOWS), POOL_GROUP_WIDTH, POOL_GROUP_WIDTH),
                          POOL_GROUP_WIDTH),
        "pool_scale": 1.0 + 0.1 * jax.random.normal(ks[5], (DEPTH, POOL_WIDTH), f32),
        "w_pool_out": nrm(ks[6], (DEPTH, POOL_WIDTH, D_MODEL), POOL_WIDTH),
        "w_out": nrm(ks[7], (DEPTH, D_MODEL, D_MODEL), D_MODEL),
        "norm_mlp_g": gain(ks[8], (DEPTH, D_MODEL)),
        "w_mlp_in": nrm(ks[9], (DEPTH, D_MODEL, D_FF), D_MODEL),
        "w_mlp_out": nrm(ks[10], (DEPTH, D_FF, D_MODEL), D_FF),
        "norm_final_g": gain(ks[11], (D_MODEL,)),
    }

def first_block(x, norm_mix_g, w_in, w_att_out, w_pool_grp, pool_scale, w_pool_out, w_out,
              norm_mlp_g, w_mlp_in, w_mlp_out, norm_final_g):
    dt = x.dtype
    offs = np.cumsum([ATT_WIDTH, ATT_WIDTH, ATT_WIDTH, POOL_WIDTH, D_MODEL]).tolist()
    h = x
    for l in range(DEPTH):
        u = _rmsnorm(h, norm_mix_g[l])
        z = jnp.einsum('bsd,dn->bsn', u, w_in[l])
        q, k, v, pz, ga, gp = jnp.split(z, offs, axis=-1)
        a = _attention_branch(q, k, v).astype(dt)
        p = _pool_branch(pz, w_pool_grp[l], pool_scale[l]).astype(dt)
        merged = (jax.nn.sigmoid(ga) * jnp.einsum('bsc,cd->bsd', a, w_att_out[l])
                  + jax.nn.sigmoid(gp) * jnp.einsum('bsc,cd->bsd', p, w_pool_out[l]))
        h = h + jnp.einsum('bsd,de->bse', merged, w_out[l])
        m = _rmsnorm(h, norm_mlp_g[l])
        hid = jnp.square(jax.nn.relu(jnp.einsum('bsd,df->bsf', m, w_mlp_in[l])))
        h = h + jnp.einsum('bsf,fd->bsd', hid, w_mlp_out[l])
    return _rmsnorm(h, norm_final_g)


GRID_W = 64
N_ATT_HEADS_2 = 8
ATT_HEAD_DIM = 64
D_ATT = N_ATT_HEADS_2 * ATT_HEAD_DIM
WIN_H_MAX = 8
WIN_W = 16
Q_BLOCK_W = 16
KV_BLOCK_W = Q_BLOCK_W + WIN_W
N_COL_BLOCKS = GRID_W // Q_BLOCK_W
D_REC = D_MODEL
N_REC_BLOCKS = 16
REC_BLOCK = D_REC // N_REC_BLOCKS
CONV_W = 4
LRU_C = 8.0
N_DIR = 2
D_FF_2 = 4 * D_MODEL
EPS = 1e-6
D_IN = 3 * D_ATT + 2 * D_REC + 2 * D_MODEL
SPLITS = [int(v) for v in np.cumsum([D_ATT, D_ATT, D_ATT, D_REC, D_REC, D_MODEL])]


def rms_norm(x, g):
    x32 = x.astype(jnp.float32)
    y = x32 * lax.rsqrt(jnp.mean(x32 * x32, axis=-1, keepdims=True) + EPS)
    return (y * g.astype(jnp.float32)).astype(x.dtype)

def neighbourhood_attention(q, k, v, rpb):
    b, s, h, dh = q.shape
    rows = s // GRID_W
    kh = min(WIN_H_MAX, rows)
    r = np.arange(rows)
    row_start = np.clip(r - kh // 2, 0, rows - kh)
    row_idx = row_start[:, None] + np.arange(kh)[None, :]
    n = np.arange(N_COL_BLOCKS)
    col_start = np.clip(n * Q_BLOCK_W - WIN_W // 2, 0, GRID_W - KV_BLOCK_W)
    col_idx = col_start[:, None] + np.arange(KV_BLOCK_W)[None, :]
    qc = n[:, None] * Q_BLOCK_W + np.arange(Q_BLOCK_W)[None, :]
    win_start = np.clip(qc - WIN_W // 2, 0, GRID_W - WIN_W)
    kc = col_idx[:, None, :]
    valid = (kc >= win_start[..., None]) & (kc < win_start[..., None] + WIN_W)
    d_row = row_idx - r[:, None] + (WIN_H_MAX - 1)
    d_col = np.clip(kc - qc[..., None], -(WIN_W - 1), WIN_W - 1) + (WIN_W - 1)

    scale = ATT_HEAD_DIM ** -0.5
    q_blk = (q * scale).reshape(b, rows, N_COL_BLOCKS, Q_BLOCK_W, h, dh).transpose(0, 4, 1, 2, 3, 5)
    k_grid = k.reshape(b, rows, GRID_W, h, dh).transpose(0, 3, 1, 2, 4)
    v_grid = v.reshape(b, rows, GRID_W, h, dh).transpose(0, 3, 1, 2, 4)
    ri = row_idx[:, None, :, None]
    ci = col_idx[None, :, None, :]
    kg = k_grid[:, :, ri, ci]
    vg = v_grid[:, :, ri, ci]

    scores = jnp.einsum('bhrnqd,bhrnikd->bhrnqik', q_blk, kg).astype(jnp.float32)
    bias = rpb.astype(jnp.float32)[:, d_row[:, None, None, :, None], d_col[None, :, :, None, :]]
    scores = scores + bias[None]
    scores = jnp.where(valid[:, :, None, :], scores, -1e30)
    probs = jax.nn.softmax(scores, axis=(-2, -1)).astype(v.dtype)
    out = jnp.einsum('bhrnqik,bhrnikd->bhrnqd', probs, vg)
    return out.transpose(0, 2, 3, 4, 1, 5).reshape(b, s, h * dh)

def centred_depthwise_conv(u, w, bias):
    s = u.shape[1]
    left = CONV_W // 2
    right = CONV_W - 1 - left
    up = jnp.pad(u, ((0, 0), (left, right), (0, 0)))
    out = bias
    for j in range(CONV_W):
        out = out + up[:, j:j + s] * w[j]
    return out

def block_diag_linear(u, w, b):
    bsz, s, c = u.shape
    ub = u.reshape(bsz, s, N_REC_BLOCKS, REC_BLOCK)
    return jnp.einsum('bsnc,ncd->bsnd', ub, w).reshape(bsz, s, c) + b

def rg_lru(u, w_a, b_a, w_i, b_i, lam, reverse):
    r_gate = jax.nn.sigmoid(block_diag_linear(u, w_a, b_a)).astype(jnp.float32)
    i_gate = jax.nn.sigmoid(block_diag_linear(u, w_i, b_i))
    log_a = -LRU_C * r_gate * jax.nn.softplus(-lam.astype(jnp.float32))
    a = jnp.exp(log_a)
    mult = jnp.sqrt(jnp.maximum(-jnp.expm1(2.0 * log_a), 0.0))
    bx = mult * (i_gate * u).astype(jnp.float32)

    def combine(c1, c2):
        a1, b1 = c1
        a2, b2 = c2
        return a1 * a2, a2 * b1 + b2

    _, h = lax.associative_scan(combine, (a, bx), axis=1, reverse=reverse)
    return h.astype(u.dtype)

def second_inputs(seed: int = 0) -> dict:
    key = jax.random.key(seed)
    ks = jax.random.split(key, 20)
    f32 = jnp.float32
    nrm = lambda k, shape, fan_in: jax.random.normal(k, shape, f32) * (fan_in ** -0.5)
    x = jax.random.normal(ks[0], (BATCH, SEQ, D_MODEL), f32)
    ln1_g = 1.0 + 0.05 * jax.random.normal(ks[1], (DEPTH, D_MODEL), f32)
    w_in = nrm(ks[2], (DEPTH, D_MODEL, D_IN), D_MODEL)
    b_in = 0.02 * jax.random.normal(ks[3], (DEPTH, D_IN), f32)
    rpb = 0.02 * jax.random.normal(ks[4], (DEPTH, N_ATT_HEADS_2, 2 * WIN_H_MAX - 1, 2 * WIN_W - 1), f32)
    w_att_o = nrm(ks[5], (DEPTH, D_ATT, D_MODEL), D_ATT)
    conv_w = nrm(ks[6], (DEPTH, CONV_W, D_REC), CONV_W)
    conv_b = 0.02 * jax.random.normal(ks[7], (DEPTH, D_REC), f32)
    w_rg_a = nrm(ks[8], (DEPTH, N_DIR, N_REC_BLOCKS, REC_BLOCK, REC_BLOCK), REC_BLOCK)
    b_rg_a = 0.02 * jax.random.normal(ks[9], (DEPTH, N_DIR, D_REC), f32)
    w_rg_i = nrm(ks[10], (DEPTH, N_DIR, N_REC_BLOCKS, REC_BLOCK, REC_BLOCK), REC_BLOCK)
    b_rg_i = 0.02 * jax.random.normal(ks[11], (DEPTH, N_DIR, D_REC), f32)
    a_c = jax.random.uniform(ks[12], (DEPTH, N_DIR, D_REC), f32, 0.9, 0.999)
    a0 = a_c ** (1.0 / LRU_C)
    lru_lambda = jnp.log(a0) - jnp.log1p(-a0)
    w_rec_o = nrm(ks[13], (DEPTH, D_REC, D_MODEL), D_REC)
    w_out = nrm(ks[14], (DEPTH, D_MODEL, D_MODEL), D_MODEL)
    ln2_g = 1.0 + 0.05 * jax.random.normal(ks[15], (DEPTH, D_MODEL), f32)
    w_ff1 = nrm(ks[16], (DEPTH, D_MODEL, D_FF_2), D_MODEL)
    w_ff2 = nrm(ks[17], (DEPTH, D_FF_2, D_MODEL), D_FF_2)
    lnf_g = 1.0 + 0.05 * jax.random.normal(ks[18], (D_MODEL,), f32)
    return {"x": x, "ln1_g": ln1_g, "w_in": w_in, "b_in": b_in, "rpb": rpb,
            "w_att_o": w_att_o, "conv_w": conv_w, "conv_b": conv_b,
            "w_rg_a": w_rg_a, "b_rg_a": b_rg_a, "w_rg_i": w_rg_i, "b_rg_i": b_rg_i,
            "lru_lambda": lru_lambda, "w_rec_o": w_rec_o, "w_out": w_out,
            "ln2_g": ln2_g, "w_ff1": w_ff1, "w_ff2": w_ff2, "lnf_g": lnf_g}

def second_block(x, ln1_g, w_in, b_in, rpb, w_att_o, conv_w, conv_b, w_rg_a, b_rg_a,
              w_rg_i, b_rg_i, lru_lambda, w_rec_o, w_out, ln2_g, w_ff1, w_ff2, lnf_g):
    b, s, _ = x.shape
    for l in range(DEPTH):
        h = rms_norm(x, ln1_g[l])
        z = h @ w_in[l] + b_in[l]
        q, k, v, u, y_branch, g_att, g_rec = jnp.split(z, SPLITS, axis=-1)

        q = q.reshape(b, s, N_ATT_HEADS_2, ATT_HEAD_DIM)
        k = k.reshape(b, s, N_ATT_HEADS_2, ATT_HEAD_DIM)
        v = v.reshape(b, s, N_ATT_HEADS_2, ATT_HEAD_DIM)
        y_att = neighbourhood_attention(q, k, v, rpb[l]) @ w_att_o[l]

        u = centred_depthwise_conv(u, conv_w[l], conv_b[l])
        h_fwd = rg_lru(u, w_rg_a[l, 0], b_rg_a[l, 0], w_rg_i[l, 0], b_rg_i[l, 0], lru_lambda[l, 0], False)
        h_bwd = rg_lru(u, w_rg_a[l, 1], b_rg_a[l, 1], w_rg_i[l, 1], b_rg_i[l, 1], lru_lambda[l, 1], True)
        y_rec = ((h_fwd + h_bwd) * jax.nn.gelu(y_branch)) @ w_rec_o[l]

        mixed = jax.nn.sigmoid(g_att) * y_att + jax.nn.sigmoid(g_rec) * y_rec
        x = x + mixed @ w_out[l]

        h2 = rms_norm(x, ln2_g[l])
        x = x + jnp.square(jax.nn.relu(h2 @ w_ff1[l])) @ w_ff2[l]
    return rms_norm(x, lnf_g)


def setup_inputs(seed=0):
    out = dict(first_inputs(seed))
    for name, value in second_inputs(seed + 1).items():
        if name != "x":
            out[name + "_2"] = value
    return out


def reference(
    x, norm_mix_g, w_in, w_att_out, w_pool_grp, pool_scale, w_pool_out, w_out, norm_mlp_g,
    w_mlp_in, w_mlp_out, norm_final_g, ln1_g_2, w_in_2, b_in_2, rpb_2, w_att_o_2, conv_w_2,
    conv_b_2, w_rg_a_2, b_rg_a_2, w_rg_i_2, b_rg_i_2, lru_lambda_2, w_rec_o_2, w_out_2, ln2_g_2,
    w_ff1_2, w_ff2_2, lnf_g_2,
):
    x = first_block(
        x, norm_mix_g, w_in, w_att_out, w_pool_grp, pool_scale, w_pool_out, w_out, norm_mlp_g,
        w_mlp_in, w_mlp_out, norm_final_g,
    )
    return second_block(
        x, ln1_g_2, w_in_2, b_in_2, rpb_2, w_att_o_2, conv_w_2, conv_b_2, w_rg_a_2, b_rg_a_2,
        w_rg_i_2, b_rg_i_2, lru_lambda_2, w_rec_o_2, w_out_2, ln2_g_2, w_ff1_2, w_ff2_2,
        lnf_g_2,
    )


_drawn_inputs = setup_inputs


def setup_inputs(seed=0):
    import zlib

    import numpy as np

    out = dict(_drawn_inputs(seed))
    spreads = {}
    factors = {'norm_mix_g': 4.162, 'norm_mlp_g': 3.072, 'rpb_2': 64.0, 'b_rg_a_2': 8.0, 'b_rg_i_2': 8.0}
    for name, (base, spread) in spreads.items():
        noise = np.random.default_rng([zlib.crc32(name.encode()), seed]).standard_normal(out[name].shape)
        drawn = base * np.exp(spread * noise) if base else spread * noise
        out[name] = __import__('jax').numpy.asarray(drawn.astype(out[name].dtype))
    for name, factor in factors.items():
        out[name] = (out[name] * factor).astype(out[name].dtype)
    return out
```

```python
from contextlib import ExitStack

import numpy as np

import concourse.bass as bass
from concourse import mybir

F32 = mybir.dt.float32
FR = mybir.dt.float32r
ALU = mybir.AluOpType
ACT = mybir.ActivationFunctionType
AXX = mybir.AxisListType.X

P = 128
S = 1024
D = 1024
KT = D // P
HC = 512
EPS = 1e-6
KB = 1024

N_PAIR1 = 6
DIL = (1, 4, 16)
SLOPE = [2.0 ** (-8.0 * (h + 1) / 12) for h in range(12)]
PW = 96
WINDOWS = (2, 4, 8, 16)
N_PAIR2 = 4
COL_START = (0, 8, 24, 32)
NEG = -1e30
BIG = 1e30
UNITS_PER_PAIR = 16

VEC = {}
_n = 0
for _name, _w in (("g_mix", 8), ("g_mlp", 8), ("g_fin", 8), ("g_ln1", 8), ("g_ln2", 8), ("g_lnf", 8),
                  ("b_in", 44), ("conv_w", 32), ("conv_b", 8), ("b_rg", 32), ("lam", 16), ("p_scale", 8)):
    VEC[_name] = _n
    _n += _w
NVEC = _n

U_ATT1, U_POOL, U_MRG1, U_OUT, U_MLP = 3 * N_PAIR1, 12, 32, 8, 64
U_ATT2, U_GATT, U_REC, U_MRG2 = 3 * N_PAIR2, 16, 24, 16


SPLIT_NORM = {0: 0, 1: 1, 3: 2, 4: 3}


class Stage:

    def __init__(self, u, t, a, d):
        self.u, self.t, self.a, self.d = u, t, a, d


STAGES = {}
_u = _t = _a = _d = 0
for _name, _nu, _na, _nd in (
        ("att1", U_ATT1, 18, 0), ("pool", U_POOL, 8, 8), ("mrg1", U_MRG1, 16, 16), ("out1", U_OUT, 0, 8),
        ("mlp1", U_MLP, 32, 64), ("att2", U_ATT2, 12, 0), ("gatt", U_GATT, 8, 8), ("rec", U_REC, 48, 0),
        ("mrg2", U_MRG2, 8, 8), ("out2", U_OUT, 0, 8), ("mlp2", U_MLP, 32, 64)):
    STAGES[_name] = Stage(_u, _t, _a, _d)
    _u, _t, _a, _d = _u + _nu, _t + _na + _nd, _a + _na, _d + _nd
N_UNITS = _u


def build(nc, xT, wstream, vecs, consts, mask2, bias2, outT, x2):
    ctx = ExitStack()
    with ctx:
        base = (nc.sbuf_base + 31) // 32 * 32
        A0 = base
        B0 = A0 + 64 * KB
        G0 = B0 + 64 * KB
        Z0 = G0 + 32 * KB
        T0 = Z0 + 8 * KB
        W0 = T0 + 16 * KB + 64
        C0 = W0 + 24 * KB

        def at(name, shape, off, dt=F32):
            return nc.alloc_sbuf_tensor_at(name, shape, dt, offset=off)

        a_hi = at("a_hi", [P, KT, S], A0, FR)
        a_lo = at("a_lo", [P, KT, S], A0 + 32 * KB, FR)
        b_hi = at("b_hi", [P, KT, S], B0, FR)
        b_lo = at("b_lo", [P, KT, S], B0 + 32 * KB, FR)
        res = at("res", [P, KT, S], G0)
        zt = at("zt", [P, 2, S], Z0)
        w_raw = at("w_raw", [P, 2, S], W0)
        w_hi = at("w_hi", [P, 2, S], W0 + 8 * KB, FR)
        w_lo = at("w_lo", [P, 2, S], W0 + 16 * KB, FR)
        sq = at("sq", [P, 2, S], T0)
        sqsum = at("sqsum", [P, S], T0 + 8 * KB)
        diag = at("diag", [P, KT, P], T0 + 12 * KB)
        og = at("og", [P, N_PAIR1, S], B0)
        qkv1 = at("qkv1", [P, 2, 3, S], B0 + 24 * KB)
        vtok1 = at("vtok1", [P, 2, 8, P], B0 + 48 * KB)
        sm1 = at("sm1", [P, 3, 256], Z0)
        pt1 = at("pt1", [P, 2, 256], Z0 + 3 * KB)
        mrow = at("mrow", [4, 3, S], B0 + 24 * KB)
        lrow = at("lrow", [4, 3, S], B0 + 36 * KB)
        mmin = at("mmin", [4, S], B0 + 48 * KB)
        den = at("den", [4, S], B0 + 52 * KB)
        mg = at("mg", [P, 2, S], G0)
        mgt = at("mgt", [P, 2, HC], G0 + 8 * KB)
        att1_hi = at("att1_hi", [P, 2, S], T0, FR)
        att1_lo = at("att1_lo", [P, 2, S], T0 + 8 * KB, FR)
        PADL = 8
        SP_ = S + PADL
        zp = at("zp", [P, 2, SP_], G0)
        win = at("win", [P, 2, SP_], G0 + 2 * 4 * SP_)
        pl_hi = at("pl_hi", [P, 2, S], G0 + 16 * SP_, FR)
        pl_lo = at("pl_lo", [P, 2, S], G0 + 16 * SP_ + 8 * KB, FR)
        pooled = at("pooled", [P, S], G0 + 16 * SP_ + 16 * KB)
        att2_hi = at("att2_hi", [P, 4, S], B0, FR)
        att2_lo = at("att2_lo", [P, 4, S], B0 + 16 * KB, FR)
        qk2 = at("qk2", [P, 2, 2, S], B0 + 32 * KB)
        v2 = at("v2", [P, 4, HC], B0 + 48 * KB)
        o2 = at("o2", [P, 2, S], B0 + 56 * KB)
        vtok2 = at("vtok2", [P, 2, 16, P], G0)
        braw = at("braw", [P, 6, HC], G0 + 16 * KB)
        msk = at("msk", [P, 6, 384], T0)
        bm = at("bm", [P, 4, 384], T0 + 9 * KB + 512)
        sm2 = at("sm2", [P, 3, 384], Z0)
        pt2 = at("pt2", [P, 2, 384], Z0 + 4 * KB + 512)
        rec = at("rec", [P, KT, S], B0)
        R0 = B0 + 32 * KB
        uh = at("uh", [P, S], R0, FR)
        ul = at("ul", [P, S], R0 + 4 * KB, FR)
        th = at("th", [P, 4, S], R0 + 8 * KB)
        uc = at("uc", [P, 2, S], R0 + 24 * KB)
        URW = S + 8
        y_in = at("y_in", [P, 2, S], Z0)
        ur = at("ur", [P, URW], T0)
        tm = at("tm", [P, 2, S], T0 + 4 * URW)
        gt = at("gt", [P, S], T0 + 4 * URW + 8 * KB)
        r_hi = at("r_hi", [P, KT, S], R0, FR)
        r_lo = at("r_lo", [P, KT, S], B0, FR)

        off = [C0]

        def const(name, shape):
            n = 4 * int(np.prod(shape[1:]))
            h = at(name, shape, off[0])
            off[0] += (n + 31) // 32 * 32
            return h

        vec = const("vec", [P, NVEC])
        cst = const("cst", [P, 128 + 256 + 128 + 256 + 64])
        ident, dist0, dist2 = cst[:, 0:128], cst[:, 128:384], cst[:, 384:512]
        sel = cst[0:4, 512:768].rearrange("p (a m) -> p a m", a=2)
        invc = cst[:, 768:832].rearrange("p (g t) -> p g t", g=4)
        ones = const("ones", [P, 128])
        mhalf = const("mhalf", [P, 8])
        tick = const("tick", [P, 1])
        gate_b = const("gate_b", [P, 1])
        negm = const("negm", [P, 96])
        lsum = const("lsum", [P, 96])
        rl = const("rl", [P, 96])
        ms = const("ms", [P, 8])
        rstd = const("rstd", [P, 8])
        hb = const("hb", [P, 44 + 32])
        cl = const("cl", [P, 6, 16])
        assert off[0] <= nc.sbuf_usable_end, (off[0], nc.sbuf_usable_end)

        ps = [ctx.enter_context(nc.psum_tensor(f"ps{i}", [P, 2, HC], F32)) for i in range(2)]
        pa = ctx.enter_context(nc.psum_tensor("pa", [P, 4, HC], F32))

        def pair(t):
            return ps[t % 2]

        def pair_flat(t, n=P):
            return ps[t % 2][0:n].rearrange("p c n -> p (c n)")

        sems = {}

        def sem(name):
            if name not in sems:
                sems[name] = ctx.enter_context(nc.semaphore(name))
            return sems[name]

        s_w = [sem("s_w0"), sem("s_w1")]
        s_whi, s_wlo = sem("s_whi"), sem("s_wlo")
        s_mm, s_outA, s_outD = sem("s_mm"), sem("s_outA"), sem("s_outD")

        def V(name, i=0, n=1):
            return vec[:, VEC[name] + i:VEC[name] + i + n]

        block = ctx.enter_context(nc.Block())

        def load_unit(sp, u, slot, first=False):
            if not first:
                sp.wait_ge(s_wlo, u - 1)
            sp.dma_start(w_raw[:, slot:slot + 1], wstream[:, bass.ds(u, 1)]).then_inc(s_w[slot], 16)

        def split_hi(act, u, slot, half_u, t_free):
            act.wait_ge(s_w[slot], 16 * (half_u + 1))
            if t_free is not None:
                act.wait_ge(s_mm, t_free)
            nc.scalar.activation(w_hi[:, slot], w_raw[:, slot], ACT.Copy).then_inc(s_whi, 1)

        def split_lo(dve, u, slot, t_free):
            dve.wait_ge(s_whi, u + 1)
            if t_free is not None:
                dve.wait_ge(s_mm, t_free)
            nc.vector.tensor_tensor(w_lo[:, slot], w_raw[:, slot], w_hi[:, slot].bitcast(F32),
                                    ALU.subtract).then_inc(s_wlo, 1)

        def product(slot, out, xh, xl, k, first, last, kk=None, m=P, wofs=None, kp=P):
            kk = k if kk is None else kk
            wofs = kk * P if wofs is None else wofs
            mm = None
            for n, (w, x) in enumerate(((w_hi, xh), (w_hi, xl), (w_lo, xh))):
                for c in range(2):
                    mm = nc.tensor.matmul(out[0:m, c], w[0:kp, slot, wofs:wofs + m],
                                          x[0:kp, k, c * HC:(c + 1) * HC],
                                          start=first and n == 0, stop=last and n == 2)
            return mm

        def unit8(pe, u, slot, t, xh, xl, m=P, kp=P, nk=KT):
            pe.wait_ge(s_wlo, u + 1)
            mm = None
            for k in range(nk):
                mm = product(slot, pair(t), xh, xl, k, k == 0, k == nk - 1, m=m, kp=kp)
            mm.then_inc(s_mm, 1)

        @block.sync
        def _(sp):
            sp.dma_start(vec[:], vecs).then_inc(sem("s_const"), 16)
            sp.dma_start(cst[:], consts).then_inc(sem("s_const"), 16)
            for k in range(KT):
                sp.dma_start(res[:, k], xT[k * P:(k + 1) * P]).then_inc(sem(f"s_x{k}"), 16)
            load_unit(sp, 0, 0, True)
            load_unit(sp, 1, 1, True)

            def units(u0, u1):
                with sp.Fori(u0 // 2, u1 // 2) as i:
                    for slot in range(2):
                        load_unit(sp, 2 * i + slot, slot)

            def out_stage(b, src):
                st = STAGES[f"out{b}"]
                for n in range(KT):
                    if n >= 2:
                        sp.wait_ge(s_outD, st.d + n - 1)
                    else:
                        sp.wait_ge(sem(f"s_msplit{b}"), KT)
                    sp.dma_start(zt[:, n % 2], src[n * P:(n + 1) * P]).then_inc(sem(f"s_xr{b}{n % 2}"), 16)
                    load_unit(sp, st.u + n + 2, n % 2)

            units(2, STAGES["out1"].u + 2)
            out_stage(1, xT)
            units(STAGES["mlp1"].u + 2, STAGES["att2"].u + 2)
            for k in range(KT):
                sp.wait_ge(sem("s_nrm1"), k + 1)
                sp.dma_start(x2[k * P:(k + 1) * P], res[:, k]).then_inc(sem("s_stored"), 16)
            sp.wait_ge(sem("s_bc"), 3 + 1)
            sp.dma_start(msk[:], mask2).then_inc(sem("s_msk"), 16)
            units(STAGES["att2"].u + 2, STAGES["out2"].u + 2)
            out_stage(2, x2)
            units(STAGES["mlp2"].u + 2, N_UNITS)
            for k in range(KT):
                sp.wait_ge(sem("s_nrm2"), k + 1)
                sp.dma_start(outT[k * P:(k + 1) * P], res[:, k]).then_inc(sem("s_done"), 16)
            sp.wait_ge(sem("s_done"), 16 * KT)

        def tile_of(idx):
            return idx // 8, idx // 4 % 2, idx // 8 * 4 + idx % 4

        def has_prev(g, i):
            return (g == 0 and i > 0) or (g == 1 and i % 2 == 1)

        def stat(x, b, j):
            p, idx = divmod(j, UNITS_PER_PAIR)
            _, hh, i = tile_of(idx)
            c = 32 * (p // 2) + 4 * i + 2 * (p % 2) + hh if b == 1 else j
            return x[:, c:c + 1]

        def width(b, j):
            p, idx = divmod(j, UNITS_PER_PAIR)
            if b == 2:
                return 384
            return 256 if has_prev(p // 2, tile_of(idx)[2]) else 128

        VB = {1: 2, 2: 4}
        NP_ = {1: N_PAIR1, 2: N_PAIR2}
        V_STEP = 9
        UNIT_STEPS = {5: 0, 10: 1, 15: 2}

        @block.gpsimd
        def _(pool):
            nc.gpsimd.memset(ones[:], 1.0).then_inc(sem("s_pc"), 1)
            nc.gpsimd.memset(mhalf[:], -0.5).then_inc(sem("s_pc"), 1)
            nc.gpsimd.memset(tick[:], 0.0).then_inc(sem("s_gsum"), 1)

            def norm_stats(n, wait_start=None):
                if wait_start is not None:
                    pool.wait_ge(*wait_start)
                nc.gpsimd.memset(sqsum[:], 0.0).then_inc(sem("s_sqz"), 1)
                pool.wait_ge(sem("s_sqz"), n + 1)
                for k in range(KT):
                    pool.wait_ge(sem("s_sq"), KT * n + k + 1)
                    if k:
                        pool.wait_ge(sem("s_sqs"), KT * n + k)
                    nc.gpsimd.tensor_tensor(sqsum[:], sqsum[:], sq[:, k % 2], ALU.add).then_inc(sem("s_sqs"), 1)
                pool.wait_ge(sem("s_ms"), n + 1)
                nc.gpsimd.tensor_tensor(rstd[:], ms[:], mhalf[:], ALU.pow).then_inc(sem("s_rstd"), 1)

            def norm_lo(n):
                for k in range(KT):
                    pool.wait_ge(sem("s_nh"), KT * SPLIT_NORM[n] + k + 1)
                    nc.gpsimd.tensor_tensor(a_lo[:, k], zt[:, k % 2], a_hi[:, k].bitcast(F32),
                                            ALU.subtract).then_inc(sem("s_nl"), 1)

            pool.wait_ge(sem("s_pc"), 2)
            norm_stats(0)
            norm_lo(0)
            st = STAGES["mrg1"]
            with pool.Fori(0, KT) as n:
                pool.wait_ge(s_outD, st.d + 2 * n + 2)
                nc.gpsimd.tensor_tensor(res[:, bass.ds(n, 1)], zt[:, 0:1], zt[:, 1:2], ALU.add).then_inc(sem("s_gsum"), 1)
            norm_stats(1, (sem("s_msplit1"), KT))
            norm_lo(1)
            norm_stats(2, (sem("s_stat"), 1 + 1))
            norm_stats(3, (sem("s_stat"), 2 + 1))
            norm_lo(3)
            pool.wait_ge(sem("s_msk"), 16)
            for j in range(N_PAIR2 * UNITS_PER_PAIR):
                p, idx = divmod(j, UNITS_PER_PAIR)
                hf, hh, i = tile_of(idx)
                o = (0, 1, 1, 2)[i % 4]
                if idx == 0:
                    pool.wait_ge(sem("s_braw"), 16 * (p + 1))
                if j >= 4:
                    pool.wait_ge(sem("s_add2"), j - 3)
                w0 = 0 if hf else 128
                nc.gpsimd.tensor_tensor(bm[:, j % 4], braw[:, 2 * o + hh, w0:w0 + 384], msk[:, 2 * o + hf],
                                        ALU.add).then_inc(sem("s_bm"), 1)
            norm_stats(4, (sem("s_msplit2"), KT))
            norm_lo(4)
            norm_stats(5, (sem("s_stat"), 4 + 1))

        @block.scalar
        def _(act):
            def squares(n, ready):
                for k in range(KT):
                    ready(k)
                    if k >= 2:
                        act.wait_ge(sem("s_sqs"), KT * n + k - 1)
                    else:
                        act.wait_ge(sem("s_sqz"), n + 1)
                    nc.scalar.activation(sq[:, k % 2], res[:, k], ACT.Square).then_inc(sem("s_sq"), 1)

            def norm_hi(n):
                for k in range(KT):
                    act.wait_ge(sem("s_nd"), KT * SPLIT_NORM[n] + k + 1)
                    nc.scalar.activation(a_hi[:, k], zt[:, k % 2], ACT.Copy).then_inc(sem("s_nh"), 1)

            def evac(t, dst, func=ACT.Copy, waits=(), **kw):
                act.wait_ge(s_mm, t + 1)
                for s, v in waits:
                    act.wait_ge(s, v)
                return nc.scalar.activation(dst, pair_flat(t), func, **kw)

            def attention(b):
                st = STAGES[f"att{b}"]
                vtok = vtok1 if b == 1 else vtok2
                sm, pt = (sm1, pt1) if b == 1 else (sm2, pt2)
                s_S, s_max, s_exp, s_T, s_pt, s_pv, s_oev, s_vt, s_vev = [sem(f"s_{x}{b}") for x in (
                    "S", "max", "exp", "T", "pt", "pv", "oev", "vt", "vev")]
                npair = NP_[b]

                def qkv_out(p, which):
                    u = st.u + 3 * p + which
                    t = st.t + 3 * p + which
                    split_hi(act, u + 2, u % 2, (u + 2) // 2, t + 1)
                    act.wait_ge(s_mm, t + 1)
                    if which == 0 and p >= 1:
                        act.wait_ge(s_vt, VB[b] * p)
                    if which and p >= 2:
                        act.wait_ge(s_S, UNITS_PER_PAIR * (p - 1))
                    src = pair_flat(t)
                    if b == 2 and which == 0:
                        src = src.rearrange("p (r c) -> p r c", c=64)
                        for n, c0 in enumerate(COL_START):
                            last = nc.scalar.activation(v2[:, n].rearrange("p (r c) -> p r c", c=32),
                                                        src[:, :, c0:c0 + 32], ACT.Identity, bias=V("b_in", 8 + p))
                        last.then_inc(s_outA, 1)
                        return
                    dst = qkv1[:, p % 2, which] if b == 1 else qk2[:, p % 2, which - 1]
                    kw = {}
                    func = ACT.Copy
                    if b == 2:
                        func = ACT.Identity
                        if which == 1:
                            dst = dst.rearrange("p (n r a) -> p n r a", n=4, a=16)
                            src = src.rearrange("p (r n a) -> p n r a", n=4, a=16)
                            kw = {"bias": q8[p], "scale": 0.125}
                        else:
                            kw = {"bias": V("b_in", 4 + p)}
                    else:
                        dil = DIL[p // 2]
                        if dil > 1:
                            dst = dst.rearrange("p (z l) -> p z l", z=dil)
                            src = src.rearrange("p (l z) -> p z l", z=dil)
                        if which == 1:
                            kw = {"scale": 0.125}
                    nc.scalar.activation(dst, src, func, **kw).then_inc(s_outA, 1)

                q8 = [hb[:, p:p + 1] for p in range(4)]

                def v_out(n):
                    p, bt = divmod(n, VB[b])
                    act.wait_ge(s_vt, n + 1)
                    if p >= 2:
                        act.wait_ge(s_pv, UNITS_PER_PAIR * (p - 1))
                    nc.scalar.activation(vtok[:, p % 2, 4 * bt:4 * bt + 4].rearrange("p a c -> p (a c)"),
                                         pa[:, 2], ACT.Copy).then_inc(s_vev, 1)

                def exp(j):
                    w = width(b, j)
                    act.wait_ge(s_max, j + 1)
                    nc.scalar.activation(sm[:, j % 3, 0:w], sm[:, j % 3, 0:w], ACT.Exp, bias=stat(negm, b, j),
                                         accum_out=stat(lsum, b, j)).then_inc(s_exp, 1)

                def probs_out(j):
                    w = width(b, j)
                    act.wait_ge(s_T, j + 1)
                    if j >= 2:
                        act.wait_ge(s_pv, j - 1)
                    nc.scalar.activation(pt[:, j % 2, 0:w], pa[:, 2, 0:w], ACT.Copy).then_inc(s_pt, 1)

                def o_out(c):
                    p, q = divmod(c, 4)
                    chunk, hh = divmod(q, 2)
                    act.wait_ge(s_pv, 4 * (c + 1))
                    rows = slice(64 * hh, 64 * hh + 64)
                    src = pa[rows, 3]
                    if b == 1:
                        dil = DIL[p // 2]
                        dst = og[rows, p]
                        if dil > 1:
                            zc = dil // 2
                            dst = dst.rearrange("p (l z) -> p z l", z=dil)[:, zc * chunk:zc * chunk + zc]
                            src = src.rearrange("p (z l) -> p z l", z=zc)
                        else:
                            dst = dst[:, chunk * HC:(chunk + 1) * HC]
                        nc.scalar.activation(dst, src, ACT.Copy).then_inc(s_oev, 1)
                        return
                    if p >= 2:
                        act.wait_ge(sem("s_a2lo"), p - 1)
                    dst = o2[rows, p % 2, chunk * HC:(chunk + 1) * HC].rearrange("p (r n a) -> p n r a", n=4, a=16)
                    nc.scalar.activation(dst, src.rearrange("p (n r a) -> p n r a", n=4, a=16), ACT.Copy
                                         ).then_inc(s_oev, 1)

                def load_bias(p):
                    if p:
                        act.wait_ge(sem("s_bm"), UNITS_PER_PAIR * p)
                    act.dma_start(braw[:], bias2[p]).then_inc(sem("s_braw"), 16)

                if b == 2:
                    act.wait_ge(sem("s_stored"), 16 * KT)
                    act.wait_ge(sem("s_nd"), 16 + KT)
                    load_bias(0)
                for w in range(3):
                    qkv_out(0, w)
                for n in range(VB[b]):
                    v_out(n)
                nt = npair * UNITS_PER_PAIR
                for t in range(nt + 2):
                    p, idx = divmod(t, UNITS_PER_PAIR)
                    if p + 1 < npair and V_STEP <= idx < V_STEP + VB[b]:
                        v_out(VB[b] * (p + 1) + idx - V_STEP)
                    if t < nt:
                        exp(t)
                    if 1 <= t <= nt:
                        probs_out(t - 1)
                    if t >= 6 and (t - 6) % 4 == 0:
                        o_out((t - 6) // 4)
                    if b == 2 and p + 1 < npair and idx == 13:
                        load_bias(p + 1)
                    if p + 1 < npair and idx in UNIT_STEPS:
                        qkv_out(p + 1, UNIT_STEPS[idx])
                    if b == 2 and t >= 18 and (t - 18) % 16 == 0:
                        a2_hi((t - 18) // 16)
                o_out(nt // 4 - 1)
                if b == 2:
                    a2_hi(npair - 1)

            def a2_hi(p):
                act.wait_ge(sem("s_oev2"), 4 * (p + 1))
                nc.scalar.activation(att2_hi[:, p], o2[:, p % 2], ACT.Copy).then_inc(sem("s_a2hi"), 1)

            act.wait_ge(sem("s_const"), 32)
            nc.scalar.activation(hb[:, 0:4], V("b_in", 0, 4), ACT.Copy, scale=0.125).then_inc(sem("s_hb"), 1)
            nc.scalar.activation(hb[:, 4:20], V("b_in", 28, 16), ACT.Copy, scale=0.5).then_inc(sem("s_hb"), 1)
            nc.scalar.activation(hb[:, 44:76], V("b_rg", 0, 32), ACT.Copy, scale=0.5).then_inc(sem("s_hb"), 1)
            act.wait_ge(sem("s_hb"), 3)
            nc.scalar.activation(cl[:, 0], V("lam", 0, 16), ACT.Abs).then_inc(sem("s_cl"), 1)
            act.wait_ge(sem("s_cl"), 1)
            nc.scalar.activation(cl[:, 1], cl[:, 0], ACT.Exp, scale=-1.0).then_inc(sem("s_cl"), 1)
            squares(0, lambda k: act.wait_ge(sem(f"s_x{k}"), 16))
            split_hi(act, 0, 0, 0, None)
            split_hi(act, 1, 1, 0, None)
            norm_hi(0)
            attention(1)
            for n in range(6):
                st_, g = divmod(n, 3)
                act.wait_ge(sem("s_row"), n + 1)
                src = pa[0:4, 2 * (n % 2):2 * (n % 2) + 2].rearrange("p c n -> p (c n)")
                dst = (mrow if st_ == 0 else lrow)[:, g]
                dil = DIL[g]
                if dil > 1:
                    dst = dst.rearrange("p (l z) -> p z l", z=dil)
                    src = src.rearrange("p (z l) -> p z l", z=dil)
                nc.scalar.activation(dst, src, ACT.Copy).then_inc(sem("s_rowc"), 1)
            act.wait_ge(sem("s_rowd"), 3)
            nc.scalar.activation(mrow[:], mrow[:], ACT.Exp, scale=-1.0).then_inc(sem("s_rowe"), 1)
            for a in range(2):
                act.wait_ge(sem("s_mgd"), 2 * (a + 1))
                nc.scalar.activation(att1_hi[:, a], mg[:, a], ACT.Copy).then_inc(sem("s_a1hi"), 1)
            st = STAGES["pool"]
            act.wait_ge(sem("s_a1lo"), 2)
            act.wait_ge(sem("s_pad"), 2)
            for g in range(4):
                for z in range(2):
                    u, t = st.u + 3 * g + z, st.t + 4 * g + z
                    split_hi(act, u + 2, u % 2, (u + 2) // 2, t + 1)
                    act.wait_ge(s_mm, t + 1)
                    if g:
                        act.wait_ge(sem("s_pooled"), 2 * (g - 1) + z + 1)
                    nc.scalar.activation(zp[0:PW, z, PADL:SP_], pair_flat(t, PW), ACT.Copy).then_inc(s_outA, 1)
                    act.wait_ge(sem("s_pooled"), 2 * g + z + 1)
                    if g:
                        act.wait_ge(s_mm, st.t + 4 * g)
                    nc.scalar.activation(pl_hi[0:PW, z], pooled[0:PW], ACT.Copy).then_inc(sem("s_plhi"), 1)
                u, t = st.u + 3 * g + 2, st.t + 4 * g + 2
                for o in range(2):
                    if o == 1:
                        split_hi(act, u + 2, u % 2, (u + 2) // 2, t + 2)
                    act.wait_ge(s_mm, t + o + 1)
                    if g == 0 and o == 0:
                        act.wait_ge(sem("s_bcu"), 12)
                    nc.scalar.activation(b_hi[0:PW, 2 * g + o], pair_flat(t + o, PW), ACT.Copy,
                                         scale=vec[0:PW, VEC["p_scale"] + 2 * g + o:VEC["p_scale"] + 2 * g + o + 1]
                                         ).then_inc(sem("s_pmhi"), 1)

            def gates(name, per, hb0=None):
                st = STAGES[name]
                s_z = sem(f"s_z{name}")
                with act.Fori(0, KT) as n:
                    for o in range(per):
                        u = st.u + per * n + o
                        t1 = st.t + per * n + o + 1
                        split_hi(act, u + 2, (st.u + o) % 2, (st.u + o + 2) // 2 + (per // 2) * n, t1)
                        if o % 2 == 0:
                            act.wait_ge(s_mm, t1)
                            z = o // 2
                            if name == "mrg1":
                                act.wait_ge(sem("s_gsum"), n + 1)
                            else:
                                act.wait_ge(s_outD, st.d + n)
                            kw = {}
                            if hb0 is not None:
                                nc.scalar.activation(gate_b[:], hb[:, bass.ds(hb0 + n, 1)], ACT.Copy
                                                     ).then_inc(sem(f"s_gb{name}"), 1)
                                act.wait_ge(sem(f"s_gb{name}"), n + 1)
                                kw = {"bias": gate_b[:]}
                            nc.scalar.activation(zt[:, z], pair_flat(st.t + o), ACT.Tanh, scale=0.5,
                                                 **kw).then_inc(s_outA, 1)

            gates("mrg1", 4)

            def out_stage(b):
                st = STAGES[f"out{b}"]
                n = 1 if b == 1 else 4
                act.wait_ge(s_mm, st.t)
                for k in range(KT):
                    if b == 1:
                        act.wait_ge(sem("s_gsum"), k + 2)
                    else:
                        act.wait_ge(s_outD, STAGES["mrg2"].d + k + 1)
                    nc.scalar.activation(a_hi[:, k], res[:, k], ACT.Copy, scale=0.5).then_inc(sem(f"s_mhi{b}"), 1)
                for m in range(KT):
                    split_hi(act, st.u + m + 2, m % 2, (st.u + m + 2) // 2, st.t + m + 1)
                    act.wait_ge(s_outD, st.d + m + 1)
                    if m >= 2:
                        act.wait_ge(sem("s_sqs"), KT * n + m - 1)
                    else:
                        act.wait_ge(sem("s_sqz"), n + 1)
                    nc.scalar.activation(sq[:, m % 2], res[:, m], ACT.Square).then_inc(sem("s_sq"), 1)
                norm_hi(n)

            out_stage(1)

            def mlp(b):
                st = STAGES[f"mlp{b}"]
                s_sqr, s_hhi, s_hlo = sem(f"s_sqr{b}"), sem(f"s_hhi{b}"), sem(f"s_hlo{b}")

                def hidden(u, t, tp, h0, bslot, first=False):
                    for j in range(4):
                        act.wait_ge(s_w[j % 2], 8 * (u + j + 2 - j % 2) + 16)
                        act.wait_ge(s_mm, t + j + 1)
                        nc.scalar.activation(w_hi[:, j % 2], w_raw[:, j % 2], ACT.Copy).then_inc(s_whi, 1)
                        if not (first and j < 2):
                            act.wait_ge(s_hlo, h0 + j - 1)
                        nc.scalar.activation(zt[:, j % 2], pair_flat(tp + j), ACT.Relu).then_inc(s_outA, 1)
                        act.wait_ge(s_sqr, h0 + j + 1)
                        nc.scalar.activation(b_hi[:, 4 * bslot + j], zt[:, j % 2], ACT.Copy).then_inc(s_hhi, 1)

                def down(u, t):
                    for j in range(4):
                        act.wait_ge(s_w[j % 2], 8 * (u + j + 2 - j % 2) + 16)
                        act.wait_ge(s_mm, t + 2 * j + 2)
                        nc.scalar.activation(w_hi[:, j % 2], w_raw[:, j % 2], ACT.Copy).then_inc(s_whi, 1)

                hidden(st.u, st.t, st.t, 0, 0, True)
                with act.Fori(0, 3) as i:
                    for e in range(2):
                        hidden(st.u + 4 + 8 * e + 16 * i, st.t + 4 + 12 * e + 24 * i, st.t + 4, 4 + 4 * e + 8 * i,
                               1 - e)
                        down(st.u + 8 + 8 * e + 16 * i, st.t + 8 + 12 * e + 24 * i)
                hidden(st.u + 52, st.t + 76, st.t + 4, 28, 1)
                down(st.u + 56, st.t + 80)
                n = 2 if b == 1 else 5
                for j in range(4):
                    u = st.u + 60 + j
                    if u + 2 < N_UNITS:
                        act.wait_ge(s_w[j % 2], 8 * (u + 2 - j % 2) + 16)
                        act.wait_ge(s_mm, st.t + 88 + 2 * j + 2)
                        nc.scalar.activation(w_hi[:, j % 2], w_raw[:, j % 2], ACT.Copy).then_inc(s_whi, 1)
                    for o in range(2):
                        m = 2 * j + o
                        act.wait_ge(s_outD, st.d + 56 + m + 1)
                        if m >= 2:
                            act.wait_ge(sem("s_sqs"), KT * n + m - 1)
                        else:
                            act.wait_ge(sem("s_sqz"), n + 1)
                        nc.scalar.activation(sq[:, m % 2], res[:, m], ACT.Square).then_inc(sem("s_sq"), 1)

            mlp(1)
            squares(3, lambda k: act.wait_ge(sem("s_nrm1"), k + 1))
            norm_hi(3)
            attention(2)
            gates("gatt", 2, 4)

            st = STAGES["rec"]
            s_thr = sem("s_thr")

            def u_out(c, u, t):
                split_hi(act, u + 2, u % 2, (u + 2) // 2, t + 1)
                act.wait_ge(s_mm, t + 1)
                act.wait_ge(sem("s_urpad"), 1) if c == 0 else act.wait_ge(sem("s_conv"), c)
                nc.scalar.activation(ur[:, 2:2 + S], pair_flat(t), ACT.Identity, bias=V("b_in", 12 + c)
                                     ).then_inc(s_outA, 1)

            def y_out(c, u, t):
                split_hi(act, u + 2, u % 2, (u + 2) // 2, t + 1)
                act.wait_ge(s_mm, t + 1)
                if c >= 2:
                    act.wait_ge(sem("s_rec"), c - 1)
                nc.scalar.activation(y_in[:, c % 2], pair_flat(t), ACT.Identity, bias=V("b_in", 20 + c)
                                     ).then_inc(s_outA, 1)

            def u_split(c):
                act.wait_ge(sem("s_conv"), c + 1)
                if c:
                    act.wait_ge(s_mm, gate_t(c - 1) + 4)
                nc.scalar.activation(uh[:], uc[:, c % 2], ACT.Copy).then_inc(sem("s_uh"), 1)

            def gate_t(c):
                return st.t + 1 + 6 * c + (2 if c < KT - 1 else 1)

            def gate_out(c, u):
                t = gate_t(c)
                for o in range(4):
                    act.wait_ge(s_mm, t + o + 1)
                    if c and o == 0:
                        act.wait_ge(sem("s_rec"), c)
                    nc.scalar.activation(th[:, o], pair_flat(t + o), ACT.Tanh, scale=0.5,
                                         bias=hb[:, 44 + 8 * o + c:45 + 8 * o + c]).then_inc(s_outA, 1)
                split_hi(act, u + 2, u % 2, (u + 2) // 2, t + 4)
                for d in range(2):
                    act.wait_ge(s_outA, st.a + (t - st.t) + 2 * d + 1)
                    nc.scalar.activation(tm[:, d], th[:, 2 * d], ACT.Tanh, scale=cl[:, 4, 8 * d + c:8 * d + c + 1],
                                         bias=cl[:, 4, 8 * d + c:8 * d + c + 1]).then_inc(s_thr, 1)
                    act.wait_ge(s_thr, 3 * c + d + 1)
                    nc.scalar.activation(th[:, 2 * d], th[:, 2 * d], ACT.Exp, scale=cl[:, 5, 8 * d + c:8 * d + c + 1],
                                         bias=cl[:, 5, 8 * d + c:8 * d + c + 1]).then_inc(sem("s_dec"), 1)
                act.wait_ge(sem("s_gin"), c + 1)
                nc.scalar.activation(gt[:], gt[:], ACT.Tanh, scale=0.7978845608028654).then_inc(s_thr, 1)
                for d in range(2):
                    act.wait_ge(sem("s_neg"), 2 * c + d + 1)
                    nc.scalar.activation(tm[:, d], tm[:, d], ACT.Sqrt).then_inc(sem("s_root"), 1)

            act.wait_ge(sem("s_cldone"), 1)
            u_out(0, st.u, st.t)
            for c in range(KT):
                y_out(c, st.u + 1 + 3 * c, st.t + 1 + 6 * c)
                u_split(c)
                if c < KT - 1:
                    u_out(c + 1, st.u + 2 + 3 * c, st.t + 2 + 6 * c)
                gate_out(c, st.u + 3 + 3 * c if c < KT - 1 else st.u + 23)
            for k in range(KT):
                act.wait_ge(sem("s_rec"), KT)
                nc.scalar.activation(r_hi[:, k], rec[:, k], ACT.Copy).then_inc(sem("s_rhi"), 1)
            gates("mrg2", 2, 12)
            out_stage(2)
            mlp(2)

        @block.vector
        def _(dve):
            def norm(n, gain, inplace=None):
                dve.wait_ge(sem("s_stat"), n + 1)
                nc.vector.tensor_scalar(ms[:], pa[:, 0, 0:8], 1.0 / D, EPS, ALU.mult, ALU.add).then_inc(sem("s_ms"), 1)
                dve.wait_ge(sem("s_rstd"), n + 1)
                nc.vector.tensor_tensor(diag[:], ident.unsqueeze(1).broadcast_to([P, KT, P]),
                                        rstd[:].unsqueeze(2).broadcast_to([P, KT, P]), ALU.mult
                                        ).then_inc(sem("s_diag"), 1)
                dve.wait_ge(sem("s_bc"), n + 1)
                bc = pa[:, 2:4].rearrange("p c n -> p (c n)")
                for k in range(KT):
                    if inplace is None and k >= 2:
                        dve.wait_ge(sem("s_nl"), KT * SPLIT_NORM[n] + k - 1)
                    dst = zt[:, k % 2] if inplace is None else res[:, k]
                    nc.vector.scalar_tensor_tensor(out=dst, in0=res[:, k], scalar=V(gain, k), in1=bc,
                                                   op0=ALU.mult, op1=ALU.mult
                                                   ).then_inc(sem("s_nd") if inplace is None else sem(inplace), 1)

            def attention(b):
                st = STAGES[f"att{b}"]
                sm = sm1 if b == 1 else sm2
                s_S, s_add, s_max, s_exp, s_rl, s_pn, s_T, s_oev = [sem(f"s_{x}{b}") for x in (
                    "S", "add", "max", "exp", "rl", "pn", "T", "oev")]
                npair = NP_[b]
                nt = npair * UNITS_PER_PAIR

                def add_max(j):
                    p, idx = divmod(j, UNITS_PER_PAIR)
                    _, hh, i = tile_of(idx)
                    w = width(b, j)
                    dve.wait_ge(s_S, j + 1)
                    if j >= 3:
                        dve.wait_ge(s_T, j - 2)
                    sc = pa[:, j % 2, 0:w]
                    if b == 1:
                        g = p // 2
                        dist = dist2 if g == 2 else dist0[:, 256 - w:256]
                        nc.vector.scalar_tensor_tensor(out=sm[:, j % 3, 0:w], in0=dist,
                                                       scalar=-SLOPE[2 * p + hh] * DIL[g], in1=sc,
                                                       op0=ALU.mult, op1=ALU.add).then_inc(s_add, 1)
                    else:
                        dve.wait_ge(sem("s_bm"), j + 1)
                        nc.vector.tensor_tensor(sm[:, j % 3, 0:w], bm[:, j % 4], sc, ALU.add).then_inc(s_add, 1)
                    dve.wait_ge(s_add, j + 1)
                    nc.vector.tensor_reduce(stat(negm, b, j), sm[:, j % 3, 0:w], axis=AXX, op=ALU.max,
                                            negate=True).then_inc(s_max, 1)

                def normalise(j):
                    w = width(b, j)
                    dve.wait_ge(s_exp, j + 1)
                    nc.vector.reciprocal(rl[:, j:j + 1], stat(lsum, b, j)).then_inc(s_rl, 1)
                    dve.wait_ge(s_rl, j + 1)
                    nc.vector.tensor_scalar(sm[:, j % 3, 0:w], sm[:, j % 3, 0:w], rl[:, j:j + 1], None,
                                            ALU.mult).then_inc(s_pn, 1)

                def weights(p, which):
                    u, t = st.u + 3 * p + which, st.t + 3 * p + which
                    split_lo(dve, u + 2, u % 2, t + 1)

                for w in range(3):
                    weights(0, w)
                for t in range(nt + 1):
                    p, idx = divmod(t, UNITS_PER_PAIR)
                    if t < nt:
                        add_max(t)
                    if t >= 1:
                        normalise(t - 1)
                    if p + 1 < npair and idx in UNIT_STEPS:
                        weights(p + 1, UNIT_STEPS[idx])
                    if b == 2 and t >= 19 and (t - 19) % 16 == 0:
                        a2_lo((t - 19) // 16)
                if b == 2:
                    a2_lo(npair - 1)

            def a2_lo(p):
                dve.wait_ge(sem("s_a2hi"), p + 1)
                nc.vector.tensor_tensor(att2_lo[:, p], o2[:, p % 2], att2_hi[:, p].bitcast(F32),
                                        ALU.subtract).then_inc(sem("s_a2lo"), 1)

            chain = sem("s_chain")
            nch = [0]

            def link(ins):
                nch[0] += 1
                ins.then_inc(chain, 1)
                dve.wait_ge(chain, nch[0])

            dve.wait_ge(sem("s_const"), 32)
            dve.wait_ge(sem("s_cl"), 2)
            link(nc.vector.tensor_scalar(cl[:, 2], cl[:, 1], 2.0, None, ALU.add))
            link(nc.vector.reciprocal(cl[:, 3], cl[:, 2]))
            link(nc.vector.tensor_tensor(cl[:, 1], cl[:, 1], cl[:, 3], ALU.mult))
            link(nc.vector.tensor_tensor(cl[:, 2], cl[:, 1], cl[:, 1], ALU.mult))
            link(nc.vector.memset(cl[:, 3], 1.0 / 17))
            for i in range(7, -1, -1):
                link(nc.vector.tensor_tensor(cl[:, 3], cl[:, 3], cl[:, 2], ALU.mult))
                link(nc.vector.tensor_scalar(cl[:, 3], cl[:, 3], 1.0 / (2 * i + 1), None, ALU.add))
            link(nc.vector.tensor_tensor(cl[:, 3], cl[:, 3], cl[:, 1], ALU.mult))
            link(nc.vector.tensor_scalar(cl[:, 0], V("lam", 0, 16), -1.0, 0.0, ALU.mult, ALU.max))
            link(nc.vector.scalar_tensor_tensor(out=cl[:, 0], in0=cl[:, 3], scalar=2.0, in1=cl[:, 0],
                                                op0=ALU.mult, op1=ALU.add))
            link(nc.vector.tensor_scalar(cl[:, 4], cl[:, 0], -2.0, None, ALU.mult))
            nc.vector.tensor_scalar(cl[:, 5], cl[:, 0], -4.0, None, ALU.mult).then_inc(sem("s_cldone"), 1)
            norm(0, "g_mix")
            split_lo(dve, 0, 0, None)
            split_lo(dve, 1, 1, None)
            attention(1)
            dve.wait_ge(sem("s_rowc"), 3)
            link(nc.vector.tensor_tensor(mmin[:], mrow[:, 0], mrow[:, 1], ALU.min))
            link(nc.vector.tensor_tensor(mmin[:], mmin[:], mrow[:, 2], ALU.min))
            for g in range(3):
                nc.vector.tensor_tensor(mrow[:, g], mrow[:, g], mmin[:], ALU.subtract).then_inc(sem("s_rowd"), 1)
            dve.wait_ge(sem("s_rowe"), 1)
            dve.wait_ge(sem("s_rowc"), 6)
            link(nc.vector.tensor_tensor(lrow[:], lrow[:], mrow[:], ALU.mult))
            link(nc.vector.tensor_tensor(den[:], lrow[:, 0], lrow[:, 1], ALU.add))
            link(nc.vector.tensor_tensor(den[:], den[:], lrow[:, 2], ALU.add))
            link(nc.vector.reciprocal(mmin[:], den[:]))
            for g in range(3):
                nc.vector.tensor_tensor(lrow[:, g], lrow[:, g], mmin[:], ALU.mult).then_inc(sem("s_wts"), 1)
            nb = 0
            for a in range(2):
                for c in range(2):
                    cs = slice(c * HC, (c + 1) * HC)
                    for g in range(3):
                        dve.wait_ge(sem("s_bcm"), nb + 1)
                        bc = pa[:, nb % 4]
                        dst = mg[:, a, cs] if g == 0 else mgt[:, g - 1]
                        nb += 1
                        nc.vector.tensor_tensor(dst, og[:, 2 * g + a, cs], bc, ALU.mult).then_inc(sem("s_bcu"), 1)
                        dve.wait_ge(sem("s_bcu"), nb)
                        if g:
                            ins = nc.vector.tensor_tensor(mg[:, a, cs], mg[:, a, cs], mgt[:, g - 1], ALU.add)
                            if g == 2:
                                ins.then_inc(sem("s_mgd"), 1)
                                dve.wait_ge(sem("s_mgd"), 2 * a + c + 1)
                            else:
                                link(ins)
            for a in range(2):
                dve.wait_ge(sem("s_a1hi"), a + 1)
                nc.vector.tensor_tensor(att1_lo[:, a], mg[:, a], att1_hi[:, a].bitcast(F32),
                                        ALU.subtract).then_inc(sem("s_a1lo"), 1)
            dve.wait_ge(sem("s_a1lo"), 2)
            nc.vector.memset(zp[0:PW, :, 0:PADL], 0.0).then_inc(sem("s_pad"), 1)
            nc.vector.memset(win[0:PW, :, 0:PADL], 0.0).then_inc(sem("s_pad"), 1)
            dve.wait_ge(sem("s_pad"), 2)
            st = STAGES["pool"]
            for g in range(4):
                for z in range(2):
                    u, t = st.u + 3 * g + z, st.t + 4 * g + z
                    split_lo(dve, u + 2, u % 2, t + 1)
                    dve.wait_ge(s_outA, st.a + 2 * g + z + 1)
                    src, shift = zp[0:PW, z], 1
                    for lv in range(g + 1):
                        dst = win[0:PW, lv % 2]
                        link(nc.vector.tensor_tensor(dst[:, PADL:], src[:, PADL:], src[:, PADL - shift:SP_ - shift],
                                                     ALU.add))
                        src, shift = dst, shift * 2
                    if 2 * g + z >= 1:
                        dve.wait_ge(sem("s_pllo"), 2 * g + z)
                    link(nc.vector.scalar_tensor_tensor(out=pooled[0:PW], in0=src[:, PADL:], scalar=1.0 / WINDOWS[g],
                                                        in1=zp[0:PW, z, PADL:], op0=ALU.mult, op1=ALU.subtract))
                    link(nc.vector.tensor_tensor(pooled[0:PW, 0:16], src[:, PADL:PADL + 16], invc[0:PW, g], ALU.mult))
                    nc.vector.tensor_tensor(pooled[0:PW, 0:16], pooled[0:PW, 0:16], zp[0:PW, z, PADL:PADL + 16],
                                            ALU.subtract).then_inc(sem("s_pooled"), 1)
                    dve.wait_ge(sem("s_plhi"), 2 * g + z + 1)
                    nc.vector.tensor_tensor(pl_lo[0:PW, z], pooled[0:PW], pl_hi[0:PW, z].bitcast(F32),
                                            ALU.subtract).then_inc(sem("s_pllo"), 1)
                u, t = st.u + 3 * g + 2, st.t + 4 * g + 2
                for o in range(2):
                    if o == 1:
                        split_lo(dve, u + 2, u % 2, t + 2)
                    dve.wait_ge(sem("s_pmhi"), 2 * g + o + 1)
                    nc.vector.scalar_tensor_tensor(
                        out=b_lo[0:PW, 2 * g + o], in0=pair_flat(t + o, PW),
                        scalar=vec[0:PW, VEC["p_scale"] + 2 * g + o:VEC["p_scale"] + 2 * g + o + 1],
                        in1=b_hi[0:PW, 2 * g + o].bitcast(F32), op0=ALU.mult, op1=ALU.subtract).then_inc(s_outD, 1)
            st = STAGES["mrg1"]
            with dve.Fori(0, KT) as n:
                for o in range(4):
                    u, t1 = st.u + 4 * n + o, st.t + 4 * n + o + 1
                    split_lo(dve, u + 2, (st.u + o) % 2, t1)
                    if o % 2 == 1:
                        dve.wait_ge(s_outA, st.a + 2 * n + o // 2 + 1)
                        dve.wait_ge(s_mm, t1)
                        nc.vector.scalar_tensor_tensor(out=zt[:, o // 2], in0=zt[:, o // 2], scalar=1.0,
                                                       in1=pair_flat(st.t + o), op0=ALU.add, op1=ALU.mult
                                                       ).then_inc(s_outD, 1)

            def out_stage(b):
                st = STAGES[f"out{b}"]
                for k in range(KT):
                    dve.wait_ge(sem(f"s_mhi{b}"), k + 1)
                    nc.vector.scalar_tensor_tensor(out=a_lo[:, k], in0=res[:, k], scalar=0.5,
                                                   in1=a_hi[:, k].bitcast(F32), op0=ALU.mult, op1=ALU.subtract
                                                   ).then_inc(sem(f"s_msplit{b}"), 1)
                for m in range(KT):
                    split_lo(dve, st.u + m + 2, m % 2, st.t + m + 1)
                    dve.wait_ge(s_mm, st.t + m + 1)
                    dve.wait_ge(sem(f"s_xr{b}{m % 2}"), 16 * (m // 2 + 1))
                    nc.vector.tensor_tensor(res[:, m], pair_flat(st.t + m), zt[:, m % 2], ALU.add).then_inc(s_outD, 1)

            out_stage(1)
            norm(1, "g_mlp")

            def mlp(b):
                st = STAGES[f"mlp{b}"]
                s_sqr, s_hhi, s_hlo = sem(f"s_sqr{b}"), sem(f"s_hhi{b}"), sem(f"s_hlo{b}")

                def hidden(u, t, a, h0, bslot, first=False):
                    for j in range(4):
                        split_lo(dve, u + j + 2, j % 2, t + j + 1)
                        dve.wait_ge(s_outA, a + j + 1)
                        nc.vector.tensor_tensor(zt[:, j % 2], zt[:, j % 2], zt[:, j % 2], ALU.mult).then_inc(s_sqr, 1)
                        dve.wait_ge(s_hhi, h0 + j + 1)
                        nc.vector.tensor_tensor(b_lo[:, 4 * bslot + j], zt[:, j % 2], b_hi[:, 4 * bslot + j].bitcast(F32),
                                                ALU.subtract).then_inc(s_hlo, 1)

                def down(u, t, tp, d=None):
                    for j in range(4):
                        for o in range(2):
                            m = 2 * j + o
                            if o == 1 and not (isinstance(u, int) and u + j + 2 >= N_UNITS):
                                split_lo(dve, u + j + 2, j % 2, t + 2 * j + 2)
                            dve.wait_ge(s_mm, t + m + 1)
                            nc.vector.tensor_tensor(res[:, m], pair_flat(tp + m), res[:, m], ALU.add
                                                    ).then_inc(s_outD, 1)

                hidden(st.u, st.t, st.a, 0, 0, True)
                with dve.Fori(0, 3) as i:
                    for e in range(2):
                        hidden(st.u + 4 + 8 * e + 16 * i, st.t + 4 + 12 * e + 24 * i, st.a + 4 + 4 * e + 8 * i,
                               4 + 4 * e + 8 * i, 1 - e)
                        down(st.u + 8 + 8 * e + 16 * i, st.t + 8 + 12 * e + 24 * i, st.t)
                hidden(st.u + 52, st.t + 76, st.a + 28, 28, 1)
                down(st.u + 56, st.t + 80, st.t)
                down(st.u + 60, st.t + 88, st.t)

            mlp(1)
            norm(2, "g_fin", "s_nrm1")
            norm(3, "g_ln1")
            attention(2)

            def gated(name):
                st = STAGES[name]
                with dve.Fori(0, KT) as n:
                    for o in range(2):
                        u, t1 = st.u + 2 * n + o, st.t + 2 * n + o + 1
                        split_lo(dve, u + 2, (st.u + o) % 2, t1)
                    dve.wait_ge(s_outA, st.a + n + 1)
                    dve.wait_ge(s_mm, st.t + 2 * n + 2)
                    if name == "gatt":
                        nc.vector.scalar_tensor_tensor(out=res[:, bass.ds(n, 1)].rearrange("p a b -> p (a b)"),
                                                       in0=zt[:, 0], scalar=1.0,
                                                       in1=pair_flat(st.t + 1), op0=ALU.add, op1=ALU.mult
                                                       ).then_inc(s_outD, 1)
                    else:
                        nc.vector.scalar_tensor_tensor(out=zt[:, 0], in0=zt[:, 0], scalar=1.0,
                                                       in1=pair_flat(st.t + 1), op0=ALU.add, op1=ALU.mult
                                                       ).then_inc(sem("s_gz"), 1)
                        dve.wait_ge(sem("s_gz"), n + 1)
                        r = res[:, bass.ds(n, 1)].rearrange("p a b -> p (a b)")
                        nc.vector.tensor_tensor(r, r, zt[:, 0], ALU.add).then_inc(s_outD, 1)

            gated("gatt")

            st = STAGES["rec"]

            def conv(c):
                dve.wait_ge(s_outA, st.a + (1 if c == 0 else 3 + 6 * (c - 1)))
                if c >= 2:
                    dve.wait_ge(sem("s_rec"), c - 1)
                dst = uc[:, c % 2]
                w = [V("conv_w", 8 * j + c) for j in range(4)]
                link(nc.vector.tensor_scalar(dst, ur[:, 0:S], w[0], V("conv_b", c), ALU.mult, ALU.add))
                for j in (1, 2, 3):
                    ins = nc.vector.scalar_tensor_tensor(out=dst, in0=ur[:, j:j + S], scalar=w[j], in1=dst,
                                                         op0=ALU.mult, op1=ALU.add)
                    if j < 3:
                        link(ins)
                ins.then_inc(sem("s_conv"), 1)

            def u_lo(c):
                dve.wait_ge(sem("s_uh"), c + 1)
                nc.vector.tensor_tensor(ul[:], uc[:, c % 2], uh[:].bitcast(F32), ALU.subtract).then_inc(sem("s_ul"), 1)

            def recur(c):
                y = y_in[:, c % 2]
                u_ = uc[:, c % 2]
                dve.wait_ge(s_outA, st.a + 2 + 6 * c)
                link(nc.vector.tensor_tensor(gt[:], y, y, ALU.mult))
                link(nc.vector.tensor_scalar(gt[:], gt[:], 0.044715, 1.0, ALU.mult, ALU.add))
                nc.vector.tensor_tensor(gt[:], gt[:], y, ALU.mult).then_inc(sem("s_gin"), 1)
                for d in range(2):
                    dve.wait_ge(sem("s_thr"), 3 * c + d + 1)
                    nc.vector.tensor_scalar(tm[:, d], tm[:, d], -1.0, 0.0, ALU.mult, ALU.max).then_inc(sem("s_neg"), 1)
                for d in range(2):
                    a, i = th[:, 2 * d], th[:, 2 * d + 1]
                    dve.wait_ge(sem("s_dec"), 2 * c + d + 1)
                    link(nc.vector.scalar_tensor_tensor(out=i, in0=i, scalar=1.0, in1=u_, op0=ALU.add, op1=ALU.mult))
                    dve.wait_ge(sem("s_root"), 2 * c + d + 1)
                    link(nc.vector.scalar_tensor_tensor(out=tm[:, d], in0=a, scalar=1.0, in1=tm[:, d],
                                                        op0=ALU.add, op1=ALU.mult))
                    link(nc.vector.scalar_tensor_tensor(out=i, in0=i, scalar=0.5, in1=tm[:, d],
                                                        op0=ALU.mult, op1=ALU.mult))
                    if d == 0:
                        link(nc.vector.tensor_tensor_scan(tm[:, 0], a, i, 0.0, ALU.mult, ALU.add))
                    else:
                        link(nc.vector.tensor_tensor_scan(tm[:, 1, ::-1], a[:, ::-1], i[:, ::-1], 0.0, ALU.mult, ALU.add))
                link(nc.vector.tensor_tensor(tm[:, 0], tm[:, 0], tm[:, 1], ALU.add))
                dve.wait_ge(sem("s_thr"), 3 * c + 3)
                link(nc.vector.scalar_tensor_tensor(out=gt[:], in0=gt[:], scalar=1.0, in1=y, op0=ALU.add, op1=ALU.mult))
                nc.vector.scalar_tensor_tensor(out=rec[:, c], in0=gt[:], scalar=0.5, in1=tm[:, 0],
                                               op0=ALU.mult, op1=ALU.mult).then_inc(sem("s_rec"), 1)
                dve.wait_ge(sem("s_rec"), c + 1)

            nc.vector.memset(ur[:], 0.0).then_inc(sem("s_urpad"), 1)
            split_lo(dve, st.u + 2, st.u % 2, st.t + 1)
            conv(0)
            for c in range(KT):
                split_lo(dve, st.u + 1 + 3 * c + 2, (st.u + 1 + 3 * c) % 2, st.t + 2 + 6 * c)
                u_lo(c)
                if c < KT - 1:
                    split_lo(dve, st.u + 4 + 3 * c, (st.u + 3 * c) % 2, st.t + 3 + 6 * c)
                    conv(c + 1)
                    split_lo(dve, st.u + 5 + 3 * c, (st.u + 1 + 3 * c) % 2, st.t + 7 + 6 * c)
                else:
                    split_lo(dve, st.u + 25, (st.u + 1) % 2, st.t + 48)
                recur(c)
            for k in range(KT):
                dve.wait_ge(sem("s_rhi"), k + 1)
                nc.vector.tensor_tensor(r_lo[:, k], rec[:, k], r_hi[:, k].bitcast(F32), ALU.subtract
                                        ).then_inc(sem("s_rlo"), 1)
            gated("mrg2")
            out_stage(2)
            norm(4, "g_ln2")
            mlp(2)
            norm(5, "g_lnf", "s_nrm2")

        @block.tensor
        def _(pe):
            def norm(n):
                if n == 0:
                    pe.wait_ge(sem("s_pc"), 1)
                pe.wait_ge(sem("s_sqs"), KT * n + KT)
                for i in range(KT):
                    mm = nc.tensor.matmul(pa[:, 0, i:i + 1], sqsum[:, i * P:(i + 1) * P], ones[:, 0:1],
                                          start=True, stop=True)
                mm.then_inc(sem("s_stat"), 1)
                pe.wait_ge(sem("s_diag"), n + 1)
                for c in range(2):
                    mm = nc.tensor.matmul(pa[:, 2 + c], ones[:], diag[:, 4 * c:4 * c + 4].rearrange("p a n -> p (a n)"),
                                          start=True, stop=True)
                mm.then_inc(sem("s_bc"), 1)

            def enter(name):
                st = STAGES[name]
                if st.a:
                    pe.wait_ge(s_outA, st.a)
                if st.d:
                    pe.wait_ge(s_outD, st.d)
                return st

            def attention(b):
                st = STAGES[f"att{b}"]
                n_norm = 0 if b == 1 else 3
                vtok = vtok1 if b == 1 else vtok2
                sm, pt = (sm1, pt1) if b == 1 else (sm2, pt2)
                s_S, s_add, s_pn, s_T, s_pt, s_pv, s_oev, s_vt, s_vev = [sem(f"s_{x}{b}") for x in (
                    "S", "add", "pn", "T", "pt", "pv", "oev", "vt", "vev")]
                npair = NP_[b]
                nt = npair * UNITS_PER_PAIR
                batches = [0]

                def part(p, m0, m1):
                    for m in range(m0, m1):
                        which, r = divmod(m, 48)
                        k, r = divmod(r, 6)
                        n, c = divmod(r, 2)
                        u, t = st.u + 3 * p + which, st.t + 3 * p + which
                        if k == 0 and r == 0:
                            pe.wait_ge(s_wlo, u + 1)
                            if 3 * p + which >= 2:
                                pe.wait_ge(s_outA, st.a + 3 * p + which - 1)
                        if p == 0 and which == 0 and r == 0:
                            pe.wait_ge(sem("s_nl"), KT * SPLIT_NORM[n_norm] + k + 1)
                        w, x = ((w_hi, a_hi), (w_hi, a_lo), (w_lo, a_hi))[n]
                        mm = nc.tensor.matmul(pair(t)[:, c], w[:, u % 2, k * P:(k + 1) * P],
                                              x[:, k, c * HC:(c + 1) * HC], start=(k == 0 and n == 0),
                                              stop=(k == KT - 1 and n == 2))
                        if m % 48 == 47:
                            mm.then_inc(s_mm, 1)

                def v_batch(n):
                    p, bt = divmod(n, VB[b])
                    pe.wait_ge(s_outA, st.a + 3 * p + 1)
                    if n:
                        pe.wait_ge(s_vev, n)
                    for a in range(4):
                        if b == 1:
                            src = qkv1[:, p % 2, 0, (4 * bt + a) * P:(4 * bt + a + 1) * P]
                        else:
                            src = v2[:, bt, a * P:(a + 1) * P]
                        mm = nc.tensor.transpose(pa[:, 2, a * P:(a + 1) * P], src, ident)
                    mm.then_inc(s_vt, 1)
                    batches[0] = n + 1

                def scores(j):
                    p, idx = divmod(j, UNITS_PER_PAIR)
                    _, hh, i = tile_of(idx)
                    w = width(b, j)
                    rows = slice(64 * hh, 64 * hh + 64)
                    if idx == 0:
                        pe.wait_ge(s_outA, st.a + 3 * p + 3)
                    if j >= 2:
                        pe.wait_ge(s_add, j - 1)
                    q, k = (qkv1[rows, p % 2, 1], qkv1[rows, p % 2, 2]) if b == 1 else (
                        qk2[rows, p % 2, 0], qk2[rows, p % 2, 1])
                    if b == 1:
                        lhsT = q[:, i * P:(i + 1) * P]
                        rhs = k[:, (i + 1) * P - w:(i + 1) * P]
                        out = pa[:, j % 2, 0:w]
                    else:
                        hf, n = divmod(i, 4)
                        lhsT = q[:, n * 256 + hf * 128:n * 256 + hf * 128 + 128]
                        c0 = COL_START[n]
                        rhs = k.rearrange("p (r c) -> p r c", c=64)[:, 4 * hf:4 * hf + 12, c0:c0 + 32]
                        out = pa[:, j % 2, 0:w].rearrange("p (r c) -> p r c", c=32)
                    nc.tensor.matmul(out, lhsT, rhs, start=True, stop=True).then_inc(s_S, 1)

                def transpose_probs(j):
                    w = width(b, j)
                    pe.wait_ge(s_pn, j + 1)
                    if j:
                        pe.wait_ge(s_pt, j)
                    pe.wait_ge(s_vev, batches[0])
                    for a in range(w // P):
                        mm = nc.tensor.transpose(pa[:, 2, a * P:(a + 1) * P], sm[:, j % 3, a * P:(a + 1) * P], ident)
                    mm.then_inc(s_T, 1)

                def values(j):
                    p, idx = divmod(j, UNITS_PER_PAIR)
                    _, hh, i = tile_of(idx)
                    nb = width(b, j) // P
                    pe.wait_ge(s_pt, j + 1)
                    if idx == 0:
                        pe.wait_ge(s_vev, VB[b] * (p + 1))
                    if idx % 4 == 0 and j >= 8:
                        pe.wait_ge(s_oev, j // 4 - 1)
                    for a in range(nb):
                        if b == 1:
                            blk = i - nb + 1 + a
                        else:
                            hf, n = divmod(i, 4)
                            blk = 4 * n + hf + a
                        mm = nc.tensor.matmul(pa[64 * hh:64 * hh + 64, 3, (i % 4) * P:(i % 4 + 1) * P],
                                              vtok[:, p % 2, blk, 64 * hh:64 * hh + 64],
                                              pt[:, j % 2, a * P:(a + 1) * P], start=(a == 0), stop=(a == nb - 1))
                    mm.then_inc(s_pv, 1)

                part(0, 0, 144)
                for n in range(VB[b]):
                    if n == 0:
                        pe.wait_ge(sem("s_nd"), KT * SPLIT_NORM[n_norm] + KT)
                    v_batch(n)
                for t in range(nt + 2):
                    p, idx = divmod(t, UNITS_PER_PAIR)
                    if t < nt:
                        scores(t)
                    if p + 1 < npair and V_STEP <= idx < V_STEP + VB[b]:
                        if t >= 2:
                            pe.wait_ge(s_pt, t - 1)
                        v_batch(VB[b] * (p + 1) + idx - V_STEP)
                    if p + 1 < npair:
                        part(p + 1, 9 * idx, 9 * idx + 9)
                    if 1 <= t <= nt:
                        transpose_probs(t - 1)
                    if t >= 2:
                        values(t - 2)

            norm(0)
            pe.wait_ge(sem("s_const"), 32)
            attention(1)
            pe.wait_ge(sem("s_oev1"), 4 * N_PAIR1)
            for n in range(6):
                st_, g = divmod(n, 3)
                if n >= 2:
                    pe.wait_ge(sem("s_rowc"), n - 1)
                src = negm if st_ == 0 else lsum
                for i in range(8):
                    mm = nc.tensor.matmul(pa[0:4, 2 * (n % 2) + i // 4, (i % 4) * P:(i % 4 + 1) * P],
                                          src[:, 32 * g + 4 * i:32 * g + 4 * i + 4], ident, start=True, stop=True)
                mm.then_inc(sem("s_row"), 1)
            nb = 0
            for a in range(2):
                for c in range(2):
                    for g in range(3):
                        if nb == 0:
                            pe.wait_ge(sem("s_wts"), 3)
                        if nb >= 4:
                            pe.wait_ge(sem("s_bcu"), nb - 3)
                        nc.tensor.matmul(pa[:, nb % 4], sel[:, a], lrow[:, g, c * HC:(c + 1) * HC],
                                         start=True, stop=True).then_inc(sem("s_bcm"), 1)
                        nb += 1
            st = enter("pool")
            for g in range(4):
                for z in range(2):
                    u, t = st.u + 3 * g + z, st.t + 4 * g + z
                    if g:
                        pe.wait_ge(s_outD, st.d + 2 * (g - 1) + z + 1)
                    pe.wait_ge(s_wlo, u + 1)
                    for k in range(KT):
                        mm = product(u % 2, pair(t), a_hi, a_lo, k, k == 0, k == KT - 1, m=PW, wofs=k * P)
                    mm.then_inc(s_mm, 1)
                u, t = st.u + 3 * g + 2, st.t + 4 * g + 2
                pe.wait_ge(s_wlo, u + 1)
                for o in range(2):
                    pe.wait_ge(s_outA, st.a + 2 * g + o + 1)
                    for k in range(2):
                        pe.wait_ge(sem("s_pllo"), 2 * g + k + 1)
                        mm = product(u % 2, pair(t + o), pl_hi, pl_lo, k, k == 0, k == 1, m=PW, kp=PW,
                                     wofs=(2 * k + o) * PW)
                    mm.then_inc(s_mm, 1)
            st = enter("mrg1")
            with pe.Fori(0, KT) as n:
                u = st.u + 4 * n
                pe.wait_ge(s_outA, st.a + 2 * n)
                unit8(pe, u, 0, 0, a_hi, a_lo)
                pe.wait_ge(s_outD, st.d + 2 * n)
                unit8(pe, u + 1, 1, 1, att1_hi, att1_lo, nk=2)
                pe.wait_ge(s_outA, st.a + 2 * n + 1)
                unit8(pe, u + 2, 0, 0, a_hi, a_lo)
                pe.wait_ge(s_outD, st.d + 2 * n + 1)
                unit8(pe, u + 3, 1, 1, b_hi, b_lo, kp=PW)

            def out_stage(b):
                st = enter(f"out{b}")
                for m in range(KT):
                    if m >= 2:
                        pe.wait_ge(s_outD, st.d + m - 1)
                    pe.wait_ge(s_wlo, st.u + m + 1)
                    for k in range(KT):
                        if m == 0:
                            pe.wait_ge(sem(f"s_msplit{b}"), k + 1)
                        mm = product(m % 2, pair(m), a_hi, a_lo, k, k == 0, k == KT - 1)
                    mm.then_inc(s_mm, 1)

            out_stage(1)
            norm(1)

            def mlp(b):
                st = enter(f"mlp{b}")
                n_norm = 1 if b == 1 else 4
                s_hlo = sem(f"s_hlo{b}")

                def hidden(u, a, d, first=False):
                    for j in range(4):
                        if not first and j < 2:
                            pe.wait_ge(s_outD, d - 1 + j)
                        if not first or j >= 2:
                            pe.wait_ge(s_outA, a + j - 1)
                        pe.wait_ge(s_wlo, u + j + 1)
                        for k in range(KT):
                            if first and j == 0:
                                pe.wait_ge(sem("s_nl"), KT * SPLIT_NORM[n_norm] + k + 1)
                            mm = product(j % 2, pair(j), a_hi, a_lo, k, k == 0, k == KT - 1)
                        mm.then_inc(s_mm, 1)

                def down(u, a, d, h, bslot):
                    pe.wait_ge(s_hlo, h)
                    for j in range(4):
                        pe.wait_ge(s_wlo, u + j + 1)
                        for o in range(2):
                            m = 2 * j + o
                            if m < 2:
                                if a is not None:
                                    pe.wait_ge(s_outA, a - 1 + m)
                                else:
                                    pe.wait_ge(s_outD, d - 1 + m)
                            else:
                                pe.wait_ge(s_outD, d + m - 1)
                            for k in range(4):
                                mm = product(j % 2, pair(m), b_hi, b_lo, 4 * bslot + k, k == 0, k == 3,
                                             wofs=(2 * k + o) * P)
                            mm.then_inc(s_mm, 1)

                hidden(st.u, st.a, st.d, True)
                with pe.Fori(0, 3) as i:
                    for e in range(2):
                        g = 2 * i + e
                        hidden(st.u + 4 + 8 * g, st.a + 4 + 4 * g, st.d + 8 * g)
                        down(st.u + 8 + 8 * g, st.a + 8 + 4 * g, st.d + 8 * g, 4 + 4 * g, e)
                hidden(st.u + 52, st.a + 28, st.d + 48)
                down(st.u + 56, st.a + 32, st.d + 48, 28, 0)
                down(st.u + 60, None, st.d + 56, 32, 1)

            mlp(1)
            norm(2)
            norm(3)
            attention(2)
            st = enter("gatt")
            with pe.Fori(0, KT) as n:
                pe.wait_ge(s_outA, st.a + n)
                unit8(pe, st.u + 2 * n, st.u % 2, 0, a_hi, a_lo)
                pe.wait_ge(s_outD, st.d + n)
                pe.wait_ge(sem("s_a2lo"), N_PAIR2)
                unit8(pe, st.u + 2 * n + 1, (st.u + 1) % 2, 1, att2_hi, att2_lo, nk=4)
            st = enter("rec")

            def proj(c_out, u, t):
                if t - st.t >= 2:
                    pe.wait_ge(s_outA, st.a + t - st.t - 1)
                unit8(pe, u, u % 2, t, a_hi, a_lo)

            def gates(c, u, t):
                pe.wait_ge(s_wlo, u + 1)
                pe.wait_ge(sem("s_ul"), c + 1)
                for o in range(4):
                    pe.wait_ge(s_outA, st.a + t + o - st.t - 1)
                    mm = product(u % 2, pair(t + o), uh3, ul3, 0, True, True, wofs=o * P)
                    mm.then_inc(s_mm, 1)

            uh3 = uh[:].unsqueeze(1)
            ul3 = ul[:].unsqueeze(1)
            proj(0, st.u, st.t)
            for c in range(KT):
                proj(c, st.u + 1 + 3 * c, st.t + 1 + 6 * c)
                if c < KT - 1:
                    proj(c + 1, st.u + 2 + 3 * c, st.t + 2 + 6 * c)
                    gates(c, st.u + 3 + 3 * c, st.t + 3 + 6 * c)
                else:
                    gates(c, st.u + 23, st.t + 44)
            st = enter("mrg2")
            with pe.Fori(0, KT) as n:
                pe.wait_ge(s_outA, st.a + n)
                unit8(pe, st.u + 2 * n, st.u % 2, 0, a_hi, a_lo)
                pe.wait_ge(s_outD, st.d + n)
                pe.wait_ge(sem("s_rlo"), KT)
                unit8(pe, st.u + 2 * n + 1, (st.u + 1) % 2, 1, r_hi, r_lo)
            out_stage(2)
            norm(4)
            mlp(2)
            norm(5)


def tiles(w, n, width=P, rows=P):
    k = w.shape[0] // rows
    return w.reshape(k, rows, w.shape[1])[:, :, n * width:(n + 1) * width].transpose(1, 0, 2)


def weight_stream(i):
    out = np.zeros((P, N_UNITS, KT, P), np.float32)
    flat = out.reshape(P, N_UNITS, S)
    u = 0
    w = i["w_in"][0]
    for p in range(N_PAIR1):
        for c in (12, 0, 6):
            out[:, u] = tiles(w, c + p)
            u += 1
    for g in range(4):
        for z in range(2):
            out[:, u, :, 0:PW] = tiles(w[:, 2304:3072], 2 * g + z, PW)
            u += 1
        for k in range(2):
            for o in range(2):
                flat[0:PW, u, (2 * k + o) * PW:(2 * k + o + 1) * PW] = (
                    i["w_pool_grp"][0, g, k * PW:(k + 1) * PW, o * PW:(o + 1) * PW])
        u += 1
    for n in range(KT):
        out[:, u] = tiles(w, 24 + n)
        out[:, u + 1, 0:2] = tiles(i["w_att_out"][0], n)
        out[:, u + 2] = tiles(w, 32 + n)
        out[0:PW, u + 3] = tiles(i["w_pool_out"][0], n, rows=PW)
        u += 4
    u = mlp_units(out, u, i["w_out"][0], i["w_mlp_in"][0], i["w_mlp_out"][0])
    w = i["w_in_2"][0]
    for p in range(N_PAIR2):
        for c in (8, 0, 4):
            out[:, u] = tiles(w, c + p)
            u += 1
    for n in range(KT):
        out[:, u] = tiles(w, 28 + n)
        out[:, u + 1, 0:4] = tiles(i["w_att_o_2"][0], n)
        u += 2
    out[:, u] = tiles(w, 12)
    u += 1
    for c in range(KT):
        out[:, u] = tiles(w, 20 + c)
        u += 1
        if c < KT - 1:
            out[:, u] = tiles(w, 13 + c)
            u += 1
        for d in range(2):
            for g, name in enumerate(("w_rg_a_2", "w_rg_i_2")):
                for h in range(2):
                    r = slice(64 * h, 64 * h + 64)
                    out[r, u, 2 * d + g, r] = i[name][0, d, 2 * c + h]
        u += 1
    for n in range(KT):
        out[:, u] = tiles(w, 36 + n)
        out[:, u + 1] = tiles(i["w_rec_o_2"][0], n)
        u += 2
    u = mlp_units(out, u, i["w_out_2"][0], i["w_ff1_2"][0], i["w_ff2_2"][0])
    return flat


def mlp_units(out, u, w_out, w1, w2):
    for n in range(KT):
        out[:, u] = tiles(w_out, n)
        u += 1

    def hidden(g, u):
        for j in range(4):
            out[:, u + j] = tiles(w1, 4 * g + j)
        return u + 4

    def down(g, u):
        for j in range(4):
            out[:, u + j] = tiles(w2[4 * g * P:4 * (g + 1) * P], j, 2 * P).reshape(P, KT, P)
        return u + 4

    u = hidden(0, u)
    for g in range(8):
        if g < 7:
            u = hidden(g + 1, u)
        u = down(g, u)
    return u


def columns(v):
    return v.reshape(-1, P).T


def packed_vectors(i):
    out = np.zeros((P, NVEC), np.float32)

    def put(name, a):
        out[0:a.shape[0], VEC[name]:VEC[name] + a.shape[1]] = a

    for name, key in (("g_mix", "norm_mix_g"), ("g_mlp", "norm_mlp_g"), ("g_ln1", "ln1_g_2"), ("g_ln2", "ln2_g_2"),
                      ("b_in", "b_in_2"), ("conv_b", "conv_b_2")):
        put(name, columns(i[key][0]))
    put("g_fin", columns(i["norm_final_g"]))
    put("g_lnf", columns(i["lnf_g_2"]))
    put("conv_w", columns(i["conv_w_2"][0].reshape(-1)))
    put("lam", columns(i["lru_lambda_2"][0].reshape(-1)))
    put("b_rg", columns(np.stack([i["b_rg_a_2"][0], i["b_rg_i_2"][0]], 1).reshape(-1)))
    put("p_scale", i["pool_scale"][0].reshape(8, PW).T)
    return out


def shape_constants():
    q = np.arange(P)[:, None]
    c = np.zeros((P, 832), np.float32)
    c[:, 0:128] = np.eye(P)
    step = P + q - np.arange(256)[None, :]
    c[:, 128:384] = np.where((step >= 0) & (step <= P), step, BIG)
    k = np.arange(P)[None, :]
    c[:, 384:512] = np.where((q // 64 == k // 64) & (q >= k), q - k, BIG)
    for h in range(4):
        c[h, 512 + 128 * (h // 2) + 64 * (h % 2):512 + 128 * (h // 2) + 64 * (h % 2) + 64] = 1.0
    for g, w in enumerate(WINDOWS):
        c[:, 768 + 16 * g:784 + 16 * g] = 1.0 / np.minimum(np.arange(16) + 1, w)
    return c


def neighbourhood_mask():
    out = np.full((P, 6, 12, 32), NEG, np.float32)
    for o, n in enumerate((0, 1, 3)):
        cs = (0, 8, 24, 32)[n]
        for hf in range(2):
            for r in range(8):
                row = 8 * hf + r
                rs = min(max(row - 4, 0), 8)
                for a in range(16):
                    qc = 16 * n + a
                    ws = min(max(qc - 8, 0), 48)
                    r0, c0 = rs - 4 * hf, ws - cs
                    out[16 * r + a, 2 * o + hf, r0:r0 + 8, max(c0, 0):c0 + 16] = 0.0
    return out.reshape(P, 6, 384)


def relative_bias(rpb):
    h = rpb.shape[0]
    pad = np.zeros((h, 15 + 8, 31 + 32), np.float32)
    pad[:, 4:19, 16:47] = rpb
    out = np.zeros((h // 2, 8, 16, 3, 2, 16, 32), np.float32)
    for r in range(8):
        for a in range(16):
            for o, s in enumerate((0, -8, -16)):
                c0 = s - a + 31
                out[:, r, a, o] = pad[:, 7 - r:23 - r, c0:c0 + 32].reshape(h // 2, 2, 16, 32)
    return out.reshape(h // 2, P, 6, HC)


def kernel(**inputs):
    import concourse.bacc as bacc
    from concourse.bass_utils import run_bass_kernel_spmd

    i = {k: np.ascontiguousarray(v) for k, v in inputs.items()}
    arrays = {
        "xT": np.ascontiguousarray(i["x"][0].T),
        "wstream": weight_stream(i),
        "vecs": packed_vectors(i),
        "consts": shape_constants(),
        "mask2": neighbourhood_mask(),
        "bias2": relative_bias(i["rpb_2"][0]),
    }
    nc = bacc.Bacc("TRN2", target_bir_lowering=False, num_devices=1, dynamic_dma_scratch_size=8192)
    args = [nc.dram_tensor(n, a.shape, F32, kind="ExternalInput").ap() for n, a in arrays.items()]
    args.append(nc.dram_tensor("outT", (D, S), F32, kind="ExternalOutput").ap())
    args.append(nc.dram_tensor("x2", (D, S), F32, kind="Internal").ap())
    build(nc, *args)
    r = run_bass_kernel_spmd(nc, [arrays], core_ids=[0])
    return np.ascontiguousarray(np.asarray(r.results[0]["outT"]).T).reshape(1, S, D)
```

```python
from contextlib import ExitStack

import numpy as np

import concourse.bass as bass
from concourse import mybir

F32 = mybir.dt.float32
FR = mybir.dt.float32r
ALU = mybir.AluOpType
ACT = mybir.ActivationFunctionType
AXX = mybir.AxisListType.X

P = 128
S = 1024
D = 1024
KT = D // P
HC = 512
EPS = 1e-6
KB = 1024

N_PAIR1 = 6
DIL = (1, 4, 16)
SLOPE = [2.0 ** (-8.0 * (h + 1) / 12) for h in range(12)]
PW = 96
WINDOWS = (2, 4, 8, 16)
REC_ORDER = (0, 1, 6, 2, 3, 4, 5, 7)
N_PAIR2 = 4
COL_START = (0, 8, 24, 32)
NEG = -1e30
BIG = 1e30
UNITS_PER_PAIR = 16

VEC = {}
_n = 0
for _name, _w in (("g_mix", 8), ("g_mlp", 8), ("g_fin", 8), ("g_ln1", 8), ("g_ln2", 8), ("g_lnf", 8),
                  ("b_in", 44), ("conv_w", 32), ("conv_b", 8), ("b_rg", 32), ("lam", 16), ("p_scale", 8)):
    VEC[_name] = _n
    _n += _w
NVEC = _n

AHEAD = 4
EXTRA = 4
U_ATT1, U_POOL, U_MRG1, U_OUT, U_MLP = 3 * N_PAIR1 + EXTRA, 8, 32, 8, 64
U_ATT2, U_GAT0, U_GATT, U_REC, U_MRG2 = 3 * N_PAIR2 + EXTRA, 2, 8, 24, 16


SPLIT_NORM = {0: 0, 2: 1}
SPREADS = (1, 2, 4, 5, 6)


class Stage:

    def __init__(self, u, t, a, d):
        self.u, self.t, self.a, self.d = u, t, a, d


STAGES = {}
_u = _t = _a = _d = 0
for _name, _nu, _na, _nd in (
        ("att1", U_ATT1, U_ATT1, 0), ("pool", U_POOL, 4, 8), ("mrg1", U_MRG1, 16, 16), ("out1", U_OUT, 0, 8),
        ("mlp1", U_MLP, 0, 96), ("att2", U_ATT2, U_ATT2, 0), ("gat0", U_GAT0, 0, 4), ("gatt", U_GATT, 4, 4), ("rec", U_REC, 48, 0),
        ("mrg2", U_MRG2, 8, 8), ("out2", U_OUT, 0, 8), ("mlp2", U_MLP, 0, 96)):
    STAGES[_name] = Stage(_u, _t, _a, _d)
    _u, _t, _a, _d = _u + _nu, _t + _na + _nd, _a + _na, _d + _nd
N_UNITS = _u


def build(nc, xT, wstream, vecs, consts, mask2, bias2, outT, x2):
    ctx = ExitStack()
    with ctx:
        base = (nc.sbuf_base + 31) // 32 * 32
        A0 = base
        B0 = A0 + 64 * KB
        G0 = B0 + 64 * KB
        Z0 = G0 + 32 * KB
        T0 = Z0 + 8 * KB + 64
        W0 = T0 + 16 * KB + 64
        C0 = W0 + 24 * KB

        def at(name, shape, off, dt=F32):
            return nc.alloc_sbuf_tensor_at(name, shape, dt, offset=off)

        a_hi = at("a_hi", [P, KT, S], A0, FR)
        a_lo = at("a_lo", [P, KT, S], A0 + 32 * KB, FR)
        b_hi = at("b_hi", [P, KT, S], B0, FR)
        b_lo = at("b_lo", [P, KT, S], B0 + 32 * KB, FR)
        res = at("res", [P, KT, S], G0)
        zt = at("zt", [P, 2, S], Z0)
        w_raw = at("w_raw", [P, 2, S], W0)
        w_hi = at("w_hi", [P, 2, S], W0 + 8 * KB, FR)
        w_lo = at("w_lo", [P, 2, S], W0 + 16 * KB, FR)
        sq = at("sq", [P, 2, S], T0)
        sqsum = at("sqsum", [P, S], T0 + 8 * KB)
        diag = at("diag", [P, KT, P], T0 + 12 * KB)
        sqsum_g = at("sqsum_g", [P, S], Z0)
        sq_g = at("sq_g", [P, S], Z0 + 4 * KB)
        diag_r = at("diag_r", [P, KT, P], T0)
        og = at("og", [P, N_PAIR1, S], B0)
        qkv1 = at("qkv1", [P, 2, 3, S], B0 + 24 * KB)
        vtok1 = at("vtok1", [P, 2, 8, P], B0 + 48 * KB)
        sm1 = at("sm1", [P, 3, 256], T0)
        pt1 = at("pt1", [P, 2, 256], T0 + 3 * KB)
        mrow = at("mrow", [4, 3, S], B0 + 24 * KB)
        lrow = at("lrow", [4, 3, S], B0 + 36 * KB)
        mmin = at("mmin", [4, S], B0 + 48 * KB)
        den = at("den", [4, S], B0 + 52 * KB)
        mg = at("mg", [P, 2, S], B0 + 56 * KB)
        mgt = at("mgt", [P, 2, HC], B0 + 48 * KB)
        att1_hi = at("att1_hi", [P, 2, S], T0, FR)
        att1_lo = at("att1_lo", [P, 2, S], T0 + 8 * KB, FR)
        PADL = 8
        SP_ = S + PADL
        win = at("win", [P, 2, SP_], Z0)
        att2_hi = at("att2_hi", [P, 4, S], B0, FR)
        att2_lo = at("att2_lo", [P, 4, S], B0 + 16 * KB, FR)
        qk2 = at("qk2", [P, 2, 2, S], B0 + 32 * KB)
        v2 = at("v2", [P, 4, HC], B0 + 48 * KB)
        o2 = at("o2", [P, 2, S], B0 + 56 * KB)
        vtok2 = at("vtok2", [P, 2, 16, P], G0)
        tg01 = at("tg01", [P, 2, S], B0 + 48 * KB)
        tg23 = at("tg23", [P, 2, S], B0 + 32 * KB)
        braw = at("braw", [P, 6, HC], G0 + 16 * KB)
        msk = at("msk", [P, 6, 384], T0)
        bm = at("bm", [P, 4, 384], T0 + 9 * KB + 512)
        sm2 = at("sm2", [P, 3, 384], Z0)
        pt2 = at("pt2", [P, 2, 384], Z0 + 4 * KB + 512)
        rec = at("rec", [P, KT, S], B0)
        R0 = B0 + 32 * KB
        uh = at("uh", [P, S], R0, FR)
        ul = at("ul", [P, S], R0 + 4 * KB, FR)
        th = at("th", [P, 4, S], R0 + 8 * KB)
        uc = at("uc", [P, 2, S], R0 + 24 * KB)
        URW = S + 8
        y_in = at("y_in", [P, 2, S], Z0)
        tm = at("tm", [P, 2, S], T0 + 4 * URW)
        gt = at("gt", [P, S], T0 + 4 * URW + 8 * KB)
        r_hi = at("r_hi", [P, KT, S], R0, FR)
        r_lo = at("r_lo", [P, KT, S], B0, FR)

        off = [C0]

        def const(name, shape):
            n = 4 * int(np.prod(shape[1:]))
            h = at(name, shape, off[0])
            off[0] += (n + 31) // 32 * 32
            return h

        vec = const("vec", [P, NVEC])
        cst = const("cst", [P, 128 + 256 + 128 + 256 + 64])
        ident, dist0, dist2 = cst[:, 0:128], cst[:, 128:384], cst[:, 384:512]
        sel = cst[0:4, 512:768].rearrange("p (a m) -> p a m", a=2)
        invc = cst[:, 768:832].rearrange("p (g t) -> p g t", g=4)
        ones = const("ones", [P, 128])
        mhalf = const("mhalf", [P, 8])
        tick = const("tick", [P, 1])
        warm = const("warm", [P, 1])
        first16 = const("first16", [P, 16])
        gate_b = const("gate_b", [P, 1])
        negm = const("negm", [P, 96])
        lsum = const("lsum", [P, 96])
        rl = const("rl", [P, 96])
        rb_at = off[0]
        rb = const("rb", [P, URW])[:, 0:S]
        ur = (at("ur0", [P, URW], T0), at("ur1", [P, URW], rb_at))
        ms = const("ms", [P, 8])
        msg = const("msg", [P, 8])
        rstd1 = const("rstd1", [P, 8])
        gg = const("gg", [P, 8])
        rstd = const("rstd", [P, 8])
        hb = const("hb", [P, 44 + 32])
        cl = const("cl", [P, 6, 16])
        assert off[0] <= nc.sbuf_usable_end, (off[0], nc.sbuf_usable_end)

        ps = [ctx.enter_context(nc.psum_tensor(f"ps{i}", [P, 2, HC], F32)) for i in range(2)]
        pa = ctx.enter_context(nc.psum_tensor("pa", [P, 4, HC], F32))

        def pair(t):
            return ps[t % 2]

        def pair_flat(t, n=P):
            return ps[t % 2][0:n].rearrange("p c n -> p (c n)")

        def normed(k):
            return (zt[:, 0], zt[:, 1], sq[:, 1], sqsum[:])[k % 4]

        def group_out(g, o):
            out = pa[0:PW, 2 * o:2 * o + 2] if g % 2 else ps[(STAGES["pool"].t + 4 + o) % 2][0:PW]
            return out.rearrange("p c n -> p (c n)")

        sems = {}

        def sem(name):
            if name not in sems:
                sems[name] = ctx.enter_context(nc.semaphore(name))
            return sems[name]

        s_w = [sem("s_w0"), sem("s_w1")]
        s_whi, s_wlo = sem("s_whi"), sem("s_wlo")
        s_mm, s_outA, s_outD = sem("s_mm"), sem("s_outA"), sem("s_outD")

        def V(name, i=0, n=1):
            return vec[:, VEC[name] + i:VEC[name] + i + n]

        block = ctx.enter_context(nc.Block())

        def load_unit(sp, u, slot, first=False):
            if not first:
                sp.wait_ge(s_wlo, u - 1)
            sp.dma_start(w_raw[:, slot:slot + 1], wstream[:, bass.ds(u, 1)]).then_inc(s_w[slot], 16)

        def split_hi(act, u, slot, half_u, t_free):
            act.wait_ge(s_w[slot], 16 * (half_u + 1))
            if t_free is not None:
                act.wait_ge(s_mm, t_free)
            nc.scalar.activation(w_hi[:, slot], w_raw[:, slot], ACT.Copy).then_inc(s_whi, 1)

        def split_lo(dve, u, slot, t_free):
            dve.wait_ge(s_whi, u + 1)
            if t_free is not None:
                dve.wait_ge(s_mm, t_free)
            nc.vector.tensor_tensor(w_lo[:, slot], w_raw[:, slot], w_hi[:, slot].bitcast(F32),
                                    ALU.subtract).then_inc(s_wlo, 1)

        def product(slot, out, xh, xl, k, first, last, kk=None, m=P, wofs=None, kp=P):
            kk = k if kk is None else kk
            wofs = kk * P if wofs is None else wofs
            mm = None
            for n, (w, x) in enumerate(((w_hi, xh), (w_hi, xl), (w_lo, xh))):
                for c in range(2):
                    mm = nc.tensor.matmul(out[0:m, c], w[0:kp, slot, wofs:wofs + m],
                                          x[0:kp, k, c * HC:(c + 1) * HC],
                                          start=first and n == 0, stop=last and n == 2)
            return mm

        def unit8(pe, u, slot, t, xh, xl, m=P, kp=P, nk=KT):
            pe.wait_ge(s_wlo, u + 1)
            mm = None
            for k in range(nk):
                mm = product(slot, pair(t), xh, xl, k, k == 0, k == nk - 1, m=m, kp=kp)
            mm.then_inc(s_mm, 1)

        @block.sync
        def _(sp):
            sp.dma_start(vec[:], vecs).then_inc(sem("s_const"), 16)
            sp.dma_start(cst[:], consts).then_inc(sem("s_const"), 16)
            for k in range(KT):
                sp.dma_start(res[:, k], xT[k * P:(k + 1) * P]).then_inc(sem(f"s_x{k}"), 16)
            load_unit(sp, 0, 0, True)
            load_unit(sp, 1, 1, True)

            def units(u0, u1):
                with sp.Fori(u0 // 2, u1 // 2) as i:
                    for slot in range(2):
                        load_unit(sp, 2 * i + slot, slot)

            def out_stage(b, src):
                st = STAGES[f"out{b}"]
                for n in range(KT):
                    if n >= 2:
                        sp.wait_ge(s_outD, st.d + n - 1)
                    else:
                        sp.wait_ge(sem(f"s_msplit{b}"), KT)
                    sp.dma_start(zt[:, n % 2], src[n * P:(n + 1) * P]).then_inc(sem(f"s_xr{b}{n % 2}"), 16)
                    load_unit(sp, st.u + n + 2, n % 2)

            units(2, STAGES["out1"].u + 2)
            out_stage(1, xT)
            units(STAGES["mlp1"].u + 2, STAGES["att2"].u + 2)
            for k in range(KT):
                sp.wait_ge(sem("s_nrm1"), k + 1)
                sp.dma_start(x2[k * P:(k + 1) * P], res[:, k]).then_inc(sem("s_stored"), 16)
            sp.wait_ge(sem("s_nlo"), KT)
            sp.wait_ge(sem("s_nle"), KT)
            sp.dma_start(msk[:], mask2).then_inc(sem("s_msk"), 16)
            units(STAGES["att2"].u + 2, STAGES["out2"].u + 2)
            out_stage(2, x2)
            units(STAGES["mlp2"].u + 2, N_UNITS)
            for k in range(KT):
                sp.wait_ge(sem("s_nrm2"), k + 1)
                sp.dma_start(outT[k * P:(k + 1) * P], res[:, k]).then_inc(sem("s_done"), 16)
            sp.wait_ge(sem("s_done"), 16 * KT)

        def tile_of(idx):
            return idx // 8, idx // 4 % 2, idx // 8 * 4 + idx % 4

        def has_prev(g, i):
            return (g == 0 and i > 0) or (g == 1 and i % 2 == 1)

        def stat(x, b, j):
            p, idx = divmod(j, UNITS_PER_PAIR)
            _, hh, i = tile_of(idx)
            c = 32 * (p // 2) + 4 * i + 2 * (p % 2) + hh if b == 1 else j
            return x[:, c:c + 1]

        def width(b, j):
            p, idx = divmod(j, UNITS_PER_PAIR)
            if b == 2:
                return 384
            return 256 if has_prev(p // 2, tile_of(idx)[2]) else 128

        VB = {1: 2, 2: 4}
        NP_ = {1: N_PAIR1, 2: N_PAIR2}
        V_STEP = 9
        FILL = 9

        def unit_at(b, t):
            for m in range(AHEAD, 3 * NP_[b] + EXTRA):
                if (48 * (m + 1 - AHEAD) - 1) // FILL == t:
                    return m
            return None

        @block.gpsimd
        def _(pool):
            nc.gpsimd.memset(ones[:], 1.0).then_inc(sem("s_pc"), 1)
            nc.gpsimd.memset(mhalf[:], -0.5).then_inc(sem("s_pc"), 1)
            nc.gpsimd.memset(tick[:], 0.0).then_inc(sem("s_gsum"), 1)

            def norm_power(i):
                pool.wait_ge(sem("s_ms"), i + 1)
                nc.gpsimd.tensor_tensor(rstd[:], ms[:], mhalf[:], ALU.pow).then_inc(sem("s_rstd"), 1)

            def norm_lo(n):
                for k in range(1, KT, 2):
                    pool.wait_ge(sem("s_nh"), KT * SPLIT_NORM[n] + k + 1)
                    nc.gpsimd.tensor_tensor(a_lo[:, k], normed(k), a_hi[:, k].bitcast(F32),
                                            ALU.subtract).then_inc(sem("s_nlo"), 1)

            pool.wait_ge(sem("s_pc"), 2)
            norm_power(0)
            norm_lo(0)
            pool.wait_ge(sem("s_nlo"), 4)
            pool.wait_ge(sem("s_nle"), 4)
            nc.gpsimd.memset(win[:, :, 0:PADL], 0.0).then_inc(sem("s_win"), 1)
            pool.wait_ge(sem("s_win"), 1)
            nwin = 1
            for z in range(8):
                if z < 4:
                    pool.wait_ge(s_outA, STAGES["att1"].a + 3 * N_PAIR1 + z + 1)
                else:
                    pool.wait_ge(s_outA, STAGES["pool"].a + z - 3)
                if z:
                    pool.wait_ge(sem("s_pooled"), z)
                for lv in range(z // 2 + 1):
                    dst, src, shift = win[0:PW, lv % 2], win[0:PW, 1 - lv % 2], 1 << lv
                    if lv == 0:
                        nc.gpsimd.tensor_tensor(dst[:, PADL + 1:], res[0:PW, z, 1:], res[0:PW, z, 0:S - 1], ALU.add
                                                ).then_inc(sem("s_win"), 1)
                        ins = nc.gpsimd.tensor_tensor(dst[:, PADL:PADL + 1], res[0:PW, z, 0:1],
                                                      dst[:, PADL - 1:PADL], ALU.add)
                        nwin += 1
                    else:
                        ins = nc.gpsimd.tensor_tensor(dst[:, PADL:], src[:, PADL:], src[:, PADL - shift:SP_ - shift],
                                                      ALU.add)
                    nwin += 1
                    if lv < z // 2:
                        ins.then_inc(sem("s_win"), 1)
                        pool.wait_ge(sem("s_win"), nwin)
                    else:
                        nwin -= 1
                        ins.then_inc(sem("s_wsum"), 1)
            st = STAGES["mrg1"]
            with pool.Fori(0, KT) as n:
                pool.wait_ge(s_outD, st.d + 2 * n + 2)
                nc.gpsimd.tensor_tensor(res[:, bass.ds(n, 1)], zt[:, 0:1], zt[:, 1:2], ALU.add).then_inc(sem("s_gsum"), 1)
            norm_power(1)
            norm_power(2)
            norm_power(3)
            norm_lo(2)
            pool.wait_ge(sem("s_msk"), 16)
            for j in range(N_PAIR2 * UNITS_PER_PAIR):
                p, idx = divmod(j, UNITS_PER_PAIR)
                hf, hh, i = tile_of(idx)
                o = (0, 1, 1, 2)[i % 4]
                if idx == 0:
                    pool.wait_ge(sem("s_braw"), 16 * (p + 1))
                if j >= 4:
                    pool.wait_ge(sem("s_add2"), j - 3)
                w0 = 0 if hf else 128
                nc.gpsimd.tensor_tensor(bm[:, j % 4], braw[:, 2 * o + hh, w0:w0 + 384], msk[:, 2 * o + hf],
                                        ALU.add).then_inc(sem("s_bm"), 1)
            def u_lo(c):
                pool.wait_ge(sem("s_uh"), c + 1)
                if c:
                    pool.wait_ge(s_mm, STAGES["rec"].t + 6 * c + 1)
                nc.gpsimd.tensor_tensor(ul[:], uc[:, c % 2], uh[:].bitcast(F32), ALU.subtract).then_inc(sem("s_ul"), 1)

            u_lo(0)
            for c in range(KT):
                pool.wait_ge(sem("s_gpoly"), c + 1)
                nc.gpsimd.tensor_tensor(gt[:], gt[:], y_in[:, c % 2], ALU.mult).then_inc(sem("s_gin"), 1)
                if c < KT - 1:
                    u_lo(c + 1)
                pool.wait_ge(sem("s_scan"), 2 * c + 2)
                nc.gpsimd.tensor_tensor(tm[:, 0], tm[:, 0], tm[:, 1], ALU.add).then_inc(sem("s_dirs"), 1)
            norm_power(4)
            norm_power(5)

        @block.scalar
        def _(act):
            def square(n, k):
                if k == 0:
                    if n:
                        act.wait_ge(sem("s_stat"), n)
                elif k >= 3:
                    act.wait_ge(sem("s_sqs"), 7 * n + k - 2)
                nc.scalar.activation(sqsum[:] if k == 0 else sq[:, k % 2], res[:, k], ACT.Square
                                     ).then_inc(sem("s_sq"), 1)

            def copy_rb(n):
                act.wait_ge(sem("s_bc"), SPREADS[n])
                nc.scalar.activation(rb[:], pa[:, 2:4].rearrange("p c n -> p (c n)"), ACT.Copy
                                     ).then_inc(sem("s_rb"), 1)

            def norm_hi(n):
                for k in range(KT):
                    act.wait_ge(sem("s_nd"), KT * SPLIT_NORM[n] + k + 1)
                    nc.scalar.activation(a_hi[:, k], normed(k), ACT.Copy).then_inc(sem("s_nh"), 1)

            def evac(t, dst, func=ACT.Copy, waits=(), **kw):
                act.wait_ge(s_mm, t + 1)
                for s, v in waits:
                    act.wait_ge(s, v)
                return nc.scalar.activation(dst, pair_flat(t), func, **kw)

            def attention(b):
                st = STAGES[f"att{b}"]
                vtok = vtok1 if b == 1 else vtok2
                sm, pt = (sm1, pt1) if b == 1 else (sm2, pt2)
                s_S, s_max, s_exp, s_T, s_pt, s_pv, s_oev, s_vt, s_vev = [sem(f"s_{x}{b}") for x in (
                    "S", "max", "exp", "T", "pt", "pv", "oev", "vt", "vev")]
                npair = NP_[b]

                def unit_out(m):
                    p, which = divmod(m, 3)
                    u = st.u + m
                    t = st.t + m
                    split_hi(act, u + 2, u % 2, (u + 2) // 2, t + 1)
                    act.wait_ge(s_mm, t + 1)
                    if m >= 3 * npair:
                        e = m - 3 * npair
                        if b == 1:
                            nc.scalar.activation(res[0:PW, e], pair_flat(t, PW), ACT.Copy).then_inc(s_outA, 1)
                            return
                        if e == 0:
                            act.wait_ge(s_vt, VB[b] * npair)
                        if e == 2:
                            act.wait_ge(s_S, UNITS_PER_PAIR * (npair - 1))
                        nc.scalar.activation((tg01 if e < 2 else tg23)[:, e % 2], pair_flat(t), ACT.Tanh, scale=0.5,
                                             bias=hb[:, 4 + e:5 + e]).then_inc(s_outA, 1)
                        return
                    if which == 0 and p >= 1:
                        act.wait_ge(s_vt, VB[b] * p)
                    if which and p >= 2:
                        act.wait_ge(s_S, UNITS_PER_PAIR * (p - 1))
                    src = pair_flat(t)
                    if b == 2 and which == 0:
                        src = src.rearrange("p (r c) -> p r c", c=64)
                        for n, c0 in enumerate(COL_START):
                            last = nc.scalar.activation(v2[:, n].rearrange("p (r c) -> p r c", c=32),
                                                        src[:, :, c0:c0 + 32], ACT.Identity, bias=V("b_in", 8 + p))
                        last.then_inc(s_outA, 1)
                        return
                    dst = qkv1[:, p % 2, which] if b == 1 else qk2[:, p % 2, which - 1]
                    kw = {}
                    func = ACT.Copy
                    if b == 2:
                        func = ACT.Identity
                        if which == 1:
                            dst = dst.rearrange("p (n r a) -> p n r a", n=4, a=16)
                            src = src.rearrange("p (r n a) -> p n r a", n=4, a=16)
                            kw = {"bias": q8[p], "scale": 0.125}
                        else:
                            kw = {"bias": V("b_in", 4 + p)}
                    else:
                        dil = DIL[p // 2]
                        if dil > 1:
                            dst = dst.rearrange("p (z l) -> p z l", z=dil)
                            src = src.rearrange("p (l z) -> p z l", z=dil)
                        if which == 1:
                            kw = {"scale": 0.125}
                    nc.scalar.activation(dst, src, func, **kw).then_inc(s_outA, 1)

                q8 = [hb[:, p:p + 1] for p in range(4)]

                def v_out(n):
                    p, bt = divmod(n, VB[b])
                    act.wait_ge(s_vt, n + 1)
                    if p >= 2:
                        act.wait_ge(s_pv, UNITS_PER_PAIR * (p - 1))
                    nc.scalar.activation(vtok[:, p % 2, 4 * bt:4 * bt + 4].rearrange("p a c -> p (a c)"),
                                         pa[:, 2], ACT.Copy).then_inc(s_vev, 1)

                def exp(j):
                    w = width(b, j)
                    act.wait_ge(s_max, j + 1)
                    nc.scalar.activation(sm[:, j % 3, 0:w], sm[:, j % 3, 0:w], ACT.Exp, bias=stat(negm, b, j),
                                         accum_out=stat(lsum, b, j)).then_inc(s_exp, 1)

                def probs_out(j):
                    w = width(b, j)
                    act.wait_ge(s_T, j + 1)
                    if j >= 2:
                        act.wait_ge(s_pv, j - 1)
                    nc.scalar.activation(pt[:, j % 2, 0:w], pa[:, 2, 0:w], ACT.Copy).then_inc(s_pt, 1)

                def o_out(c):
                    p, q = divmod(c, 4)
                    chunk, hh = divmod(q, 2)
                    act.wait_ge(s_pv, 4 * (c + 1))
                    rows = slice(64 * hh, 64 * hh + 64)
                    src = pa[rows, 3]
                    if b == 1:
                        dil = DIL[p // 2]
                        dst = og[rows, p]
                        if dil > 1:
                            zc = dil // 2
                            dst = dst.rearrange("p (l z) -> p z l", z=dil)[:, zc * chunk:zc * chunk + zc]
                            src = src.rearrange("p (z l) -> p z l", z=zc)
                        else:
                            dst = dst[:, chunk * HC:(chunk + 1) * HC]
                        nc.scalar.activation(dst, src, ACT.Copy).then_inc(s_oev, 1)
                        return
                    if p >= 2:
                        act.wait_ge(sem("s_a2lo"), p - 1)
                    dst = o2[rows, p % 2, chunk * HC:(chunk + 1) * HC].rearrange("p (r n a) -> p n r a", n=4, a=16)
                    nc.scalar.activation(dst, src.rearrange("p (n r a) -> p n r a", n=4, a=16), ACT.Copy
                                         ).then_inc(s_oev, 1)

                def load_bias(p):
                    if p:
                        act.wait_ge(sem("s_bm"), UNITS_PER_PAIR * p)
                    act.dma_start(braw[:], bias2[p]).then_inc(sem("s_braw"), 16)

                for m in range(3):
                    unit_out(m)
                    if b == 2 and m == 1:
                        act.wait_ge(sem("s_stored"), 16 * KT)
                        load_bias(0)
                for n in range(VB[b]):
                    v_out(n)
                unit_out(3)
                nt = npair * UNITS_PER_PAIR
                for t in range(nt + 2):
                    p, idx = divmod(t, UNITS_PER_PAIR)
                    if p + 1 < npair and V_STEP <= idx < V_STEP + VB[b]:
                        v_out(VB[b] * (p + 1) + idx - V_STEP)
                    if t < nt:
                        exp(t)
                    if 1 <= t <= nt:
                        probs_out(t - 1)
                    if t >= 6 and (t - 6) % 4 == 0:
                        o_out((t - 6) // 4)
                    if b == 2 and p + 1 < npair and idx == 13:
                        load_bias(p + 1)
                    if unit_at(b, t) is not None:
                        unit_out(unit_at(b, t))
                    if b == 2 and t >= 18 and (t - 18) % 16 == 0:
                        a2_hi((t - 18) // 16)
                o_out(nt // 4 - 1)
                if b == 2:
                    a2_hi(npair - 1)

            def a2_hi(p):
                act.wait_ge(sem("s_oev2"), 4 * (p + 1))
                nc.scalar.activation(att2_hi[:, p], o2[:, p % 2], ACT.Copy).then_inc(sem("s_a2hi"), 1)

            act.wait_ge(sem("s_const"), 32)
            nc.scalar.activation(hb[:, 0:4], V("b_in", 0, 4), ACT.Copy, scale=0.125).then_inc(sem("s_hb"), 1)
            nc.scalar.activation(hb[:, 4:20], V("b_in", 28, 16), ACT.Copy, scale=0.5).then_inc(sem("s_hb"), 1)
            nc.scalar.activation(hb[:, 44:76], V("b_rg", 0, 32), ACT.Copy, scale=0.5).then_inc(sem("s_hb"), 1)
            act.wait_ge(sem("s_hb"), 3)
            nc.scalar.activation(cl[:, 0], V("lam", 0, 16), ACT.Abs).then_inc(sem("s_cl"), 1)
            act.wait_ge(sem("s_cl"), 1)
            nc.scalar.activation(cl[:, 1], cl[:, 0], ACT.Exp, scale=-1.0).then_inc(sem("s_cl"), 1)
            for k in range(KT):
                act.wait_ge(sem(f"s_x{k}"), 16)
                square(0, k)
            split_hi(act, 0, 0, 0, None)
            split_hi(act, 1, 1, 0, None)
            norm_hi(0)
            attention(1)
            st = STAGES["pool"]

            def row_out(n):
                st_, g = divmod(n, 3)
                act.wait_ge(sem("s_row"), n + 1)
                src = pa[0:4, 2 * (n % 2):2 * (n % 2) + 2].rearrange("p c n -> p (c n)")
                dst = (mrow if st_ == 0 else lrow)[:, g]
                dil = DIL[g]
                if dil > 1:
                    dst = dst.rearrange("p (l z) -> p z l", z=dil)
                    src = src.rearrange("p (z l) -> p z l", z=dil)
                nc.scalar.activation(dst, src, ACT.Copy).then_inc(sem("s_rowc"), 1)

            def z_out(z):
                u, t = st.u + z - 4, st.t + z - 4
                split_hi(act, u + 2, u % 2, (u + 2) // 2, t + 1)
                act.wait_ge(s_mm, t + 1)
                nc.scalar.activation(res[0:PW, z], pair_flat(t, PW), ACT.Copy).then_inc(s_outA, 1)

            def pool_hi(z):
                act.wait_ge(sem("s_pooled"), z + 1)
                nc.scalar.activation(b_hi[0:PW, z], res[0:PW, z], ACT.Copy).then_inc(sem("s_plhi"), 1)

            def mixed_hi(g):
                t = st.t + 4 + 2 * g
                split_hi(act, st.u + 6 + g, (st.u + g) % 2, (st.u + 6 + g) // 2, t + 2)
                act.wait_ge(s_mm, t + 2)
                for o in range(2):
                    nc.scalar.activation(b_hi[0:PW, 2 * g + o], group_out(g, o), ACT.Copy,
                                         scale=vec[0:PW, VEC["p_scale"] + 2 * g + o:VEC["p_scale"] + 2 * g + o + 1]
                                         ).then_inc(sem("s_pmhi"), 1)

            z_out(4)
            for n in range(6):
                row_out(n)
            act.wait_ge(sem("s_rowd"), 3)
            nc.scalar.activation(mrow[:], mrow[:], ACT.Exp, scale=-1.0).then_inc(sem("s_rowe"), 1)
            z_out(5)
            z_out(6)
            z_out(7)
            for a in range(2):
                act.wait_ge(sem("s_mgd"), 2 * (a + 1))
                nc.scalar.activation(att1_hi[:, a], mg[:, a], ACT.Copy).then_inc(sem("s_a1hi"), 1)
            act.wait_ge(sem("s_bcu"), 12)
            for z in range(8):
                pool_hi(z)
                if z in (3, 6):
                    mixed_hi(z // 3 - 1)
            mixed_hi(2)
            mixed_hi(3)

            def gates(name, per, hb0=None, n0=0):
                st = STAGES[name]
                s_z = sem(f"s_z{name}")
                with act.Fori(0, KT - n0) as n:
                    for o in range(per):
                        u = st.u + per * n + o
                        t1 = st.t + per * n + o + 1
                        split_hi(act, u + 2, (st.u + o) % 2, (st.u + o + 2) // 2 + (per // 2) * n, t1)
                        if o % 2 == 0:
                            act.wait_ge(s_mm, t1)
                            z = o // 2
                            if name == "mrg1":
                                act.wait_ge(sem("s_gsum"), n + 1)
                            else:
                                act.wait_ge(s_outD, st.d + n)
                            kw = {}
                            if hb0 is not None:
                                nc.scalar.activation(gate_b[:], hb[:, bass.ds(hb0 + n, 1)], ACT.Copy
                                                     ).then_inc(sem(f"s_gb{name}"), 1)
                                act.wait_ge(sem(f"s_gb{name}"), n + 1)
                                kw = {"bias": gate_b[:]}
                            nc.scalar.activation(zt[:, z], pair_flat(st.t + o), ACT.Tanh, scale=0.5,
                                                 **kw).then_inc(s_outA, 1)

            gates("mrg1", 4)

            def out_stage(b):
                st = STAGES[f"out{b}"]
                n = 1 if b == 1 else 3
                act.wait_ge(s_mm, st.t)
                for k in range(KT):
                    if b == 1:
                        act.wait_ge(sem("s_gsum"), k + 2)
                    else:
                        act.wait_ge(s_outD, STAGES["mrg2"].d + k + 1)
                    nc.scalar.activation(a_hi[:, k], res[:, k], ACT.Copy, scale=0.5).then_inc(sem(f"s_mhi{b}"), 1)
                for m in range(KT):
                    split_hi(act, st.u + m + 2, m % 2, (st.u + m + 2) // 2, st.t + m + 1)
                    act.wait_ge(s_outD, st.d + m + 1)
                    nc.scalar.activation(b_hi[:, m], res[:, m], ACT.Copy, scale=V("g_mlp" if b == 1 else "g_ln2", m)
                                         ).then_inc(sem(f"s_bhi{b}"), 1)
                    square(n, m)

            out_stage(1)

            def mlp(b):
                st = STAGES[f"mlp{b}"]
                s_sqr, s_hhi = sem(f"s_sqr{b}"), sem(f"s_hhi{b}")

                def hidden(u, t, d, h0, slot):
                    for j in range(4):
                        act.wait_ge(s_w[j % 2], 8 * (u + j + 2 - j % 2) + 16)
                        act.wait_ge(s_mm, t + j + 1)
                        nc.scalar.activation(w_hi[:, j % 2], w_raw[:, j % 2], ACT.Copy).then_inc(s_whi, 1)
                        act.wait_ge(s_outD, d + j + 1)
                        nc.scalar.activation(zt[:, j % 2], zt[:, j % 2], ACT.Square).then_inc(s_sqr, 1)
                        act.wait_ge(s_sqr, h0 + j + 1)
                        nc.scalar.activation(a_hi[:, 4 * slot + j], zt[:, j % 2], ACT.Copy).then_inc(s_hhi, 1)

                def down(u, t):
                    for j in range(4):
                        act.wait_ge(s_w[j % 2], 8 * (u + j + 2 - j % 2) + 16)
                        act.wait_ge(s_mm, t + 2 * j + 2)
                        nc.scalar.activation(w_hi[:, j % 2], w_raw[:, j % 2], ACT.Copy).then_inc(s_whi, 1)

                copy_rb(1 if b == 1 else 3)
                hidden(st.u, st.t, st.d, 0, 0)
                with act.Fori(0, 3) as i:
                    for e in range(2):
                        hidden(st.u + 4 + 8 * e + 16 * i, st.t + 4 + 12 * e + 24 * i, st.d + 4 + 12 * e + 24 * i,
                               4 + 4 * e + 8 * i, 1 - e)
                        down(st.u + 8 + 8 * e + 16 * i, st.t + 8 + 12 * e + 24 * i)
                hidden(st.u + 52, st.t + 76, st.d + 76, 28, 1)
                down(st.u + 56, st.t + 80)
                n = 2 if b == 1 else 4
                for j in range(4):
                    u = st.u + 60 + j
                    if u + 2 < N_UNITS:
                        act.wait_ge(s_w[j % 2], 8 * (u + 2 - j % 2) + 16)
                        act.wait_ge(s_mm, st.t + 88 + 2 * j + 2)
                        nc.scalar.activation(w_hi[:, j % 2], w_raw[:, j % 2], ACT.Copy).then_inc(s_whi, 1)
                    for o in range(2):
                        m = 2 * j + o
                        act.wait_ge(s_outD, st.d + 88 + m + 1)
                        square(n, m)
                        if b == 1:
                            if m >= 2:
                                act.wait_ge(sem("s_sqgs"), m - 1)
                            nc.scalar.activation(sqsum_g[:] if m == 0 else sq_g[:], res[:, m], ACT.Square,
                                                 scale=V("g_fin", m)).then_inc(sem("s_sqg"), 1)

            mlp(1)
            norm_hi(2)
            attention(2)
            st = STAGES["gat0"]
            for j in range(U_GAT0):
                split_hi(act, st.u + j + 2, (st.u + j) % 2, (st.u + j + 2) // 2, st.t + 2 * j + 2)
            gates("gatt", 2, 4 + 4, 4)

            st = STAGES["rec"]
            s_thr = sem("s_thr")

            def u_out(c, u, t):
                act.wait_ge(s_mm, t + 1)
                act.wait_ge(sem("s_urpad"), 2)
                if c >= 2:
                    act.wait_ge(sem("s_conv"), c - 1)
                nc.scalar.activation(ur[c % 2][:, 2:2 + S], pair_flat(t), ACT.Identity, bias=V("b_in", 12 + c)
                                     ).then_inc(s_outA, 1)
                split_hi(act, u + 2, u % 2, (u + 2) // 2, t + 1)

            def y_out(c, u, t):
                split_hi(act, u + 2, u % 2, (u + 2) // 2, t + 1)
                act.wait_ge(s_mm, t + 1)
                if c >= 2:
                    act.wait_ge(sem("s_rec"), c - 1)
                nc.scalar.activation(y_in[:, c % 2], pair_flat(t), ACT.Identity, bias=V("b_in", 20 + c)
                                     ).then_inc(s_outA, 1)

            def u_split(c):
                act.wait_ge(sem("s_conv"), c + 1)
                if c:
                    act.wait_ge(s_mm, gate_t(c - 1) + 4)
                nc.scalar.activation(uh[:], uc[:, c % 2], ACT.Copy).then_inc(sem("s_uh"), 1)

            def gate_t(c):
                return st.t + 1 + 6 * c + (2 if c < KT - 1 else 1)

            def gate_out(c, u):
                t = gate_t(c)
                for o in range(4):
                    act.wait_ge(s_mm, t + o + 1)
                    if c and o == 0:
                        act.wait_ge(sem("s_scan"), 2 * c)
                    nc.scalar.activation(th[:, o], pair_flat(t + o), ACT.Tanh, scale=0.5,
                                         bias=hb[:, 44 + 8 * o + c:45 + 8 * o + c]).then_inc(s_outA, 1)
                split_hi(act, u + 2, u % 2, (u + 2) // 2, t + 4)
                if c:
                    act.wait_ge(sem("s_rec"), c)
                nc.scalar.activation(gt[:], y_in[:, c % 2], ACT.Square).then_inc(sem("s_gsq"), 1)
                for d in range(2):
                    act.wait_ge(s_outA, st.a + (t - st.t) + 2 * d + 1)
                    nc.scalar.activation(tm[:, d], th[:, 2 * d], ACT.Tanh, scale=cl[:, 4, 8 * d + c:8 * d + c + 1],
                                         bias=cl[:, 4, 8 * d + c:8 * d + c + 1]).then_inc(s_thr, 1)
                    act.wait_ge(s_thr, 3 * c + d + 1)
                    nc.scalar.activation(th[:, 2 * d], th[:, 2 * d], ACT.Exp, scale=cl[:, 5, 8 * d + c:8 * d + c + 1],
                                         bias=cl[:, 5, 8 * d + c:8 * d + c + 1]).then_inc(sem("s_dec"), 1)
                act.wait_ge(sem("s_gin"), c + 1)
                nc.scalar.activation(gt[:], gt[:], ACT.Tanh, scale=0.7978845608028654).then_inc(s_thr, 1)
                for d in range(2):
                    act.wait_ge(sem("s_neg"), 2 * c + d + 1)
                    nc.scalar.activation(tm[:, d], tm[:, d], ACT.Sqrt).then_inc(sem("s_root"), 1)
                if c:
                    act.wait_ge(sem("s_warm"), c)
                nc.scalar.activation(warm[:], ones[:, 0:1], ACT.Tanh).then_inc(sem("s_warm"), 1)

            act.wait_ge(sem("s_cldone"), 1)
            u_out(0, st.u, st.t)
            for c in range(KT):
                y_out(c, st.u + 1 + 3 * c, st.t + 1 + 6 * c)
                u_split(c)
                if c < KT - 1:
                    u_out(c + 1, st.u + 2 + 3 * c, st.t + 2 + 6 * c)
                gate_out(c, st.u + 3 + 3 * c if c < KT - 1 else st.u + 23)
            act.wait_ge(s_mm, gate_t(KT - 1) + 4)
            for n, k in enumerate(REC_ORDER):
                act.wait_ge(sem("s_rec"), KT if n >= 3 else KT - 1)
                nc.scalar.activation(r_hi[:, k], rec[:, k], ACT.Copy).then_inc(sem("s_rhi"), 1)
            st = STAGES["mrg2"]
            with act.Fori(0, KT // 2) as i:
                for o in range(4):
                    t1 = st.t + 4 * i + o + 1
                    split_hi(act, st.u + 4 * i + o + 2, (st.u + o) % 2, (st.u + o + 2) // 2 + 2 * i, t1)
                    if o < 2:
                        n = 2 * i + o
                        act.wait_ge(s_outD, st.d + n - 1)
                        act.wait_ge(s_outA, st.a + n)
                        nc.scalar.activation(gate_b[:], hb[:, bass.ds(12 + n, 1)], ACT.Copy).then_inc(sem("s_gb2"), 1)
                        act.wait_ge(sem("s_gb2"), n + 1)
                        act.wait_ge(s_mm, t1)
                        nc.scalar.activation(zt[:, o], pair_flat(st.t + o), ACT.Tanh, scale=0.5, bias=gate_b[:]
                                             ).then_inc(s_outA, 1)
            out_stage(2)
            mlp(2)

        @block.vector
        def _(dve):
            def add_square(n, k):
                if k == 0:
                    return
                dve.wait_ge(sem("s_sq"), KT * n + k + 1)
                if k > 1:
                    dve.wait_ge(sem("s_sqs"), 7 * n + k - 1)
                nc.vector.tensor_tensor(sqsum[:], sqsum[:], sq[:, k % 2], ALU.add).then_inc(sem("s_sqs"), 1)

            def spread_diag(out, r):
                nc.vector.tensor_tensor(out[:], ident.unsqueeze(1).broadcast_to([P, KT, P]),
                                        r[:].unsqueeze(2).broadcast_to([P, KT, P]), ALU.mult
                                        ).then_inc(sem("s_diag"), 1)

            def rms(n):
                i = SPREADS[n] - 1
                dve.wait_ge(sem("s_stat"), n + 1)
                nc.vector.tensor_scalar(ms[:], pa[:, 0, 0:8], 1.0 / D, EPS, ALU.mult, ALU.add).then_inc(sem("s_ms"), 1)
                dve.wait_ge(sem("s_rstd"), i + 1)
                spread_diag(diag, rstd)

            def scale_tiles(n, gain, inplace=None):
                dve.wait_ge(sem("s_bc"), SPREADS[n] - (n == 2))
                bc = pa[:, 2:4].rearrange("p c n -> p (c n)")
                def lo(k):
                    dve.wait_ge(sem("s_nh"), KT * SPLIT_NORM[n] + k + 1)
                    nc.vector.tensor_tensor(a_lo[:, k], normed(k), a_hi[:, k].bitcast(F32),
                                            ALU.subtract).then_inc(sem("s_nle"), 1)

                for k in range(KT):
                    if inplace is None and k >= 4:
                        dve.wait_ge(sem("s_nlo" if k % 2 else "s_nle"), 4 * SPLIT_NORM[n] + (k - 4) // 2 + 1)
                    dst = normed(k) if inplace is None else res[:, k]
                    nc.vector.scalar_tensor_tensor(out=dst, in0=res[:, k], scalar=gain[:, k:k + 1], in1=bc,
                                                   op0=ALU.mult, op1=ALU.mult
                                                   ).then_inc(sem("s_nd") if inplace is None else sem(inplace), 1)
                    if inplace is None and k % 2:
                        lo(k - 1)

            def two_norms():
                dve.wait_ge(sem("s_stat"), 3)
                nc.vector.tensor_scalar(ms[:], pa[:, 0, 0:8], 1.0 / D, EPS, ALU.mult, ALU.add).then_inc(sem("s_ms"), 1)
                dve.wait_ge(sem("s_statg"), 1)
                link(nc.vector.tensor_scalar(msg[:], pa[:, 1, 0:8], 1.0 / D, None, ALU.mult))
                dve.wait_ge(sem("s_rstd"), 3)
                link(nc.vector.tensor_tensor(msg[:], msg[:], rstd[:], ALU.mult))
                link(nc.vector.tensor_tensor(msg[:], msg[:], rstd[:], ALU.mult))
                link(nc.vector.tensor_scalar(rstd1[:], rstd[:], 1.0, None, ALU.mult))
                nc.vector.tensor_scalar(ms[:], msg[:], EPS, None, ALU.add).then_inc(sem("s_ms"), 1)
                spread_diag(diag_r, rstd1)
                dve.wait_ge(sem("s_rstd"), 4)
                dve.wait_ge(sem("s_diag"), 3)
                link(nc.vector.tensor_tensor(rstd1[:], rstd1[:], rstd[:], ALU.mult))
                spread_diag(diag, rstd1)
                scale_tiles(2, gg)
                dve.wait_ge(sem("s_bc"), SPREADS[2])
                bc = pa[:, 0:2].rearrange("p c n -> p (c n)")
                for k in range(KT):
                    nc.vector.scalar_tensor_tensor(out=res[:, k], in0=res[:, k], scalar=V("g_fin", k), in1=bc,
                                                   op0=ALU.mult, op1=ALU.mult).then_inc(sem("s_nrm1"), 1)

            def pooled(z):
                dve.wait_ge(sem("s_wsum"), z + 1)
                g = z // 2
                src, zz = win[0:PW, g % 2], res[0:PW, z]
                link(nc.vector.tensor_tensor(first16[0:PW], src[:, PADL:PADL + 16], invc[0:PW, g], ALU.mult))
                link(nc.vector.tensor_tensor(zz[:, 0:16], first16[0:PW], zz[:, 0:16], ALU.subtract))
                nc.vector.scalar_tensor_tensor(out=zz[:, 16:], in0=src[:, PADL + 16:], scalar=1.0 / WINDOWS[g],
                                               in1=zz[:, 16:], op0=ALU.mult, op1=ALU.subtract
                                               ).then_inc(sem("s_pooled"), 1)

            POOL_STEPS = {t: unit_at(1, t) - 3 * N_PAIR1 for t in range(N_PAIR1 * UNITS_PER_PAIR)
                          if (unit_at(1, t) or 0) >= 3 * N_PAIR1}

            def attention(b):
                st = STAGES[f"att{b}"]
                sm = sm1 if b == 1 else sm2
                s_S, s_add, s_max, s_exp, s_rl, s_pn, s_T, s_oev = [sem(f"s_{x}{b}") for x in (
                    "S", "add", "max", "exp", "rl", "pn", "T", "oev")]
                npair = NP_[b]
                nt = npair * UNITS_PER_PAIR

                def add_max(j):
                    p, idx = divmod(j, UNITS_PER_PAIR)
                    _, hh, i = tile_of(idx)
                    w = width(b, j)
                    dve.wait_ge(s_S, j + 1)
                    if j >= 3:
                        dve.wait_ge(s_T, j - 2)
                    sc = pa[:, j % 2, 0:w]
                    if b == 1:
                        g = p // 2
                        dist = dist2 if g == 2 else dist0[:, 256 - w:256]
                        nc.vector.scalar_tensor_tensor(out=sm[:, j % 3, 0:w], in0=dist,
                                                       scalar=-SLOPE[2 * p + hh] * DIL[g], in1=sc,
                                                       op0=ALU.mult, op1=ALU.add).then_inc(s_add, 1)
                    else:
                        dve.wait_ge(sem("s_bm"), j + 1)
                        nc.vector.tensor_tensor(sm[:, j % 3, 0:w], bm[:, j % 4], sc, ALU.add).then_inc(s_add, 1)
                    dve.wait_ge(s_add, j + 1)
                    nc.vector.tensor_reduce(stat(negm, b, j), sm[:, j % 3, 0:w], axis=AXX, op=ALU.max,
                                            negate=True).then_inc(s_max, 1)

                def normalise(j):
                    w = width(b, j)
                    dve.wait_ge(s_exp, j + 1)
                    nc.vector.reciprocal(rl[:, j:j + 1], stat(lsum, b, j)).then_inc(s_rl, 1)
                    dve.wait_ge(s_rl, j + 1)
                    nc.vector.tensor_scalar(sm[:, j % 3, 0:w], sm[:, j % 3, 0:w], rl[:, j:j + 1], None,
                                            ALU.mult).then_inc(s_pn, 1)

                def weights(m):
                    split_lo(dve, st.u + m + 2, (st.u + m) % 2, st.t + m + 1)

                for m in range(AHEAD):
                    weights(m)
                for t in range(nt + 1):
                    p, idx = divmod(t, UNITS_PER_PAIR)
                    if t < nt:
                        add_max(t)
                    if t >= 1:
                        normalise(t - 1)
                    if unit_at(b, t) is not None:
                        weights(unit_at(b, t))
                    if b == 1 and t - 5 in POOL_STEPS:
                        pooled(POOL_STEPS[t - 5])
                    if b == 2 and t >= 19 and (t - 19) % 16 == 0:
                        a2_lo((t - 19) // 16)
                if b == 2:
                    a2_lo(npair - 1)

            def a2_lo(p):
                dve.wait_ge(sem("s_a2hi"), p + 1)
                nc.vector.tensor_tensor(att2_lo[:, p], o2[:, p % 2], att2_hi[:, p].bitcast(F32),
                                        ALU.subtract).then_inc(sem("s_a2lo"), 1)

            chain = sem("s_chain")
            nch = [0]

            def link(ins):
                nch[0] += 1
                ins.then_inc(chain, 1)
                dve.wait_ge(chain, nch[0])

            dve.wait_ge(sem("s_const"), 32)
            dve.wait_ge(sem("s_cl"), 2)
            link(nc.vector.tensor_tensor(gg[:], V("g_fin", 0, 8), V("g_ln1", 0, 8), ALU.mult))
            link(nc.vector.tensor_scalar(cl[:, 2], cl[:, 1], 2.0, None, ALU.add))
            link(nc.vector.reciprocal(cl[:, 3], cl[:, 2]))
            link(nc.vector.tensor_tensor(cl[:, 1], cl[:, 1], cl[:, 3], ALU.mult))
            link(nc.vector.tensor_tensor(cl[:, 2], cl[:, 1], cl[:, 1], ALU.mult))
            link(nc.vector.memset(cl[:, 3], 1.0 / 17))
            for i in range(7, -1, -1):
                link(nc.vector.tensor_tensor(cl[:, 3], cl[:, 3], cl[:, 2], ALU.mult))
                link(nc.vector.tensor_scalar(cl[:, 3], cl[:, 3], 1.0 / (2 * i + 1), None, ALU.add))
            link(nc.vector.tensor_tensor(cl[:, 3], cl[:, 3], cl[:, 1], ALU.mult))
            link(nc.vector.tensor_scalar(cl[:, 0], V("lam", 0, 16), -1.0, 0.0, ALU.mult, ALU.max))
            link(nc.vector.scalar_tensor_tensor(out=cl[:, 0], in0=cl[:, 3], scalar=2.0, in1=cl[:, 0],
                                                op0=ALU.mult, op1=ALU.add))
            link(nc.vector.tensor_scalar(cl[:, 4], cl[:, 0], -2.0, None, ALU.mult))
            nc.vector.tensor_scalar(cl[:, 5], cl[:, 0], -4.0, None, ALU.mult).then_inc(sem("s_cldone"), 1)
            for k in range(KT):
                add_square(0, k)
            rms(0)
            scale_tiles(0, V("g_mix", 0, 8))
            split_lo(dve, 0, 0, None)
            split_lo(dve, 1, 1, None)
            attention(1)
            split_lo(dve, STAGES["pool"].u + 2, STAGES["pool"].u % 2, STAGES["pool"].t + 1)
            dve.wait_ge(sem("s_rowc"), 3)
            link(nc.vector.tensor_tensor(mmin[:], mrow[:, 0], mrow[:, 1], ALU.min))
            link(nc.vector.tensor_tensor(mmin[:], mmin[:], mrow[:, 2], ALU.min))
            for g in range(3):
                nc.vector.tensor_tensor(mrow[:, g], mrow[:, g], mmin[:], ALU.subtract).then_inc(sem("s_rowd"), 1)
            st = STAGES["pool"]

            def weights(i):
                dones = i + 1 if i < 4 else 4 + 2 * (i - 3)
                split_lo(dve, st.u + i + 2, (st.u + i) % 2, st.t + dones)

            pooled(3)
            dve.wait_ge(sem("s_rowe"), 1)
            dve.wait_ge(sem("s_rowc"), 6)
            link(nc.vector.tensor_tensor(lrow[:], lrow[:], mrow[:], ALU.mult))
            link(nc.vector.tensor_tensor(den[:], lrow[:, 0], lrow[:, 1], ALU.add))
            link(nc.vector.tensor_tensor(den[:], den[:], lrow[:, 2], ALU.add))
            link(nc.vector.reciprocal(mmin[:], den[:]))
            weights(1)
            for g in range(3):
                nc.vector.tensor_tensor(lrow[:, g], lrow[:, g], mmin[:], ALU.mult).then_inc(sem("s_wts"), 1)
            pooled(4)
            weights(2)
            nb = 0
            for a in range(2):
                for c in range(2):
                    cs = slice(c * HC, (c + 1) * HC)
                    for g in range(3):
                        dve.wait_ge(sem("s_bcm"), nb + 1)
                        bc = pa[:, nb % 4]
                        dst = mg[:, a, cs] if g == 0 else mgt[:, g - 1]
                        nb += 1
                        nc.vector.tensor_tensor(dst, og[:, 2 * g + a, cs], bc, ALU.mult).then_inc(sem("s_bcu"), 1)
                        if nb == 6:
                            pooled(5)
                        if nb == 12:
                            pooled(6)
                        dve.wait_ge(sem("s_bcu"), nb)
                        if g:
                            ins = nc.vector.tensor_tensor(mg[:, a, cs], mg[:, a, cs], mgt[:, g - 1], ALU.add)
                            if g == 2:
                                ins.then_inc(sem("s_mgd"), 1)
                                dve.wait_ge(sem("s_mgd"), 2 * a + c + 1)
                            else:
                                link(ins)
            for a in range(2):
                dve.wait_ge(sem("s_a1hi"), a + 1)
                nc.vector.tensor_tensor(att1_lo[:, a], mg[:, a], att1_hi[:, a].bitcast(F32),
                                        ALU.subtract).then_inc(sem("s_a1lo"), 1)
            weights(3)

            def pool_lo(z):
                dve.wait_ge(sem("s_plhi"), z + 1)
                nc.vector.tensor_tensor(b_lo[0:PW, z], res[0:PW, z], b_hi[0:PW, z].bitcast(F32),
                                        ALU.subtract).then_inc(sem("s_pllo"), 1)

            def mixed_lo(g):
                t = st.t + 4 + 2 * g
                weights(4 + g)
                for o in range(2):
                    dve.wait_ge(sem("s_pmhi"), 2 * g + o + 1)
                    nc.vector.scalar_tensor_tensor(
                        out=b_lo[0:PW, 2 * g + o], in0=group_out(g, o),
                        scalar=vec[0:PW, VEC["p_scale"] + 2 * g + o:VEC["p_scale"] + 2 * g + o + 1],
                        in1=b_hi[0:PW, 2 * g + o].bitcast(F32), op0=ALU.mult, op1=ALU.subtract).then_inc(s_outD, 1)

            for z in range(7):
                if z == 6:
                    pooled(7)
                pool_lo(z)
                if z in (3, 6):
                    mixed_lo(z // 3 - 1)
            pool_lo(7)
            mixed_lo(2)
            mixed_lo(3)
            st = STAGES["mrg1"]
            with dve.Fori(0, KT) as n:
                for o in range(4):
                    u, t1 = st.u + 4 * n + o, st.t + 4 * n + o + 1
                    split_lo(dve, u + 2, (st.u + o) % 2, t1)
                    if o % 2 == 1:
                        dve.wait_ge(s_outA, st.a + 2 * n + o // 2 + 1)
                        dve.wait_ge(s_mm, t1)
                        nc.vector.scalar_tensor_tensor(out=zt[:, o // 2], in0=zt[:, o // 2], scalar=1.0,
                                                       in1=pair_flat(st.t + o), op0=ALU.add, op1=ALU.mult
                                                       ).then_inc(s_outD, 1)

            def out_stage(b):
                st = STAGES[f"out{b}"]
                for k in range(KT):
                    dve.wait_ge(sem(f"s_mhi{b}"), k + 1)
                    nc.vector.scalar_tensor_tensor(out=a_lo[:, k], in0=res[:, k], scalar=0.5,
                                                   in1=a_hi[:, k].bitcast(F32), op0=ALU.mult, op1=ALU.subtract
                                                   ).then_inc(sem(f"s_msplit{b}"), 1)
                for m in range(KT):
                    split_lo(dve, st.u + m + 2, m % 2, st.t + m + 1)
                    dve.wait_ge(s_mm, st.t + m + 1)
                    dve.wait_ge(sem(f"s_xr{b}{m % 2}"), 16 * (m // 2 + 1))
                    nc.vector.tensor_tensor(res[:, m], pair_flat(st.t + m), zt[:, m % 2], ALU.add).then_inc(s_outD, 1)
                    dve.wait_ge(sem(f"s_bhi{b}"), m + 1)
                    nc.vector.scalar_tensor_tensor(out=b_lo[:, m], in0=res[:, m],
                                                   scalar=V("g_mlp" if b == 1 else "g_ln2", m),
                                                   in1=b_hi[:, m].bitcast(F32), op0=ALU.mult, op1=ALU.subtract
                                                   ).then_inc(sem(f"s_blo{b}"), 1)
                    add_square(1 if b == 1 else 3, m)

            out_stage(1)

            def mlp(b):
                st = STAGES[f"mlp{b}"]
                s_hhi, s_hlo = sem(f"s_hhi{b}"), sem(f"s_hlo{b}")

                def hidden(u, t, tp, h0, slot):
                    for j in range(4):
                        split_lo(dve, u + j + 2, j % 2, t + j + 1)
                        dve.wait_ge(s_mm, t + j + 1)
                        nc.vector.scalar_tensor_tensor(out=zt[:, j % 2], in0=pair_flat(tp + j), scalar=0.0, in1=rb[:],
                                                       op0=ALU.max, op1=ALU.mult
                                                       ).then_inc(s_outD, 1)
                        dve.wait_ge(s_hhi, h0 + j + 1)
                        nc.vector.tensor_tensor(a_lo[:, 4 * slot + j], zt[:, j % 2], a_hi[:, 4 * slot + j].bitcast(F32),
                                                ALU.subtract).then_inc(s_hlo, 1)

                def down(u, t, tp, n=None):
                    for j in range(4):
                        for o in range(2):
                            m = 2 * j + o
                            if o == 1 and not (isinstance(u, int) and u + j + 2 >= N_UNITS):
                                split_lo(dve, u + j + 2, j % 2, t + 2 * j + 2)
                            dve.wait_ge(s_mm, t + m + 1)
                            nc.vector.tensor_tensor(res[:, m], pair_flat(tp + m), res[:, m], ALU.add
                                                    ).then_inc(s_outD, 1)
                            if n is not None:
                                add_square(n, m)
                                if b == 1 and m:
                                    dve.wait_ge(sem("s_sqg"), m + 1)
                                    if m > 1:
                                        dve.wait_ge(sem("s_sqgs"), m - 1)
                                    nc.vector.tensor_tensor(sqsum_g[:], sqsum_g[:], sq_g[:], ALU.add
                                                            ).then_inc(sem("s_sqgs"), 1)

                rms(1 if b == 1 else 3)
                dve.wait_ge(sem("s_rb"), b)
                hidden(st.u, st.t, st.t, 0, 0)
                with dve.Fori(0, 3) as i:
                    for e in range(2):
                        hidden(st.u + 4 + 8 * e + 16 * i, st.t + 4 + 12 * e + 24 * i, st.t,
                               4 + 4 * e + 8 * i, 1 - e)
                        down(st.u + 8 + 8 * e + 16 * i, st.t + 8 + 12 * e + 24 * i, st.t)
                hidden(st.u + 52, st.t + 76, st.t, 28, 1)
                down(st.u + 56, st.t + 80, st.t)
                down(st.u + 60, st.t + 88, st.t, 2 if b == 1 else 4)

            mlp(1)
            two_norms()
            attention(2)

            st = STAGES["gat0"]
            for n in range(4):
                if n % 2:
                    split_lo(dve, st.u + n // 2 + 2, (st.u + n // 2) % 2, st.t + n + 1)
                dve.wait_ge(s_mm, st.t + n + 1)
                nc.vector.scalar_tensor_tensor(out=res[:, n], in0=(tg01 if n < 2 else tg23)[:, n % 2], scalar=1.0,
                                               in1=pair_flat(st.t + n), op0=ALU.add, op1=ALU.mult
                                               ).then_inc(s_outD, 1)
            st = STAGES["gatt"]
            with dve.Fori(0, KT - 4) as n:
                for o in range(2):
                    split_lo(dve, st.u + 2 * n + o + 2, (st.u + o) % 2, st.t + 2 * n + o + 1)
                dve.wait_ge(s_outA, st.a + n + 1)
                nc.vector.scalar_tensor_tensor(out=res[:, bass.ds(4 + n, 1)].rearrange("p a b -> p (a b)"),
                                               in0=zt[:, 0], scalar=1.0,
                                               in1=pair_flat(st.t + 1), op0=ALU.add, op1=ALU.mult
                                               ).then_inc(s_outD, 1)

            st = STAGES["rec"]

            def conv(c):
                dve.wait_ge(s_outA, st.a + (1 if c == 0 else 3 + 6 * (c - 1)))
                if c >= 2:
                    dve.wait_ge(sem("s_rec"), c - 1)
                dst = uc[:, c % 2]
                w = [V("conv_w", 8 * j + c) for j in range(4)]
                link(nc.vector.tensor_scalar(dst, ur[c % 2][:, 0:S], w[0], V("conv_b", c), ALU.mult, ALU.add))
                for j in (1, 2, 3):
                    ins = nc.vector.scalar_tensor_tensor(out=dst, in0=ur[c % 2][:, j:j + S], scalar=w[j], in1=dst,
                                                         op0=ALU.mult, op1=ALU.add)
                    if j < 3:
                        link(ins)
                ins.then_inc(sem("s_conv"), 1)

            def direction(c, d):
                a, i = th[:, 2 * d], th[:, 2 * d + 1]
                dve.wait_ge(sem("s_dec"), 2 * c + d + 1)
                link(nc.vector.scalar_tensor_tensor(out=i, in0=i, scalar=1.0, in1=uc[:, c % 2],
                                                    op0=ALU.add, op1=ALU.mult))
                dve.wait_ge(sem("s_root"), 2 * c + d + 1)
                link(nc.vector.scalar_tensor_tensor(out=tm[:, d], in0=a, scalar=1.0, in1=tm[:, d],
                                                    op0=ALU.add, op1=ALU.mult))
                link(nc.vector.scalar_tensor_tensor(out=i, in0=i, scalar=0.5, in1=tm[:, d],
                                                    op0=ALU.mult, op1=ALU.mult))
                if d == 0:
                    ins = nc.vector.tensor_tensor_scan(tm[:, 0], a, i, 0.0, ALU.mult, ALU.add)
                else:
                    ins = nc.vector.tensor_tensor_scan(tm[:, 1, ::-1], a[:, ::-1], i[:, ::-1], 0.0, ALU.mult, ALU.add)
                ins.then_inc(sem("s_scan"), 1)

            def guards(c):
                dve.wait_ge(sem("s_gsq"), c + 1)
                nc.vector.tensor_scalar(gt[:], gt[:], 0.044715, 1.0, ALU.mult, ALU.add).then_inc(sem("s_gpoly"), 1)
                for d in range(2):
                    dve.wait_ge(sem("s_thr"), 3 * c + d + 1)
                    nc.vector.tensor_scalar(tm[:, d], tm[:, d], -1.0, 0.0, ALU.mult, ALU.max).then_inc(sem("s_neg"), 1)

            def gelu(c):
                dve.wait_ge(sem("s_thr"), 3 * c + 3)
                link(nc.vector.scalar_tensor_tensor(out=gt[:], in0=gt[:], scalar=1.0, in1=y_in[:, c % 2],
                                                    op0=ALU.add, op1=ALU.mult))

            def output(c):
                dve.wait_ge(sem("s_dirs"), c + 1)
                nc.vector.scalar_tensor_tensor(out=rec[:, c], in0=gt[:], scalar=0.5, in1=tm[:, 0],
                                               op0=ALU.mult, op1=ALU.mult).then_inc(sem("s_rec"), 1)

            def unit_y(c):
                split_lo(dve, st.u + 3 + 3 * c, (st.u + 1 + 3 * c) % 2, st.t + 2 + 6 * c)

            def unit_u(c):
                split_lo(dve, st.u + 1 + 3 * c, (st.u - 1 + 3 * c) % 2, st.t + 3 + 6 * (c - 1))

            def unit_gates(c):
                if c < KT - 1:
                    split_lo(dve, st.u + 5 + 3 * c, (st.u + 1 + 3 * c) % 2, st.t + 7 + 6 * c)
                else:
                    split_lo(dve, st.u + 25, (st.u + 1) % 2, st.t + 48)

            for i in range(2):
                nc.vector.memset(ur[i][:], 0.0).then_inc(sem("s_urpad"), 1)
            split_lo(dve, st.u + 2, st.u % 2, st.t + 1)
            conv(0)
            unit_y(0)
            unit_u(1)
            conv(1)
            unit_gates(0)
            for c in range(KT):
                guards(c)
                direction(c, 0)
                if c < KT - 1:
                    unit_y(c + 1)
                direction(c, 1)
                gelu(c)
                if c < KT - 2:
                    unit_u(c + 2)
                output(c)
                if c < KT - 2:
                    conv(c + 2)
                if c < KT - 1:
                    unit_gates(c + 1)
            for n, k in enumerate(REC_ORDER):
                dve.wait_ge(sem("s_rhi"), n + 1)
                nc.vector.tensor_tensor(r_lo[:, k], rec[:, k], r_hi[:, k].bitcast(F32), ALU.subtract
                                        ).then_inc(sem("s_rlo"), 1)
            st = STAGES["mrg2"]
            with dve.Fori(0, KT // 2) as i:
                for o in range(4):
                    t1 = st.t + 4 * i + o + 1
                    split_lo(dve, st.u + 4 * i + o + 2, (st.u + o) % 2, t1)
                    if o >= 2:
                        n = 2 * i + o - 2
                        dve.wait_ge(s_outA, st.a + n + 1)
                        dve.wait_ge(s_mm, t1)
                        nc.vector.scalar_tensor_tensor(out=zt[:, o - 2], in0=zt[:, o - 2], scalar=1.0,
                                                       in1=pair_flat(st.t + o), op0=ALU.add, op1=ALU.mult
                                                       ).then_inc(sem("s_gz"), 1)
                        dve.wait_ge(sem("s_gz"), n + 1)
                        r = res[:, bass.ds(n, 1)].rearrange("p a b -> p (a b)")
                        nc.vector.tensor_tensor(r, r, zt[:, o - 2], ALU.add).then_inc(s_outD, 1)
            out_stage(2)
            mlp(2)
            rms(4)
            scale_tiles(4, V("g_lnf", 0, 8), "s_nrm2")

        @block.tensor
        def _(pe):
            def stats(n):
                if n == 0:
                    pe.wait_ge(sem("s_pc"), 1)
                pe.wait_ge(sem("s_sqs"), 7 * (n + 1))
                for i in range(8):
                    mm = nc.tensor.matmul(pa[:, 0, i:i + 1], sqsum[:, i * P:(i + 1) * P], ones[:, 0:1],
                                          start=True, stop=True)
                mm.then_inc(sem("s_stat"), 1)
                if n == 2:
                    pe.wait_ge(sem("s_sqgs"), 7)
                    for i in range(8):
                        mm = nc.tensor.matmul(pa[:, 1, i:i + 1], sqsum_g[:, i * P:(i + 1) * P], ones[:, 0:1],
                                              start=True, stop=True)
                    mm.then_inc(sem("s_statg"), 1)

            def broadcast(i, src=diag, bank=2):
                pe.wait_ge(sem("s_diag"), i + 1)
                for c in range(2):
                    mm = nc.tensor.matmul(pa[:, bank + c], ones[:], src[:, 4 * c:4 * c + 4].rearrange("p a n -> p (a n)"),
                                          start=True, stop=True)
                mm.then_inc(sem("s_bc"), 1)

            def enter(name):
                st = STAGES[name]
                if st.a:
                    pe.wait_ge(s_outA, st.a)
                if st.d:
                    pe.wait_ge(s_outD, st.d)
                return st

            def attention(b):
                st = STAGES[f"att{b}"]
                n_norm = 0 if b == 1 else 2
                vtok = vtok1 if b == 1 else vtok2
                sm, pt = (sm1, pt1) if b == 1 else (sm2, pt2)
                s_S, s_add, s_pn, s_T, s_pt, s_pv, s_oev, s_vt, s_vev = [sem(f"s_{x}{b}") for x in (
                    "S", "add", "pn", "T", "pt", "pv", "oev", "vt", "vev")]
                npair = NP_[b]
                nt = npair * UNITS_PER_PAIR
                batches = [0]

                def fill(m0, m1):
                    for i in range(m0, m1):
                        m, r = divmod(i, 48)
                        k, r = divmod(r, 6)
                        n, c = divmod(r, 2)
                        u, t = st.u + m, st.t + m
                        if k == 0 and r == 0:
                            pe.wait_ge(s_wlo, u + 1)
                            if m >= 2:
                                pe.wait_ge(s_outA, st.a + m - 1)
                        if m == 0 and r == 0:
                            pe.wait_ge(sem("s_nlo" if k % 2 else "s_nle"), 4 * SPLIT_NORM[n_norm] + k // 2 + 1)
                        w, x = ((w_hi, a_hi), (w_hi, a_lo), (w_lo, a_hi))[n]
                        mm = nc.tensor.matmul(pair(t)[:, c], w[:, u % 2, k * P:(k + 1) * P],
                                              x[:, k, c * HC:(c + 1) * HC], start=(k == 0 and n == 0),
                                              stop=(k == KT - 1 and n == 2))
                        if r == 5 and k == KT - 1:
                            mm.then_inc(s_mm, 1)

                def v_batch(n):
                    p, bt = divmod(n, VB[b])
                    pe.wait_ge(s_outA, st.a + 3 * p + 1)
                    if n:
                        pe.wait_ge(s_vev, n)
                    for a in range(4):
                        if b == 1:
                            src = qkv1[:, p % 2, 0, (4 * bt + a) * P:(4 * bt + a + 1) * P]
                        else:
                            src = v2[:, bt, a * P:(a + 1) * P]
                        mm = nc.tensor.transpose(pa[:, 2, a * P:(a + 1) * P], src, ident)
                    mm.then_inc(s_vt, 1)
                    batches[0] = n + 1

                def scores(j):
                    p, idx = divmod(j, UNITS_PER_PAIR)
                    _, hh, i = tile_of(idx)
                    w = width(b, j)
                    rows = slice(64 * hh, 64 * hh + 64)
                    if idx == 0:
                        pe.wait_ge(s_outA, st.a + 3 * p + 3)
                    if j >= 2:
                        pe.wait_ge(s_add, j - 1)
                    elif b == 2:
                        pe.wait_ge(sem("s_nrm1"), KT)
                    q, k = (qkv1[rows, p % 2, 1], qkv1[rows, p % 2, 2]) if b == 1 else (
                        qk2[rows, p % 2, 0], qk2[rows, p % 2, 1])
                    if b == 1:
                        lhsT = q[:, i * P:(i + 1) * P]
                        rhs = k[:, (i + 1) * P - w:(i + 1) * P]
                        out = pa[:, j % 2, 0:w]
                    else:
                        hf, n = divmod(i, 4)
                        lhsT = q[:, n * 256 + hf * 128:n * 256 + hf * 128 + 128]
                        c0 = COL_START[n]
                        rhs = k.rearrange("p (r c) -> p r c", c=64)[:, 4 * hf:4 * hf + 12, c0:c0 + 32]
                        out = pa[:, j % 2, 0:w].rearrange("p (r c) -> p r c", c=32)
                    nc.tensor.matmul(out, lhsT, rhs, start=True, stop=True).then_inc(s_S, 1)

                def transpose_probs(j):
                    w = width(b, j)
                    pe.wait_ge(s_pn, j + 1)
                    if j:
                        pe.wait_ge(s_pt, j)
                    pe.wait_ge(s_vev, batches[0])
                    for a in range(w // P):
                        mm = nc.tensor.transpose(pa[:, 2, a * P:(a + 1) * P], sm[:, j % 3, a * P:(a + 1) * P], ident)
                    mm.then_inc(s_T, 1)

                def values(j):
                    p, idx = divmod(j, UNITS_PER_PAIR)
                    _, hh, i = tile_of(idx)
                    nb = width(b, j) // P
                    pe.wait_ge(s_pt, j + 1)
                    if idx == 0:
                        pe.wait_ge(s_vev, VB[b] * (p + 1))
                    if idx % 4 == 0 and j >= 8:
                        pe.wait_ge(s_oev, j // 4 - 1)
                    for a in range(nb):
                        if b == 1:
                            blk = i - nb + 1 + a
                        else:
                            hf, n = divmod(i, 4)
                            blk = 4 * n + hf + a
                        mm = nc.tensor.matmul(pa[64 * hh:64 * hh + 64, 3, (i % 4) * P:(i % 4 + 1) * P],
                                              vtok[:, p % 2, blk, 64 * hh:64 * hh + 64],
                                              pt[:, j % 2, a * P:(a + 1) * P], start=(a == 0), stop=(a == nb - 1))
                    mm.then_inc(s_pv, 1)

                fill(0, 48 * 3)
                for n in range(VB[b]):
                    if n == 0:
                        pe.wait_ge(sem("s_nd"), KT * SPLIT_NORM[n_norm] + KT)
                    v_batch(n)
                    fill(48 * 3 + 48 // VB[b] * n, 48 * 3 + 48 // VB[b] * (n + 1))
                for t in range(nt + 2):
                    p, idx = divmod(t, UNITS_PER_PAIR)
                    if t < nt:
                        scores(t)
                    if p + 1 < npair and V_STEP <= idx < V_STEP + VB[b]:
                        if t >= 2:
                            pe.wait_ge(s_pt, t - 1)
                        v_batch(VB[b] * (p + 1) + idx - V_STEP)
                    if t < nt:
                        fill(48 * AHEAD + FILL * t, 48 * AHEAD + FILL * (t + 1))
                    elif b == 1:
                        fill(48 * AHEAD + FILL * nt + 24 * (t - nt), 48 * AHEAD + FILL * nt + 24 * (t - nt + 1))
                    if 1 <= t <= nt:
                        transpose_probs(t - 1)
                    if t >= 2:
                        values(t - 2)

            stats(0)
            broadcast(0)
            pe.wait_ge(sem("s_const"), 32)
            attention(1)
            pe.wait_ge(sem("s_oev1"), 4 * N_PAIR1)
            st = STAGES["pool"]

            def rows(n):
                st_, g = divmod(n, 3)
                if n >= 2:
                    pe.wait_ge(sem("s_rowc"), n - 1)
                src = negm if st_ == 0 else lsum
                for i in range(8):
                    mm = nc.tensor.matmul(pa[0:4, 2 * (n % 2) + i // 4, (i % 4) * P:(i % 4 + 1) * P],
                                          src[:, 32 * g + 4 * i:32 * g + 4 * i + 4], ident, start=True, stop=True)
                mm.then_inc(sem("s_row"), 1)

            def channels(z):
                i = z - 4
                pe.wait_ge(s_outA, st.a + i - 1)
                pe.wait_ge(s_wlo, st.u + i + 1)
                for k in range(KT):
                    mm = product((st.u + i) % 2, pair(st.t + i), a_hi, a_lo, k, k == 0, k == KT - 1, m=PW, wofs=k * P)
                    if k == KT - 1:
                        mm.then_inc(s_mm, 1)
                    if z == 7:
                        spread(4 + k)

            def spread(nb):
                a, r = divmod(nb, 6)
                c, g = divmod(r, 3)
                pe.wait_ge(sem("s_wts"), 3)
                if nb >= 4:
                    pe.wait_ge(sem("s_bcu"), nb - 3)
                nc.tensor.matmul(pa[:, nb % 4], sel[:, a], lrow[:, g, c * HC:(c + 1) * HC],
                                 start=True, stop=True).then_inc(sem("s_bcm"), 1)

            for n in range(6):
                rows(n)
            channels(5)
            channels(6)
            for nb in range(4):
                spread(nb)
            channels(7)
            for g in range(4):
                u, t = st.u + 4 + g, st.t + 4 + 2 * g
                pe.wait_ge(s_wlo, u + 1)
                for o in range(2):
                    if g >= 2:
                        pe.wait_ge(s_outD, st.d + 2 * (g - 2) + o + 1)
                    elif g == 0:
                        pe.wait_ge(s_outA, st.a + 3 + o)
                    out = pa[:, 2 * o:2 * o + 2] if g % 2 else pair(t + o)
                    for k in range(2):
                        pe.wait_ge(sem("s_pllo"), 2 * g + k + 1)
                        mm = product(u % 2, out, b_hi, b_lo, 2 * g + k, k == 0, k == 1, m=PW, kp=PW,
                                     wofs=(2 * k + o) * PW)
                    mm.then_inc(s_mm, 1)
            st = enter("mrg1")
            with pe.Fori(0, KT) as n:
                u = st.u + 4 * n
                pe.wait_ge(s_outA, st.a + 2 * n)
                unit8(pe, u, 0, 0, a_hi, a_lo)
                pe.wait_ge(s_outD, st.d + 2 * n)
                unit8(pe, u + 1, 1, 1, att1_hi, att1_lo, nk=2)
                pe.wait_ge(s_outA, st.a + 2 * n + 1)
                unit8(pe, u + 2, 0, 0, a_hi, a_lo)
                pe.wait_ge(s_outD, st.d + 2 * n + 1)
                unit8(pe, u + 3, 1, 1, b_hi, b_lo, kp=PW)

            def out_stage(b):
                st = enter(f"out{b}")
                for m in range(KT):
                    if m >= 2:
                        pe.wait_ge(s_outD, st.d + m - 1)
                    pe.wait_ge(s_wlo, st.u + m + 1)
                    for k in range(KT):
                        if m == 0:
                            pe.wait_ge(sem(f"s_msplit{b}"), k + 1)
                        mm = product(m % 2, pair(m), a_hi, a_lo, k, k == 0, k == KT - 1)
                    mm.then_inc(s_mm, 1)

            out_stage(1)

            def mlp(b):
                st = enter(f"mlp{b}")
                n_norm = 1 if b == 1 else 3
                s_hlo = sem(f"s_hlo{b}")

                def hidden(u, d, first=False):
                    for j in range(4):
                        if not first or j >= 2:
                            pe.wait_ge(s_outD, d + j - 1)
                        pe.wait_ge(s_wlo, u + j + 1)
                        for k in range(KT):
                            if first and j == 0:
                                pe.wait_ge(sem(f"s_blo{b}"), k + 1)
                            mm = product(j % 2, pair(j), b_hi, b_lo, k, k == 0, k == KT - 1)
                        mm.then_inc(s_mm, 1)
                        if first and j == 0:
                            stats(n_norm)
                        if first and j == 1:
                            broadcast(SPREADS[n_norm] - 1)

                def down(u, d, h, slot):
                    pe.wait_ge(s_hlo, h)
                    for j in range(4):
                        pe.wait_ge(s_wlo, u + j + 1)
                        for o in range(2):
                            m = 2 * j + o
                            pe.wait_ge(s_outD, d + m - 1)
                            for k in range(4):
                                mm = product(j % 2, pair(m), a_hi, a_lo, 4 * slot + k, k == 0, k == 3,
                                             wofs=(2 * k + o) * P)
                            mm.then_inc(s_mm, 1)

                hidden(st.u, st.d, True)
                with pe.Fori(0, 3) as i:
                    for e in range(2):
                        hidden(st.u + 4 + 8 * e + 16 * i, st.d + 4 + 12 * e + 24 * i)
                        down(st.u + 8 + 8 * e + 16 * i, st.d + 8 + 12 * e + 24 * i, 4 + 4 * e + 8 * i, e)
                hidden(st.u + 52, st.d + 76)
                down(st.u + 56, st.d + 80, 28, 0)
                down(st.u + 60, st.d + 88, 32, 1)

            mlp(1)
            stats(2)
            broadcast(3)
            broadcast(2, diag_r, 0)
            attention(2)
            st = enter("gat0")
            pe.wait_ge(sem("s_a2lo"), N_PAIR2)
            for j in range(U_GAT0):
                pe.wait_ge(s_wlo, st.u + j + 1)
                for o in range(2):
                    if j:
                        pe.wait_ge(s_outD, st.d + o + 1)
                    for k in range(4):
                        mm = product((st.u + j) % 2, pair(st.t + 2 * j + o), att2_hi, att2_lo, k, k == 0, k == 3,
                                     wofs=(2 * k + o) * P)
                    mm.then_inc(s_mm, 1)
            st = enter("gatt")
            with pe.Fori(0, KT - 4) as n:
                pe.wait_ge(s_outA, st.a + n)
                unit8(pe, st.u + 2 * n, st.u % 2, 0, a_hi, a_lo)
                pe.wait_ge(s_outD, st.d + n)
                pe.wait_ge(sem("s_a2lo"), N_PAIR2)
                unit8(pe, st.u + 2 * n + 1, (st.u + 1) % 2, 1, att2_hi, att2_lo, nk=4)
            st = enter("rec")

            def proj(c_out, u, t):
                if t - st.t >= 2:
                    pe.wait_ge(s_outA, st.a + t - st.t - 1)
                unit8(pe, u, u % 2, t, a_hi, a_lo)

            def gates(c, u, t):
                pe.wait_ge(s_wlo, u + 1)
                pe.wait_ge(sem("s_ul"), c + 1)
                for o in range(4):
                    pe.wait_ge(s_outA, st.a + t + o - st.t - 1)
                    mm = product(u % 2, pair(t + o), uh3, ul3, 0, True, True, wofs=o * P)
                    mm.then_inc(s_mm, 1)

            uh3 = uh[:].unsqueeze(1)
            ul3 = ul[:].unsqueeze(1)
            proj(0, st.u, st.t)
            for c in range(KT):
                proj(c, st.u + 1 + 3 * c, st.t + 1 + 6 * c)
                if c < KT - 1:
                    proj(c + 1, st.u + 2 + 3 * c, st.t + 2 + 6 * c)
                    gates(c, st.u + 3 + 3 * c, st.t + 3 + 6 * c)
                else:
                    gates(c, st.u + 23, st.t + 44)
            st = enter("mrg2")
            with pe.Fori(0, KT // 2) as i:
                for o in range(2):
                    pe.wait_ge(s_outD, st.d + 2 * i + o - 1)
                    unit8(pe, st.u + 4 * i + o, (st.u + o) % 2, o, a_hi, a_lo)
                pe.wait_ge(sem("s_rlo"), KT)
                for o in range(2):
                    pe.wait_ge(s_outA, st.a + 2 * i + o + 1)
                    unit8(pe, st.u + 4 * i + 2 + o, (st.u + o) % 2, o, r_hi, r_lo)
            out_stage(2)
            mlp(2)
            stats(4)
            broadcast(5)


def tiles(w, n, width=P, rows=P):
    k = w.shape[0] // rows
    return w.reshape(k, rows, w.shape[1])[:, :, n * width:(n + 1) * width].transpose(1, 0, 2)


def weight_stream(i):
    out = np.zeros((P, N_UNITS, KT, P), np.float32)
    flat = out.reshape(P, N_UNITS, S)
    u = 0
    w = i["w_in"][0]
    for p in range(N_PAIR1):
        for c in (12, 0, 6):
            out[:, u] = tiles(w, c + p)
            u += 1
    for z in range(8):
        out[:, u, :, 0:PW] = tiles(w[:, 2304:3072], z, PW)
        u += 1
    for g in range(4):
        for k in range(2):
            for o in range(2):
                flat[0:PW, u, (2 * k + o) * PW:(2 * k + o + 1) * PW] = (
                    i["w_pool_grp"][0, g, k * PW:(k + 1) * PW, o * PW:(o + 1) * PW])
        u += 1
    for n in range(KT):
        out[:, u] = tiles(w, 24 + n)
        out[:, u + 1, 0:2] = tiles(i["w_att_out"][0], n)
        out[:, u + 2] = tiles(w, 32 + n)
        out[0:PW, u + 3] = tiles(i["w_pool_out"][0], n, rows=PW)
        u += 4
    u = mlp_units(out, u, i["w_out"][0], i["w_mlp_in"][0], i["w_mlp_out"][0])
    w = i["w_in_2"][0]
    for p in range(N_PAIR2):
        for c in (8, 0, 4):
            out[:, u] = tiles(w, c + p)
            u += 1
    for n in range(EXTRA):
        out[:, u] = tiles(w, 28 + n)
        u += 1
    for j in range(U_GAT0):
        out[:, u] = tiles(i["w_att_o_2"][0], j, 2 * P).reshape(P, KT, P)
        u += 1
    for n in range(EXTRA, KT):
        out[:, u] = tiles(w, 28 + n)
        out[:, u + 1, 0:4] = tiles(i["w_att_o_2"][0], n)
        u += 2
    out[:, u] = tiles(w, 12)
    u += 1
    for c in range(KT):
        out[:, u] = tiles(w, 20 + c)
        u += 1
        if c < KT - 1:
            out[:, u] = tiles(w, 13 + c)
            u += 1
        for d in range(2):
            for g, name in enumerate(("w_rg_a_2", "w_rg_i_2")):
                for h in range(2):
                    r = slice(64 * h, 64 * h + 64)
                    out[r, u, 2 * d + g, r] = i[name][0, d, 2 * c + h]
        u += 1
    for n in range(0, KT, 2):
        for o in range(2):
            out[:, u + o] = tiles(w, 36 + n + o)
            out[:, u + 2 + o] = tiles(i["w_rec_o_2"][0], n + o)
        u += 4
    u = mlp_units(out, u, i["w_out_2"][0], i["w_ff1_2"][0], i["w_ff2_2"][0])
    return flat


def mlp_units(out, u, w_out, w1, w2):
    for n in range(KT):
        out[:, u] = tiles(w_out, n)
        u += 1

    def hidden(g, u):
        for j in range(4):
            out[:, u + j] = tiles(w1, 4 * g + j)
        return u + 4

    def down(g, u):
        for j in range(4):
            out[:, u + j] = tiles(w2[4 * g * P:4 * (g + 1) * P], j, 2 * P).reshape(P, KT, P)
        return u + 4

    u = hidden(0, u)
    for g in range(8):
        if g < 7:
            u = hidden(g + 1, u)
        u = down(g, u)
    return u


def columns(v):
    return v.reshape(-1, P).T


def packed_vectors(i):
    out = np.zeros((P, NVEC), np.float32)

    def put(name, a):
        out[0:a.shape[0], VEC[name]:VEC[name] + a.shape[1]] = a

    for name, key in (("g_mix", "norm_mix_g"), ("g_mlp", "norm_mlp_g"), ("g_ln1", "ln1_g_2"), ("g_ln2", "ln2_g_2"),
                      ("b_in", "b_in_2"), ("conv_b", "conv_b_2")):
        put(name, columns(i[key][0]))
    put("g_fin", columns(i["norm_final_g"]))
    put("g_lnf", columns(i["lnf_g_2"]))
    put("conv_w", columns(i["conv_w_2"][0].reshape(-1)))
    put("lam", columns(i["lru_lambda_2"][0].reshape(-1)))
    put("b_rg", columns(np.stack([i["b_rg_a_2"][0], i["b_rg_i_2"][0]], 1).reshape(-1)))
    put("p_scale", i["pool_scale"][0].reshape(8, PW).T)
    return out


def shape_constants():
    q = np.arange(P)[:, None]
    c = np.zeros((P, 832), np.float32)
    c[:, 0:128] = np.eye(P)
    step = P + q - np.arange(256)[None, :]
    c[:, 128:384] = np.where((step >= 0) & (step <= P), step, BIG)
    k = np.arange(P)[None, :]
    c[:, 384:512] = np.where((q // 64 == k // 64) & (q >= k), q - k, BIG)
    for h in range(4):
        c[h, 512 + 128 * (h // 2) + 64 * (h % 2):512 + 128 * (h // 2) + 64 * (h % 2) + 64] = 1.0
    for g, w in enumerate(WINDOWS):
        c[:, 768 + 16 * g:784 + 16 * g] = 1.0 / np.minimum(np.arange(16) + 1, w)
    return c


def neighbourhood_mask():
    out = np.full((P, 6, 12, 32), NEG, np.float32)
    for o, n in enumerate((0, 1, 3)):
        cs = (0, 8, 24, 32)[n]
        for hf in range(2):
            for r in range(8):
                row = 8 * hf + r
                rs = min(max(row - 4, 0), 8)
                for a in range(16):
                    qc = 16 * n + a
                    ws = min(max(qc - 8, 0), 48)
                    r0, c0 = rs - 4 * hf, ws - cs
                    out[16 * r + a, 2 * o + hf, r0:r0 + 8, max(c0, 0):c0 + 16] = 0.0
    return out.reshape(P, 6, 384)


def relative_bias(rpb):
    h = rpb.shape[0]
    pad = np.zeros((h, 15 + 8, 31 + 32), np.float32)
    pad[:, 4:19, 16:47] = rpb
    out = np.zeros((h // 2, 8, 16, 3, 2, 16, 32), np.float32)
    for r in range(8):
        for a in range(16):
            for o, s in enumerate((0, -8, -16)):
                c0 = s - a + 31
                out[:, r, a, o] = pad[:, 7 - r:23 - r, c0:c0 + 32].reshape(h // 2, 2, 16, 32)
    return out.reshape(h // 2, P, 6, HC)


def kernel(**inputs):
    import concourse.bacc as bacc
    from concourse.bass_utils import run_bass_kernel_spmd

    i = {k: np.ascontiguousarray(v) for k, v in inputs.items()}
    arrays = {
        "xT": np.ascontiguousarray(i["x"][0].T),
        "wstream": weight_stream(i),
        "vecs": packed_vectors(i),
        "consts": shape_constants(),
        "mask2": neighbourhood_mask(),
        "bias2": relative_bias(i["rpb_2"][0]),
    }
    nc = bacc.Bacc("TRN2", target_bir_lowering=False, num_devices=1, dynamic_dma_scratch_size=4096)
    args = [nc.dram_tensor(n, a.shape, F32, kind="ExternalInput").ap() for n, a in arrays.items()]
    args.append(nc.dram_tensor("outT", (D, S), F32, kind="ExternalOutput").ap())
    args.append(nc.dram_tensor("x2", (D, S), F32, kind="Internal").ap())
    build(nc, *args)
    r = run_bass_kernel_spmd(nc, [arrays], core_ids=[0])
    return np.ascontiguousarray(np.asarray(r.results[0]["outT"]).T).reshape(1, S, D)
```

```python
from contextlib import ExitStack

import numpy as np

import concourse.bass as bass
from concourse import mybir

F32 = mybir.dt.float32
FR = mybir.dt.float32r
ALU = mybir.AluOpType
ACT = mybir.ActivationFunctionType
AXX = mybir.AxisListType.X

P = 128
S = 1024
D = 1024
KT = D // P
HC = 512
EPS = 1e-6
KB = 1024

N_PAIR1 = 6
DIL = (1, 4, 16)
SLOPE = [2.0 ** (-8.0 * (h + 1) / 12) for h in range(12)]
PW = 96
WINDOWS = (2, 4, 8, 16)
REC_ORDER = (0, 1, 6, 2, 3, 4, 5, 7)
N_PAIR2 = 4
COL_START = (0, 8, 24, 32)
NEG = -1e30
BIG = 1e30
UNITS_PER_PAIR = 16

VEC = {}
_n = 0
for _name, _w in (("g_mix", 8), ("g_mlp", 8), ("g_fin", 8), ("g_ln1", 8), ("g_ln2", 8), ("g_lnf", 8),
                  ("b_in", 44), ("conv_w", 32), ("conv_b", 8), ("b_rg", 32), ("lam", 16), ("p_scale", 8)):
    VEC[_name] = _n
    _n += _w
NVEC = _n

AHEAD = 4
EXTRA = 4
U_ATT1, U_POOL, U_MRG1, U_OUT, U_MLP = 3 * N_PAIR1 + EXTRA, 8, 32, 8, 64
U_ATT2, U_GAT0, U_GATT, U_REC, U_MRG2 = 3 * N_PAIR2 + EXTRA + 1, 3, 6, 25, 15


SPREADS = (1, 2, 4, 5, 6)


class Stage:

    def __init__(self, u, t, a, d):
        self.u, self.t, self.a, self.d = u, t, a, d


STAGES = {}
_u = _t = _a = _d = 0
for _name, _nu, _na, _nd in (
        ("att1", U_ATT1, U_ATT1, 0), ("pool", U_POOL, 0, 12), ("mrg1", U_MRG1, 0, 32), ("out1", U_OUT, 0, 8),
        ("mlp1", U_MLP, 0, 96), ("att2", U_ATT2, U_ATT2, 0), ("gat0", U_GAT0, 0, 5), ("gatt", U_GATT, 3, 3),
        ("rec", U_REC, 49, 0), ("mrg2", U_MRG2, 7, 8), ("out2", U_OUT, 0, 8), ("mlp2", U_MLP, 0, 96)):
    STAGES[_name] = Stage(_u, _t, _a, _d)
    _u, _t, _a, _d = _u + _nu, _t + _na + _nd, _a + _na, _d + _nd
N_UNITS = _u


def build(nc, xT, wstream, vecs, consts, mask2, bias2, outT, x2):
    ctx = ExitStack()
    with ctx:
        base = (nc.sbuf_base + 31) // 32 * 32
        A0 = base
        B0 = A0 + 64 * KB
        G0 = B0 + 64 * KB
        Z0 = G0 + 32 * KB
        T0 = Z0 + 8 * KB + 64
        W0 = T0 + 16 * KB + 64
        C0 = W0 + 24 * KB

        def at(name, shape, off, dt=F32):
            return nc.alloc_sbuf_tensor_at(name, shape, dt, offset=off)

        a_hi = at("a_hi", [P, KT, S], A0, FR)
        a_lo = at("a_lo", [P, KT, S], A0 + 32 * KB, FR)
        b_hi = at("b_hi", [P, KT, S], B0, FR)
        b_lo = at("b_lo", [P, KT, S], B0 + 32 * KB, FR)
        res = at("res", [P, KT, S], G0)
        zt = at("zt", [P, 2, S], Z0)
        w_raw = at("w_raw", [P, 2, S], W0)
        w_hi = at("w_hi", [P, 2, S], W0 + 8 * KB, FR)
        w_lo = at("w_lo", [P, 2, S], W0 + 16 * KB, FR)
        sq = at("sq", [P, 2, S], T0)
        sqsum = at("sqsum", [P, S], T0 + 8 * KB)
        diag = at("diag", [P, KT, P], T0 + 12 * KB)
        sqsum_g = at("sqsum_g", [P, S], Z0)
        sq_g = at("sq_g", [P, S], Z0 + 4 * KB)
        diag_r = at("diag_r", [P, KT, P], T0)
        og = at("og", [P, N_PAIR1, S], B0)
        qkv1 = at("qkv1", [P, 2, 3, S], B0 + 24 * KB)
        vtok1 = at("vtok1", [P, 2, 8, P], B0 + 48 * KB)
        sm1 = at("sm1", [P, 3, 256], T0)
        pt1 = at("pt1", [P, 2, 256], T0 + 3 * KB)
        mrow = at("mrow", [4, 3, S], B0 + 24 * KB)
        lrow = at("lrow", [4, 3, S], B0 + 36 * KB)
        mmin = at("mmin", [4, S], B0 + 48 * KB)
        den = at("den", [4, S], B0 + 52 * KB)
        mg = at("mg", [P, 2, S], B0 + 56 * KB)
        mgt = at("mgt", [P, 2, HC], B0 + 48 * KB)
        att1_hi = at("att1_hi", [P, 2, S], T0, FR)
        att1_lo = at("att1_lo", [P, 2, S], T0 + 8 * KB, FR)
        PADL = 8
        SP_ = S + PADL
        win = at("win", [P, 2, SP_], Z0)
        att2_hi = at("att2_hi", [P, 4, S], B0, FR)
        att2_lo = at("att2_lo", [P, 4, S], B0 + 16 * KB, FR)
        qk2 = at("qk2", [P, 2, 2, S], B0 + 32 * KB)
        v2 = at("v2", [P, 4, HC], B0 + 48 * KB)
        o2 = at("o2", [P, 2, S], B0 + 56 * KB)
        vtok2 = at("vtok2", [P, 2, 16, P], G0)
        tg01 = at("tg01", [P, 2, S], B0 + 48 * KB)
        tg23 = at("tg23", [P, 2, S], B0 + 32 * KB)
        braw = at("braw", [P, 6, HC], G0 + 16 * KB)
        msk = at("msk", [P, 6, 384], T0)
        bm = at("bm", [P, 4, 384], T0 + 9 * KB + 512)
        sm2 = at("sm2", [P, 3, 384], Z0)
        pt2 = at("pt2", [P, 2, 384], Z0 + 4 * KB + 512)
        rec = at("rec", [P, KT, S], B0)
        R0 = B0 + 32 * KB
        uh = at("uh", [P, S], R0, FR)
        ul = at("ul", [P, S], R0 + 4 * KB, FR)
        th = at("th", [P, 4, S], R0 + 8 * KB)
        uc = at("uc", [P, 2, S], R0 + 24 * KB)
        URW = S + 8
        y_in = at("y_in", [P, 2, S], Z0)
        tm = at("tm", [P, 2, S], T0 + 4 * URW)
        gt = at("gt", [P, S], T0 + 4 * URW + 8 * KB)
        r_hi = at("r_hi", [P, KT, S], R0, FR)
        r_lo = at("r_lo", [P, KT, S], B0, FR)

        off = [C0]

        def const(name, shape):
            n = 4 * int(np.prod(shape[1:]))
            h = at(name, shape, off[0])
            off[0] += (n + 31) // 32 * 32
            return h

        vec = const("vec", [P, NVEC])
        cst = const("cst", [P, 128 + 256 + 128 + 256 + 64])
        ident, dist0, dist2 = cst[:, 0:128], cst[:, 128:384], cst[:, 384:512]
        sel = cst[0:4, 512:768].rearrange("p (a m) -> p a m", a=2)
        invc = cst[:, 768:832].rearrange("p (g t) -> p g t", g=4)
        ones = const("ones", [P, 128])
        mhalf = const("mhalf", [P, 8])
        tick = const("tick", [P, 1])
        warm = const("warm", [P, 1])
        first16 = const("first16", [P, 16])
        gate_b = const("gate_b", [P, 1])
        negm = const("negm", [P, 96])
        lsum = const("lsum", [P, 96])
        rl = const("rl", [P, 96])
        rb_at = off[0]
        rb = const("rb", [P, URW])[:, 0:S]
        ur = (at("ur0", [P, URW], T0), at("ur1", [P, URW], rb_at))
        ms = const("ms", [P, 8])
        msg = const("msg", [P, 8])
        rstd1 = const("rstd1", [P, 8])
        gg = const("gg", [P, 8])
        rstd = const("rstd", [P, 8])
        hb = const("hb", [P, 44 + 32])
        cl = const("cl", [P, 6, 16])
        assert off[0] <= nc.sbuf_usable_end, (off[0], nc.sbuf_usable_end)

        ps = [ctx.enter_context(nc.psum_tensor(f"ps{i}", [P, 2, HC], F32)) for i in range(2)]
        pa = ctx.enter_context(nc.psum_tensor("pa", [P, 4, HC], F32))

        def pair(t):
            return ps[t % 2]

        def pair_flat(t, n=P):
            return ps[t % 2][0:n].rearrange("p c n -> p (c n)")

        def normed(k):
            return (zt[:, 0], zt[:, 1], sq[:, 1], sqsum[:])[k % 4]

        def group_out(g, o):
            out = pa[0:PW, 2 * o:2 * o + 2] if g % 2 else ps[(STAGES["pool"].t + 4 + o) % 2][0:PW]
            return out.rearrange("p c n -> p (c n)")

        sems = {}

        def sem(name):
            if name not in sems:
                sems[name] = ctx.enter_context(nc.semaphore(name))
            return sems[name]

        s_w = [sem("s_w0"), sem("s_w1")]
        s_whi, s_wlo = sem("s_whi"), sem("s_wlo")
        s_mm, s_outA, s_outD = sem("s_mm"), sem("s_outA"), sem("s_outD")

        def V(name, i=0, n=1):
            return vec[:, VEC[name] + i:VEC[name] + i + n]

        block = ctx.enter_context(nc.Block())

        def load_unit(sp, u, slot, first=False):
            if not first:
                sp.wait_ge(s_wlo, u - 1)
            sp.dma_start(w_raw[:, slot:slot + 1], wstream[:, bass.ds(u, 1)]).then_inc(s_w[slot], 16)

        def split_hi(act, u, slot, half_u, t_free):
            act.wait_ge(s_w[slot], 16 * (half_u + 1))
            if t_free is not None:
                act.wait_ge(s_mm, t_free)
            nc.scalar.activation(w_hi[:, slot], w_raw[:, slot], ACT.Copy).then_inc(s_whi, 1)

        def split_lo(dve, u, slot, t_free):
            dve.wait_ge(s_whi, u + 1)
            if t_free is not None:
                dve.wait_ge(s_mm, t_free)
            nc.vector.tensor_tensor(w_lo[:, slot], w_raw[:, slot], w_hi[:, slot].bitcast(F32),
                                    ALU.subtract).then_inc(s_wlo, 1)

        def product(slot, out, xh, xl, k, first, last, kk=None, m=P, wofs=None, kp=P):
            kk = k if kk is None else kk
            wofs = kk * P if wofs is None else wofs
            mm = None
            for n, (w, x) in enumerate(((w_hi, xh), (w_hi, xl), (w_lo, xh))):
                for c in range(2):
                    mm = nc.tensor.matmul(out[0:m, c], w[0:kp, slot, wofs:wofs + m],
                                          x[0:kp, k, c * HC:(c + 1) * HC],
                                          start=first and n == 0, stop=last and n == 2)
            return mm

        def unit8(pe, u, slot, t, xh, xl, m=P, kp=P, nk=KT):
            pe.wait_ge(s_wlo, u + 1)
            mm = None
            for k in range(nk):
                mm = product(slot, pair(t), xh, xl, k, k == 0, k == nk - 1, m=m, kp=kp)
            mm.then_inc(s_mm, 1)

        @block.sync
        def _(sp):
            sp.dma_start(vec[:], vecs).then_inc(sem("s_vec"), 16)
            load_unit(sp, 0, 0, True)
            for k in range(KT):
                sp.dma_start(res[:, k], xT[k * P:(k + 1) * P]).then_inc(sem(f"s_x{k}"), 16)
            sp.dma_start(cst[:], consts).then_inc(sem("s_cst"), 16)
            load_unit(sp, 1, 1, True)

            def units(u0, u1):
                with sp.Fori(u0 // 2, u1 // 2) as i:
                    for slot in range(2):
                        load_unit(sp, 2 * i + slot, slot)

            def out_stage(b, src):
                st = STAGES[f"out{b}"]
                for n in range(KT):
                    if n >= 2:
                        sp.wait_ge(s_outD, st.d + n - 1)
                    else:
                        sp.wait_ge(sem(f"s_msplit{b}"), KT)
                    sp.dma_start(zt[:, n % 2], src[n * P:(n + 1) * P]).then_inc(sem(f"s_xr{b}{n % 2}"), 16)
                    load_unit(sp, st.u + n + 2, n % 2)

            units(2, STAGES["out1"].u + 2)
            out_stage(1, xT)
            units(STAGES["mlp1"].u + 2, STAGES["att2"].u + 4)
            for k in range(KT):
                sp.wait_ge(sem("s_nrm1"), k + 1)
                sp.dma_start(x2[k * P:(k + 1) * P], res[:, k]).then_inc(sem("s_stored"), 16)
            sp.wait_ge(sem("s_nlo"), KT // 2)
            sp.wait_ge(sem("s_nle"), KT // 2)
            sp.dma_start(msk[:], mask2).then_inc(sem("s_msk"), 16)
            units(STAGES["att2"].u + 4, STAGES["out2"].u + 2)
            out_stage(2, x2)
            units(STAGES["mlp2"].u + 2, N_UNITS)
            for k in range(KT):
                sp.wait_ge(sem("s_nrm2"), k + 1)
                sp.dma_start(outT[k * P:(k + 1) * P], res[:, k]).then_inc(sem("s_done"), 16)
            sp.wait_ge(sem("s_done"), 16 * KT)

        def tile_of(idx):
            return idx // 8, idx // 4 % 2, idx // 8 * 4 + idx % 4

        def has_prev(g, i):
            return (g == 0 and i > 0) or (g == 1 and i % 2 == 1)

        def stat(x, b, j):
            p, idx = divmod(j, UNITS_PER_PAIR)
            _, hh, i = tile_of(idx)
            c = 32 * (p // 2) + 4 * i + 2 * (p % 2) + hh if b == 1 else j
            return x[:, c:c + 1]

        def width(b, j):
            p, idx = divmod(j, UNITS_PER_PAIR)
            if b == 2:
                return 384
            return 256 if has_prev(p // 2, tile_of(idx)[2]) else 128

        VB = {1: 2, 2: 4}
        NP_ = {1: N_PAIR1, 2: N_PAIR2}
        V_STEP = 9
        FILL = 9

        def unit_at(b, t):
            for m in range(AHEAD, 3 * NP_[b] + EXTRA):
                if (48 * (m + 1 - AHEAD) - 1) // FILL == t:
                    return m
            return None

        @block.gpsimd
        def _(pool):
            nc.gpsimd.memset(ones[:], 1.0).then_inc(sem("s_pc"), 1)
            nc.gpsimd.memset(mhalf[:], -0.5).then_inc(sem("s_pc"), 1)
            nc.gpsimd.memset(tick[:], 0.0).then_inc(sem("s_gsum"), 1)

            def norm_power(i, out=rstd, mean=ms):
                pool.wait_ge(sem("s_ms"), i + 1)
                nc.gpsimd.tensor_tensor(out[:], mean[:], mhalf[:], ALU.pow).then_inc(sem("s_rstd"), 1)

            def norm_lo():
                for k in range(1, KT, 2):
                    pool.wait_ge(sem("s_nh"), k + 1)
                    nc.gpsimd.tensor_tensor(a_lo[:, k], normed(k), a_hi[:, k].bitcast(F32),
                                            ALU.subtract).then_inc(sem("s_nlo"), 1)

            for k in range(1, KT):
                pool.wait_ge(sem("s_sq"), k + 1)
                if k > 1:
                    pool.wait_ge(sem("s_sqs"), k - 1)
                nc.gpsimd.tensor_tensor(sqsum[:], sqsum[:], sq[:, k % 2], ALU.add).then_inc(sem("s_sqs"), 1)
            pool.wait_ge(sem("s_pc"), 2)
            norm_power(0)
            pool.wait_ge(sem("s_rb"), 1)
            for m in range(3 * N_PAIR1):
                p, which = divmod(m, 3)
                r, dst, dil = rb[:], qkv1[:, p % 2, which], DIL[p // 2]
                if dil > 1:
                    dst = dst.rearrange("p (z l) -> p z l", z=dil)
                    r = r.rearrange("p (l z) -> p z l", z=dil)
                pool.wait_ge(s_outA, STAGES["att1"].a + m + 1)
                nc.gpsimd.tensor_tensor(dst, dst, r, ALU.mult).then_inc(sem("s_scaled"), 1)
            nc.gpsimd.memset(win[:, :, 0:PADL], 0.0).then_inc(sem("s_win"), 1)
            pool.wait_ge(sem("s_win"), 1)
            nwin = 1
            for z in range(8):
                if z < 4:
                    pool.wait_ge(s_outA, STAGES["att1"].a + 3 * N_PAIR1 + z + 1)
                    nc.gpsimd.tensor_tensor(res[0:PW, z], res[0:PW, z], rb[0:PW], ALU.mult).then_inc(sem("s_zr"), 1)
                    pool.wait_ge(sem("s_zr"), z + 1)
                else:
                    pool.wait_ge(s_outD, STAGES["pool"].d + z - 3)
                if z:
                    pool.wait_ge(sem("s_pooled"), z)
                for lv in range(z // 2 + 1):
                    dst, src, shift = win[0:PW, lv % 2], win[0:PW, 1 - lv % 2], 1 << lv
                    if lv == 0:
                        nc.gpsimd.tensor_tensor(dst[:, PADL + 1:], res[0:PW, z, 1:], res[0:PW, z, 0:S - 1], ALU.add
                                                ).then_inc(sem("s_win"), 1)
                        ins = nc.gpsimd.tensor_tensor(dst[:, PADL:PADL + 1], res[0:PW, z, 0:1],
                                                      dst[:, PADL - 1:PADL], ALU.add)
                        nwin += 1
                    else:
                        ins = nc.gpsimd.tensor_tensor(dst[:, PADL:], src[:, PADL:], src[:, PADL - shift:SP_ - shift],
                                                      ALU.add)
                    nwin += 1
                    if lv < z // 2:
                        ins.then_inc(sem("s_win"), 1)
                        pool.wait_ge(sem("s_win"), nwin)
                    else:
                        nwin -= 1
                        ins.then_inc(sem("s_wsum"), 1)
            st = STAGES["mrg1"]
            with pool.Fori(0, KT) as n:
                pool.wait_ge(s_outD, st.d + 4 * n + 4)
                nc.gpsimd.tensor_tensor(res[:, bass.ds(n, 1)], zt[:, 0:1], zt[:, 1:2], ALU.add
                                        ).then_inc(sem("s_gsum"), 1)
            norm_power(1)
            norm_power(2, rstd, msg)
            norm_power(3, rstd1, ms)
            norm_lo()
            pool.wait_ge(sem("s_msk"), 16)
            for j in range(N_PAIR2 * UNITS_PER_PAIR):
                p, idx = divmod(j, UNITS_PER_PAIR)
                hf, hh, i = tile_of(idx)
                o = (0, 1, 1, 2)[i % 4]
                if idx == 0:
                    pool.wait_ge(sem("s_braw"), 16 * (p + 1))
                if j >= 4:
                    pool.wait_ge(sem("s_add2"), j - 3)
                w0 = 0 if hf else 128
                nc.gpsimd.tensor_tensor(bm[:, j % 4], braw[:, 2 * o + hh, w0:w0 + 384], msk[:, 2 * o + hf],
                                        ALU.add).then_inc(sem("s_bm"), 1)
            def u_lo(c):
                pool.wait_ge(sem("s_uh"), c + 1)
                if c:
                    pool.wait_ge(s_mm, STAGES["rec"].t + 6 * c + 1)
                nc.gpsimd.tensor_tensor(ul[:], uc[:, c % 2], uh[:].bitcast(F32), ALU.subtract).then_inc(sem("s_ul"), 1)

            u_lo(0)
            for c in range(KT):
                pool.wait_ge(sem("s_gpoly"), c + 1)
                nc.gpsimd.tensor_tensor(gt[:], gt[:], y_in[:, c % 2], ALU.mult).then_inc(sem("s_gin"), 1)
                if c < KT - 1:
                    u_lo(c + 1)
                pool.wait_ge(sem("s_scan"), 2 * c + 2)
                nc.gpsimd.tensor_tensor(tm[:, 0], tm[:, 0], tm[:, 1], ALU.add).then_inc(sem("s_dirs"), 1)
            norm_power(4)
            norm_power(5)

        @block.scalar
        def _(act):
            def square(n, k):
                if k == 0:
                    if n:
                        act.wait_ge(sem("s_stat"), n)
                elif k >= 3:
                    act.wait_ge(sem("s_sqs"), 7 * n + k - 2)
                nc.scalar.activation(sqsum[:] if k == 0 else sq[:, k % 2], res[:, k], ACT.Square
                                     ).then_inc(sem("s_sq"), 1)

            def copy_rb(n):
                act.wait_ge(sem("s_bc"), SPREADS[n])
                nc.scalar.activation(rb[:], pa[:, 2:4].rearrange("p c n -> p (c n)"), ACT.Copy
                                     ).then_inc(sem("s_rb"), 1)

            def norm_hi():
                for k in range(KT):
                    act.wait_ge(sem("s_nd"), k + 1)
                    nc.scalar.activation(a_hi[:, k], normed(k), ACT.Copy).then_inc(sem("s_nh"), 1)

            def attention(b):
                st = STAGES[f"att{b}"]
                vtok = vtok1 if b == 1 else vtok2
                sm, pt = (sm1, pt1) if b == 1 else (sm2, pt2)
                s_S, s_max, s_exp, s_T, s_pt, s_pv, s_oev, s_vt, s_vev = [sem(f"s_{x}{b}") for x in (
                    "S", "max", "exp", "T", "pt", "pv", "oev", "vt", "vev")]
                npair = NP_[b]
                nt = npair * UNITS_PER_PAIR

                def unit_out(m):
                    p, which = divmod(m, 3)
                    u = st.u + m
                    t = st.t + m
                    split_hi(act, u + 2, u % 2, (u + 2) // 2, t + 1)
                    act.wait_ge(s_mm, t + 1)
                    if m >= 3 * npair:
                        e = m - 3 * npair
                        if b == 1:
                            nc.scalar.activation(res[0:PW, e], pair_flat(t, PW), ACT.Copy).then_inc(s_outA, 1)
                            return
                        if e == EXTRA:
                            act.wait_ge(s_pv, nt)
                            nc.scalar.activation(zt[:, 0], pair_flat(t), ACT.Tanh, scale=0.5,
                                                 bias=hb[:, 4 + e:5 + e]).then_inc(s_outA, 1)
                            return
                        if e == 0:
                            act.wait_ge(s_vt, VB[b] * npair)
                        if e == 2:
                            act.wait_ge(s_S, UNITS_PER_PAIR * (npair - 1))
                        nc.scalar.activation((tg01 if e < 2 else tg23)[:, e % 2], pair_flat(t), ACT.Tanh, scale=0.5,
                                             bias=hb[:, 4 + e:5 + e]).then_inc(s_outA, 1)
                        return
                    if which == 0 and p >= 1:
                        act.wait_ge(s_vt, VB[b] * p)
                    if which and p >= 2:
                        act.wait_ge(s_S, UNITS_PER_PAIR * (p - 1))
                    src = pair_flat(t)
                    if b == 1:
                        dst, dil = qkv1[:, p % 2, which], DIL[p // 2]
                        if dil > 1:
                            dst = dst.rearrange("p (z l) -> p z l", z=dil)
                            src = src.rearrange("p (l z) -> p z l", z=dil)
                        nc.scalar.activation(dst, src, ACT.Copy, scale=0.125 if which == 1 else 1.0).then_inc(s_outA, 1)
                        if m == 1:
                            copy_rb(0)
                        return
                    if which == 0:
                        src = src.rearrange("p (r c) -> p r c", c=64)
                        for n, c0 in enumerate(COL_START):
                            last = nc.scalar.activation(v2[:, n].rearrange("p (r c) -> p r c", c=32),
                                                        src[:, :, c0:c0 + 32], ACT.Identity, bias=V("b_in", 8 + p))
                        last.then_inc(s_outA, 1)
                        return
                    dst = qk2[:, p % 2, which - 1]
                    kw = {"bias": V("b_in", 4 + p)}
                    if which == 1:
                        dst = dst.rearrange("p (n r a) -> p n r a", n=4, a=16)
                        src = src.rearrange("p (r n a) -> p n r a", n=4, a=16)
                        kw = {"bias": q8[p], "scale": 0.125}
                    nc.scalar.activation(dst, src, ACT.Identity, **kw).then_inc(s_outA, 1)

                q8 = [hb[:, p:p + 1] for p in range(4)]

                def v_out(n):
                    p, bt = divmod(n, VB[b])
                    act.wait_ge(s_vt, n + 1)
                    if p >= 2:
                        act.wait_ge(s_pv, UNITS_PER_PAIR * (p - 1))
                    nc.scalar.activation(vtok[:, p % 2, 4 * bt:4 * bt + 4].rearrange("p a c -> p (a c)"),
                                         pa[:, 2], ACT.Copy).then_inc(s_vev, 1)

                def exp(j):
                    w = width(b, j)
                    act.wait_ge(s_max, j + 1)
                    nc.scalar.activation(sm[:, j % 3, 0:w], sm[:, j % 3, 0:w], ACT.Exp, bias=stat(negm, b, j),
                                         accum_out=stat(lsum, b, j)).then_inc(s_exp, 1)

                def probs_out(j):
                    w = width(b, j)
                    act.wait_ge(s_T, j + 1)
                    if j >= 2:
                        act.wait_ge(s_pv, j - 1)
                    nc.scalar.activation(pt[:, j % 2, 0:w], pa[:, 2, 0:w], ACT.Copy).then_inc(s_pt, 1)

                def o_out(c):
                    p, q = divmod(c, 4)
                    chunk, hh = divmod(q, 2)
                    act.wait_ge(s_pv, 4 * (c + 1))
                    rows = slice(64 * hh, 64 * hh + 64)
                    src = pa[rows, 3]
                    if b == 1:
                        dil = DIL[p // 2]
                        dst = og[rows, p]
                        if dil > 1:
                            zc = dil // 2
                            dst = dst.rearrange("p (l z) -> p z l", z=dil)[:, zc * chunk:zc * chunk + zc]
                            src = src.rearrange("p (z l) -> p z l", z=zc)
                        else:
                            dst = dst[:, chunk * HC:(chunk + 1) * HC]
                        nc.scalar.activation(dst, src, ACT.Copy).then_inc(s_oev, 1)
                        return
                    if p >= 2:
                        act.wait_ge(sem("s_a2lo"), p - 1)
                    dst = o2[rows, p % 2, chunk * HC:(chunk + 1) * HC].rearrange("p (r n a) -> p n r a", n=4, a=16)
                    nc.scalar.activation(dst, src.rearrange("p (n r a) -> p n r a", n=4, a=16), ACT.Copy
                                         ).then_inc(s_oev, 1)

                def load_bias(p):
                    if p:
                        act.wait_ge(sem("s_bm"), UNITS_PER_PAIR * p)
                    act.dma_start(braw[:], bias2[p]).then_inc(sem("s_braw"), 16)

                for m in range(3):
                    unit_out(m)
                    if b == 2 and m == 1:
                        act.wait_ge(sem("s_stored"), 16 * KT)
                        load_bias(0)
                for n in range(VB[b]):
                    v_out(n)
                unit_out(3)
                nt = npair * UNITS_PER_PAIR
                for t in range(nt + 2):
                    p, idx = divmod(t, UNITS_PER_PAIR)
                    if p + 1 < npair and V_STEP <= idx < V_STEP + VB[b]:
                        v_out(VB[b] * (p + 1) + idx - V_STEP)
                    if t < nt:
                        exp(t)
                    if 1 <= t <= nt:
                        probs_out(t - 1)
                    if t >= 6 and (t - 6) % 4 == 0:
                        o_out((t - 6) // 4)
                    if b == 2 and p + 1 < npair and idx == 13:
                        load_bias(p + 1)
                    if unit_at(b, t) is not None:
                        unit_out(unit_at(b, t))
                    if b == 2 and t >= 18 and (t - 18) % 16 == 0:
                        a2_hi((t - 18) // 16)
                o_out(nt // 4 - 1)
                if b == 2:
                    a2_hi(npair - 1)
                    unit_out(3 * npair + EXTRA)

            def a2_hi(p):
                act.wait_ge(sem("s_oev2"), 4 * (p + 1))
                nc.scalar.activation(att2_hi[:, p], o2[:, p % 2], ACT.Copy).then_inc(sem("s_a2hi"), 1)

            act.wait_ge(sem("s_vec"), 16)
            nc.scalar.activation(hb[:, 0:4], V("b_in", 0, 4), ACT.Copy, scale=0.125).then_inc(sem("s_hb"), 1)
            nc.scalar.activation(hb[:, 4:20], V("b_in", 28, 16), ACT.Copy, scale=0.5).then_inc(sem("s_hb"), 1)
            nc.scalar.activation(hb[:, 44:76], V("b_rg", 0, 32), ACT.Copy, scale=0.5).then_inc(sem("s_hb"), 1)
            act.wait_ge(sem("s_hb"), 3)
            nc.scalar.activation(cl[:, 0], V("lam", 0, 16), ACT.Abs).then_inc(sem("s_cl"), 1)
            act.wait_ge(sem("s_cl"), 1)
            nc.scalar.activation(cl[:, 1], cl[:, 0], ACT.Exp, scale=-1.0).then_inc(sem("s_cl"), 1)
            for k in range(KT):
                act.wait_ge(sem(f"s_x{k}"), 16)
                nc.scalar.activation(a_hi[:, k], res[:, k], ACT.Copy, scale=V("g_mix", k)).then_inc(sem("s_xh"), 1)
                if k == 0:
                    split_hi(act, 0, 0, 0, None)
                square(0, k)
            split_hi(act, 1, 1, 0, None)
            attention(1)
            st = STAGES["pool"]

            def row_out(n):
                st_, g = divmod(n, 3)
                act.wait_ge(sem("s_row"), n + 1)
                src = pa[0:4, 2 * (n % 2):2 * (n % 2) + 2].rearrange("p c n -> p (c n)")
                dst = (mrow if st_ == 0 else lrow)[:, g]
                dil = DIL[g]
                if dil > 1:
                    dst = dst.rearrange("p (l z) -> p z l", z=dil)
                    src = src.rearrange("p (z l) -> p z l", z=dil)
                nc.scalar.activation(dst, src, ACT.Copy).then_inc(sem("s_rowc"), 1)

            def z_out(z):
                u, t = st.u + z - 4, st.t + z - 4
                split_hi(act, u + 2, u % 2, (u + 2) // 2, t + 1)

            def pool_hi(z):
                act.wait_ge(sem("s_pooled"), z + 1)
                nc.scalar.activation(b_hi[0:PW, z], res[0:PW, z], ACT.Copy).then_inc(sem("s_plhi"), 1)

            def mixed_hi(g):
                t = st.t + 4 + 2 * g
                split_hi(act, st.u + 6 + g, (st.u + g) % 2, (st.u + 6 + g) // 2, t + 2)
                act.wait_ge(s_mm, t + 2)
                for o in range(2):
                    nc.scalar.activation(b_hi[0:PW, 2 * g + o], group_out(g, o), ACT.Copy,
                                         scale=vec[0:PW, VEC["p_scale"] + 2 * g + o:VEC["p_scale"] + 2 * g + o + 1]
                                         ).then_inc(sem("s_pmhi"), 1)

            z_out(4)
            for n in range(6):
                row_out(n)
            act.wait_ge(sem("s_rowd"), 3)
            nc.scalar.activation(mrow[:], mrow[:], ACT.Exp, scale=-1.0).then_inc(sem("s_rowe"), 1)
            z_out(5)
            z_out(6)
            z_out(7)
            for a in range(2):
                act.wait_ge(sem("s_mgd"), 2 * (a + 1))
                nc.scalar.activation(att1_hi[:, a], mg[:, a], ACT.Copy).then_inc(sem("s_a1hi"), 1)
            act.wait_ge(sem("s_bcu"), 12)
            for z in range(8):
                pool_hi(z)
                if z in (3, 6):
                    mixed_hi(z // 3 - 1)
            mixed_hi(2)
            mixed_hi(3)

            st = STAGES["mrg1"]
            with act.Fori(0, KT) as n:
                for o in range(4):
                    u = st.u + 4 * n + o
                    split_hi(act, u + 2, (st.u + o) % 2, (st.u + o + 2) // 2 + 2 * n, st.t + 4 * n + o + 1)
                    if o % 2 == 0:
                        act.wait_ge(s_outD, st.d + 4 * n + o + 1)
                        nc.scalar.activation(zt[:, o // 2], zt[:, o // 2], ACT.Tanh, scale=0.5
                                             ).then_inc(sem("s_tanh"), 1)

            def out_stage(b):
                st = STAGES[f"out{b}"]
                n = 1 if b == 1 else 3
                act.wait_ge(s_mm, st.t)
                for k in range(KT):
                    if b == 1:
                        act.wait_ge(sem("s_gsum"), k + 2)
                    else:
                        act.wait_ge(s_outD, STAGES["mrg2"].d + k + 1)
                    nc.scalar.activation(a_hi[:, k], res[:, k], ACT.Copy, scale=0.5).then_inc(sem(f"s_mhi{b}"), 1)
                for m in range(KT):
                    split_hi(act, st.u + m + 2, m % 2, (st.u + m + 2) // 2, st.t + m + 1)
                    act.wait_ge(s_outD, st.d + m + 1)
                    nc.scalar.activation(b_hi[:, m], res[:, m], ACT.Copy, scale=V("g_mlp" if b == 1 else "g_ln2", m)
                                         ).then_inc(sem(f"s_bhi{b}"), 1)
                    square(n, m)

            out_stage(1)

            def mlp(b):
                st = STAGES[f"mlp{b}"]
                s_sqr, s_hhi = sem(f"s_sqr{b}"), sem(f"s_hhi{b}")

                def hidden(u, t, d, h0, slot):
                    for j in range(4):
                        act.wait_ge(s_w[j % 2], 8 * (u + j + 2 - j % 2) + 16)
                        act.wait_ge(s_mm, t + j + 1)
                        nc.scalar.activation(w_hi[:, j % 2], w_raw[:, j % 2], ACT.Copy).then_inc(s_whi, 1)
                        act.wait_ge(s_outD, d + j + 1)
                        nc.scalar.activation(zt[:, j % 2], zt[:, j % 2], ACT.Square).then_inc(s_sqr, 1)
                        act.wait_ge(s_sqr, h0 + j + 1)
                        nc.scalar.activation(a_hi[:, 4 * slot + j], zt[:, j % 2], ACT.Copy).then_inc(s_hhi, 1)

                def down(u, t):
                    for j in range(4):
                        act.wait_ge(s_w[j % 2], 8 * (u + j + 2 - j % 2) + 16)
                        act.wait_ge(s_mm, t + 2 * j + 2)
                        nc.scalar.activation(w_hi[:, j % 2], w_raw[:, j % 2], ACT.Copy).then_inc(s_whi, 1)

                copy_rb(1 if b == 1 else 3)
                hidden(st.u, st.t, st.d, 0, 0)
                with act.Fori(0, 3) as i:
                    for e in range(2):
                        hidden(st.u + 4 + 8 * e + 16 * i, st.t + 4 + 12 * e + 24 * i, st.d + 4 + 12 * e + 24 * i,
                               4 + 4 * e + 8 * i, 1 - e)
                        down(st.u + 8 + 8 * e + 16 * i, st.t + 8 + 12 * e + 24 * i)
                hidden(st.u + 52, st.t + 76, st.d + 76, 28, 1)
                down(st.u + 56, st.t + 80)
                n = 2 if b == 1 else 4
                for j in range(4):
                    u = st.u + 60 + j
                    if u + 2 < N_UNITS:
                        act.wait_ge(s_w[j % 2], 8 * (u + 2 - j % 2) + 16)
                        act.wait_ge(s_mm, st.t + 88 + 2 * j + 2)
                        nc.scalar.activation(w_hi[:, j % 2], w_raw[:, j % 2], ACT.Copy).then_inc(s_whi, 1)
                    for o in range(2):
                        m = 2 * j + o
                        act.wait_ge(s_outD, st.d + 88 + m + 1)
                        square(n, m)
                        if b == 1:
                            if m >= 2:
                                act.wait_ge(sem("s_sqgs"), m - 1)
                            nc.scalar.activation(sqsum_g[:] if m == 0 else sq_g[:], res[:, m], ACT.Square,
                                                 scale=V("g_fin", m)).then_inc(sem("s_sqg"), 1)

            mlp(1)
            norm_hi()
            attention(2)
            st = STAGES["gat0"]
            for j, t1 in enumerate((2, 4, 5)):
                split_hi(act, st.u + j + 2, (st.u + j) % 2, (st.u + j + 2) // 2, st.t + t1)
            st = STAGES["gatt"]
            with act.Fori(0, KT - 5) as n:
                for o in range(2):
                    t1 = st.t + 2 * n + o + 1
                    split_hi(act, st.u + 2 * n + o + 2, (st.u + o) % 2, (st.u + o + 2) // 2 + n, t1)
                    if o == 0:
                        act.wait_ge(s_outA, st.a + n)
                        act.wait_ge(s_outD, st.d + n)
                        nc.scalar.activation(gate_b[:], hb[:, bass.ds(9 + n, 1)], ACT.Copy).then_inc(sem("s_gb1"), 1)
                        act.wait_ge(sem("s_gb1"), n + 1)
                        act.wait_ge(s_mm, t1)
                        nc.scalar.activation(zt[:, 0], pair_flat(st.t), ACT.Tanh, scale=0.5, bias=gate_b[:]
                                             ).then_inc(s_outA, 1)

            st = STAGES["rec"]
            s_thr = sem("s_thr")

            def u_out(c, u, t):
                act.wait_ge(s_mm, t + 1)
                act.wait_ge(sem("s_urpad"), 2)
                if c >= 2:
                    act.wait_ge(sem("s_conv"), c - 1)
                nc.scalar.activation(ur[c % 2][:, 2:2 + S], pair_flat(t), ACT.Identity, bias=V("b_in", 12 + c)
                                     ).then_inc(s_outA, 1)
                split_hi(act, u + 2, u % 2, (u + 2) // 2, t + 1)

            def y_out(c, u, t):
                split_hi(act, u + 2, u % 2, (u + 2) // 2, t + 1)
                act.wait_ge(s_mm, t + 1)
                if c >= 2:
                    act.wait_ge(sem("s_rec"), c - 1)
                nc.scalar.activation(y_in[:, c % 2], pair_flat(t), ACT.Identity, bias=V("b_in", 20 + c)
                                     ).then_inc(s_outA, 1)

            def u_split(c):
                act.wait_ge(sem("s_conv"), c + 1)
                if c:
                    act.wait_ge(s_mm, gate_t(c - 1) + 4)
                nc.scalar.activation(uh[:], uc[:, c % 2], ACT.Copy).then_inc(sem("s_uh"), 1)

            def gate_t(c):
                return st.t + 3 + 6 * c

            def gate_out(c, u):
                t = gate_t(c)
                for o in range(4):
                    act.wait_ge(s_mm, t + o + 1)
                    if c and o == 0:
                        act.wait_ge(sem("s_scan"), 2 * c)
                    nc.scalar.activation(th[:, o], pair_flat(t + o), ACT.Tanh, scale=0.5,
                                         bias=hb[:, 44 + 8 * o + c:45 + 8 * o + c]).then_inc(s_outA, 1)
                split_hi(act, u + 2, u % 2, (u + 2) // 2, t + 4)
                if c:
                    act.wait_ge(sem("s_rec"), c)
                nc.scalar.activation(gt[:], y_in[:, c % 2], ACT.Square).then_inc(sem("s_gsq"), 1)
                for d in range(2):
                    act.wait_ge(s_outA, st.a + (t - st.t) + 2 * d + 1)
                    nc.scalar.activation(tm[:, d], th[:, 2 * d], ACT.Tanh, scale=cl[:, 4, 8 * d + c:8 * d + c + 1],
                                         bias=cl[:, 4, 8 * d + c:8 * d + c + 1]).then_inc(s_thr, 1)
                    act.wait_ge(s_thr, 3 * c + d + 1)
                    nc.scalar.activation(th[:, 2 * d], th[:, 2 * d], ACT.Exp, scale=cl[:, 5, 8 * d + c:8 * d + c + 1],
                                         bias=cl[:, 5, 8 * d + c:8 * d + c + 1]).then_inc(sem("s_dec"), 1)
                act.wait_ge(sem("s_gin"), c + 1)
                nc.scalar.activation(gt[:], gt[:], ACT.Tanh, scale=0.7978845608028654).then_inc(s_thr, 1)
                for d in range(2):
                    act.wait_ge(sem("s_neg"), 2 * c + d + 1)
                    nc.scalar.activation(tm[:, d], tm[:, d], ACT.Sqrt).then_inc(sem("s_root"), 1)
                if c:
                    act.wait_ge(sem("s_warm"), c)
                nc.scalar.activation(warm[:], ones[:, 0:1], ACT.Tanh).then_inc(sem("s_warm"), 1)

            act.wait_ge(sem("s_cldone"), 1)
            u_out(0, st.u, st.t)
            for c in range(KT):
                y_out(c, st.u + 1 + 3 * c, st.t + 1 + 6 * c)
                u_split(c)
                if c < KT - 1:
                    u_out(c + 1, st.u + 2 + 3 * c, st.t + 2 + 6 * c)
                else:
                    split_hi(act, st.u + 25, (st.u + 23) % 2, (st.u + 25) // 2, st.t + 45)
                    act.wait_ge(sem("s_gelu"), KT - 1)
                    nc.scalar.activation(zt[:, 0], pair_flat(st.t + 44), ACT.Tanh, scale=0.5, bias=hb[:, 12:13]
                                         ).then_inc(s_outA, 1)
                gate_out(c, st.u + 3 + 3 * c)
            act.wait_ge(s_mm, gate_t(KT - 1) + 4)
            st = STAGES["mrg2"]

            def rec_hi(n, k):
                act.wait_ge(sem("s_rec"), KT if n >= 3 else KT - 1)
                nc.scalar.activation(r_hi[:, k], rec[:, k], ACT.Copy).then_inc(sem("s_rhi"), 1)

            for n in range(3):
                rec_hi(n, REC_ORDER[n])
            split_hi(act, st.u + 2, st.u % 2, (st.u + 2) // 2, st.t + 1)
            act.wait_ge(sem("s_gelu"), KT)
            nc.scalar.activation(zt[:, 1], pair_flat(st.t), ACT.Tanh, scale=0.5, bias=hb[:, 13:14]).then_inc(s_outA, 1)
            for n in range(3, KT):
                rec_hi(n, REC_ORDER[n])
            with act.Fori(0, KT // 2 - 1) as i:
                for o in range(4):
                    split_hi(act, st.u + 4 * i + o + 3, (st.u + o + 1) % 2, (st.u + o + 3) // 2 + 2 * i,
                             st.t + 4 * i + o + 2)
                    if o >= 2:
                        n = 2 * i + o
                        act.wait_ge(s_outA, st.a + n - 1)
                        nc.scalar.activation(gate_b[:], hb[:, bass.ds(12 + n, 1)], ACT.Copy).then_inc(sem("s_gb2"), 1)
                        act.wait_ge(sem("s_gb2"), n - 1)
                        act.wait_ge(s_outD, st.d + n - 1)
                        nc.scalar.activation(zt[:, o - 2], pair_flat(st.t + o - 1), ACT.Tanh, scale=0.5,
                                             bias=gate_b[:]).then_inc(s_outA, 1)
            for o in range(2):
                split_hi(act, st.u + 15 + o, (st.u + 13 + o) % 2, (st.u + 15 + o) // 2, st.t + 14 + o)
            out_stage(2)
            mlp(2)

        @block.vector
        def _(dve):
            def add_square(n, k):
                if k == 0:
                    return
                dve.wait_ge(sem("s_sq"), KT * n + k + 1)
                if k > 1:
                    dve.wait_ge(sem("s_sqs"), 7 * n + k - 1)
                nc.vector.tensor_tensor(sqsum[:], sqsum[:], sq[:, k % 2], ALU.add).then_inc(sem("s_sqs"), 1)

            def spread_diag(out, r):
                nc.vector.tensor_tensor(out[:], ident.unsqueeze(1).broadcast_to([P, KT, P]),
                                        r[:].unsqueeze(2).broadcast_to([P, KT, P]), ALU.mult
                                        ).then_inc(sem("s_diag"), 1)

            def rms(n):
                i = SPREADS[n] - 1
                dve.wait_ge(sem("s_stat"), n + 1)
                nc.vector.tensor_scalar(ms[:], pa[:, 0, 0:8], 1.0 / D, EPS, ALU.mult, ALU.add).then_inc(sem("s_ms"), 1)
                dve.wait_ge(sem("s_rstd"), i + 1)
                spread_diag(diag, rstd)

            def scale_tiles(n, gain, inplace=None):
                dve.wait_ge(sem("s_bc"), SPREADS[n] - (n == 2))
                bc = pa[:, 2:4].rearrange("p c n -> p (c n)")
                def lo(k):
                    dve.wait_ge(sem("s_nh"), k + 1)
                    nc.vector.tensor_tensor(a_lo[:, k], normed(k), a_hi[:, k].bitcast(F32),
                                            ALU.subtract).then_inc(sem("s_nle"), 1)

                for k in range(KT):
                    if inplace is None and k >= 4:
                        dve.wait_ge(sem("s_nlo" if k % 2 else "s_nle"), (k - 4) // 2 + 1)
                    dst = normed(k) if inplace is None else res[:, k]
                    nc.vector.scalar_tensor_tensor(out=dst, in0=res[:, k], scalar=gain[:, k:k + 1], in1=bc,
                                                   op0=ALU.mult, op1=ALU.mult
                                                   ).then_inc(sem("s_nd") if inplace is None else sem(inplace), 1)
                    if inplace is None and k % 2:
                        lo(k - 1)

            def two_norms():
                dve.wait_ge(sem("s_stat"), 3)
                link(nc.vector.tensor_scalar(ms[:], pa[:, 0, 0:8], 1.0 / D, EPS, ALU.mult, ALU.add))
                dve.wait_ge(sem("s_statg"), 1)
                link(nc.vector.tensor_scalar(msg[:], pa[:, 1, 0:8], 1.0 / D, None, ALU.mult))
                nc.vector.scalar_tensor_tensor(out=msg[:], in0=ms[:], scalar=EPS, in1=msg[:],
                                               op0=ALU.mult, op1=ALU.add).then_inc(sem("s_ms"), 2)
                dve.wait_ge(sem("s_rstd"), 3)
                spread_diag(diag, rstd)
                dve.wait_ge(sem("s_rstd"), 4)
                spread_diag(diag_r, rstd1)
                scale_tiles(2, gg)
                dve.wait_ge(sem("s_bc"), SPREADS[2])
                bc = pa[:, 0:2].rearrange("p c n -> p (c n)")
                for k in range(KT):
                    nc.vector.scalar_tensor_tensor(out=res[:, k], in0=res[:, k], scalar=V("g_fin", k), in1=bc,
                                                   op0=ALU.mult, op1=ALU.mult).then_inc(sem("s_nrm1"), 1)

            def pooled(z):
                dve.wait_ge(sem("s_wsum"), z + 1)
                g = z // 2
                src, zz = win[0:PW, g % 2], res[0:PW, z]
                link(nc.vector.tensor_tensor(first16[0:PW], src[:, PADL:PADL + 16], invc[0:PW, g], ALU.mult))
                link(nc.vector.tensor_tensor(zz[:, 0:16], first16[0:PW], zz[:, 0:16], ALU.subtract))
                nc.vector.scalar_tensor_tensor(out=zz[:, 16:], in0=src[:, PADL + 16:], scalar=1.0 / WINDOWS[g],
                                               in1=zz[:, 16:], op0=ALU.mult, op1=ALU.subtract
                                               ).then_inc(sem("s_pooled"), 1)

            POOL_STEPS = {t: unit_at(1, t) - 3 * N_PAIR1 for t in range(N_PAIR1 * UNITS_PER_PAIR)
                          if (unit_at(1, t) or 0) >= 3 * N_PAIR1}

            def attention(b):
                st = STAGES[f"att{b}"]
                sm = sm1 if b == 1 else sm2
                s_S, s_add, s_max, s_exp, s_rl, s_pn, s_T, s_oev = [sem(f"s_{x}{b}") for x in (
                    "S", "add", "max", "exp", "rl", "pn", "T", "oev")]
                npair = NP_[b]
                nt = npair * UNITS_PER_PAIR

                def add_max(j):
                    p, idx = divmod(j, UNITS_PER_PAIR)
                    _, hh, i = tile_of(idx)
                    w = width(b, j)
                    dve.wait_ge(s_S, j + 1)
                    if j >= 3:
                        dve.wait_ge(s_T, j - 2)
                    sc = pa[:, j % 2, 0:w]
                    if b == 1:
                        g = p // 2
                        dist = dist2 if g == 2 else dist0[:, 256 - w:256]
                        nc.vector.scalar_tensor_tensor(out=sm[:, j % 3, 0:w], in0=dist,
                                                       scalar=-SLOPE[2 * p + hh] * DIL[g], in1=sc,
                                                       op0=ALU.mult, op1=ALU.add).then_inc(s_add, 1)
                    else:
                        dve.wait_ge(sem("s_bm"), j + 1)
                        nc.vector.tensor_tensor(sm[:, j % 3, 0:w], bm[:, j % 4], sc, ALU.add).then_inc(s_add, 1)
                    dve.wait_ge(s_add, j + 1)
                    nc.vector.tensor_reduce(stat(negm, b, j), sm[:, j % 3, 0:w], axis=AXX, op=ALU.max,
                                            negate=True).then_inc(s_max, 1)

                def normalise(j):
                    w = width(b, j)
                    dve.wait_ge(s_exp, j + 1)
                    nc.vector.reciprocal(rl[:, j:j + 1], stat(lsum, b, j)).then_inc(s_rl, 1)
                    dve.wait_ge(s_rl, j + 1)
                    nc.vector.tensor_scalar(sm[:, j % 3, 0:w], sm[:, j % 3, 0:w], rl[:, j:j + 1], None,
                                            ALU.mult).then_inc(s_pn, 1)

                def weights(m):
                    split_lo(dve, st.u + m + 2, (st.u + m) % 2, st.t + m + 1)

                for m in range(AHEAD):
                    weights(m)
                    if b == 1 and m == 0:
                        rms(0)
                        softplus()
                for t in range(nt + 1):
                    p, idx = divmod(t, UNITS_PER_PAIR)
                    if t < nt:
                        add_max(t)
                    if t >= 1:
                        normalise(t - 1)
                    if unit_at(b, t) is not None:
                        weights(unit_at(b, t))
                    if b == 1 and t - 6 in POOL_STEPS:
                        pooled(POOL_STEPS[t - 6])
                    if b == 2 and t >= 19 and (t - 19) % 16 == 0:
                        a2_lo((t - 19) // 16)
                if b == 2:
                    weights(3 * npair + EXTRA)
                    a2_lo(npair - 1)

            def a2_lo(p):
                dve.wait_ge(sem("s_a2hi"), p + 1)
                nc.vector.tensor_tensor(att2_lo[:, p], o2[:, p % 2], att2_hi[:, p].bitcast(F32),
                                        ALU.subtract).then_inc(sem("s_a2lo"), 1)

            chain = sem("s_chain")
            nch = [0]

            def link(ins):
                nch[0] += 1
                ins.then_inc(chain, 1)
                dve.wait_ge(chain, nch[0])

            def softplus():
                dve.wait_ge(sem("s_vec"), 16)
                dve.wait_ge(sem("s_cl"), 2)
                link(nc.vector.tensor_tensor(gg[:], V("g_fin", 0, 8), V("g_ln1", 0, 8), ALU.mult))
                link(nc.vector.tensor_scalar(cl[:, 2], cl[:, 1], 2.0, None, ALU.add))
                link(nc.vector.reciprocal(cl[:, 3], cl[:, 2]))
                link(nc.vector.tensor_tensor(cl[:, 1], cl[:, 1], cl[:, 3], ALU.mult))
                link(nc.vector.tensor_tensor(cl[:, 2], cl[:, 1], cl[:, 1], ALU.mult))
                link(nc.vector.memset(cl[:, 3], 1.0 / 17))
                for i in range(7, -1, -1):
                    link(nc.vector.tensor_tensor(cl[:, 3], cl[:, 3], cl[:, 2], ALU.mult))
                    link(nc.vector.tensor_scalar(cl[:, 3], cl[:, 3], 1.0 / (2 * i + 1), None, ALU.add))
                link(nc.vector.tensor_tensor(cl[:, 3], cl[:, 3], cl[:, 1], ALU.mult))
                link(nc.vector.tensor_scalar(cl[:, 0], V("lam", 0, 16), -1.0, 0.0, ALU.mult, ALU.max))
                link(nc.vector.scalar_tensor_tensor(out=cl[:, 0], in0=cl[:, 3], scalar=2.0, in1=cl[:, 0],
                                                    op0=ALU.mult, op1=ALU.add))
                link(nc.vector.tensor_scalar(cl[:, 4], cl[:, 0], -2.0, None, ALU.mult))
                nc.vector.tensor_scalar(cl[:, 5], cl[:, 0], -4.0, None, ALU.mult).then_inc(sem("s_cldone"), 1)

            for k in range(KT):
                dve.wait_ge(sem("s_xh"), k + 1)
                nc.vector.scalar_tensor_tensor(out=a_lo[:, k], in0=res[:, k], scalar=V("g_mix", k),
                                               in1=a_hi[:, k].bitcast(F32), op0=ALU.mult, op1=ALU.subtract
                                               ).then_inc(sem("s_xl"), 1)
                if k == 0:
                    split_lo(dve, 0, 0, None)
            split_lo(dve, 1, 1, None)
            attention(1)
            st = STAGES["pool"]

            def z_in(z):
                i = z - 4
                split_lo(dve, st.u + i + 2, (st.u + i) % 2, st.t + i + 1)
                dve.wait_ge(s_mm, st.t + i + 1)
                nc.vector.tensor_tensor(res[0:PW, z], pair_flat(st.t + i, PW), rb[0:PW], ALU.mult).then_inc(s_outD, 1)

            z_in(4)
            dve.wait_ge(sem("s_rowc"), 3)
            link(nc.vector.tensor_tensor(mmin[:], mrow[:, 0], mrow[:, 1], ALU.min))
            link(nc.vector.tensor_tensor(mmin[:], mmin[:], mrow[:, 2], ALU.min))
            for g in range(3):
                nc.vector.tensor_tensor(mrow[:, g], mrow[:, g], mmin[:], ALU.subtract).then_inc(sem("s_rowd"), 1)
            st = STAGES["pool"]

            def weights(i):
                split_lo(dve, st.u + i + 2, (st.u + i) % 2, st.t + 4 + 2 * (i - 3))

            pooled(3)
            dve.wait_ge(sem("s_rowe"), 1)
            dve.wait_ge(sem("s_rowc"), 6)
            link(nc.vector.tensor_tensor(lrow[:], lrow[:], mrow[:], ALU.mult))
            link(nc.vector.tensor_tensor(den[:], lrow[:, 0], lrow[:, 1], ALU.add))
            link(nc.vector.tensor_tensor(den[:], den[:], lrow[:, 2], ALU.add))
            link(nc.vector.reciprocal(mmin[:], den[:]))
            z_in(5)
            for g in range(3):
                nc.vector.tensor_tensor(lrow[:, g], lrow[:, g], mmin[:], ALU.mult).then_inc(sem("s_wts"), 1)
            pooled(4)
            z_in(6)
            nb = 0
            for a in range(2):
                for c in range(2):
                    cs = slice(c * HC, (c + 1) * HC)
                    for g in range(3):
                        dve.wait_ge(sem("s_bcm"), nb + 1)
                        bc = pa[:, nb % 4]
                        dst = mg[:, a, cs] if g == 0 else mgt[:, g - 1]
                        nb += 1
                        nc.vector.tensor_tensor(dst, og[:, 2 * g + a, cs], bc, ALU.mult).then_inc(sem("s_bcu"), 1)
                        if nb == 6:
                            pooled(5)
                        if nb == 12:
                            pooled(6)
                        dve.wait_ge(sem("s_bcu"), nb)
                        if g:
                            ins = nc.vector.tensor_tensor(mg[:, a, cs], mg[:, a, cs], mgt[:, g - 1], ALU.add)
                            if g == 2:
                                ins.then_inc(sem("s_mgd"), 1)
                                dve.wait_ge(sem("s_mgd"), 2 * a + c + 1)
                            else:
                                link(ins)
            for a in range(2):
                dve.wait_ge(sem("s_a1hi"), a + 1)
                nc.vector.tensor_tensor(att1_lo[:, a], mg[:, a], att1_hi[:, a].bitcast(F32),
                                        ALU.subtract).then_inc(sem("s_a1lo"), 1)
            z_in(7)

            def pool_lo(z):
                dve.wait_ge(sem("s_plhi"), z + 1)
                nc.vector.tensor_tensor(b_lo[0:PW, z], res[0:PW, z], b_hi[0:PW, z].bitcast(F32),
                                        ALU.subtract).then_inc(sem("s_pllo"), 1)

            def mixed_lo(g):
                t = st.t + 4 + 2 * g
                weights(4 + g)
                for o in range(2):
                    dve.wait_ge(sem("s_pmhi"), 2 * g + o + 1)
                    nc.vector.scalar_tensor_tensor(
                        out=b_lo[0:PW, 2 * g + o], in0=group_out(g, o),
                        scalar=vec[0:PW, VEC["p_scale"] + 2 * g + o:VEC["p_scale"] + 2 * g + o + 1],
                        in1=b_hi[0:PW, 2 * g + o].bitcast(F32), op0=ALU.mult, op1=ALU.subtract).then_inc(s_outD, 1)

            for z in range(7):
                if z == 6:
                    pooled(7)
                pool_lo(z)
                if z in (3, 6):
                    mixed_lo(z // 3 - 1)
            pool_lo(7)
            mixed_lo(2)
            mixed_lo(3)
            st = STAGES["mrg1"]
            with dve.Fori(0, KT) as n:
                for o in range(4):
                    z, t1 = o // 2, st.t + 4 * n + o + 1
                    if o:
                        split_lo(dve, st.u + 4 * n + o + 2, (st.u + o) % 2, t1)
                    dve.wait_ge(s_mm, t1)
                    if o % 2 == 0:
                        if o == 0:
                            dve.wait_ge(sem("s_gsum"), n + 1)
                        nc.vector.tensor_tensor(zt[:, z], pair_flat(st.t + o), rb[:], ALU.mult).then_inc(s_outD, 1)
                        if o == 0:
                            split_lo(dve, st.u + 4 * n + 2, st.u % 2, t1)
                    else:
                        dve.wait_ge(sem("s_tanh"), 2 * n + z + 1)
                        nc.vector.scalar_tensor_tensor(out=zt[:, z], in0=zt[:, z], scalar=1.0,
                                                       in1=pair_flat(st.t + o), op0=ALU.add, op1=ALU.mult
                                                       ).then_inc(s_outD, 1)

            def out_stage(b):
                st = STAGES[f"out{b}"]
                for k in range(KT):
                    dve.wait_ge(sem(f"s_mhi{b}"), k + 1)
                    nc.vector.scalar_tensor_tensor(out=a_lo[:, k], in0=res[:, k], scalar=0.5,
                                                   in1=a_hi[:, k].bitcast(F32), op0=ALU.mult, op1=ALU.subtract
                                                   ).then_inc(sem(f"s_msplit{b}"), 1)
                for m in range(KT):
                    split_lo(dve, st.u + m + 2, m % 2, st.t + m + 1)
                    dve.wait_ge(s_mm, st.t + m + 1)
                    dve.wait_ge(sem(f"s_xr{b}{m % 2}"), 16 * (m // 2 + 1))
                    nc.vector.tensor_tensor(res[:, m], pair_flat(st.t + m), zt[:, m % 2], ALU.add).then_inc(s_outD, 1)
                    dve.wait_ge(sem(f"s_bhi{b}"), m + 1)
                    nc.vector.scalar_tensor_tensor(out=b_lo[:, m], in0=res[:, m],
                                                   scalar=V("g_mlp" if b == 1 else "g_ln2", m),
                                                   in1=b_hi[:, m].bitcast(F32), op0=ALU.mult, op1=ALU.subtract
                                                   ).then_inc(sem(f"s_blo{b}"), 1)
                    add_square(1 if b == 1 else 3, m)

            out_stage(1)

            def mlp(b):
                st = STAGES[f"mlp{b}"]
                s_hhi, s_hlo = sem(f"s_hhi{b}"), sem(f"s_hlo{b}")

                def hidden(u, t, tp, h0, slot):
                    for j in range(4):
                        split_lo(dve, u + j + 2, j % 2, t + j + 1)
                        dve.wait_ge(s_mm, t + j + 1)
                        nc.vector.scalar_tensor_tensor(out=zt[:, j % 2], in0=pair_flat(tp + j), scalar=0.0, in1=rb[:],
                                                       op0=ALU.max, op1=ALU.mult
                                                       ).then_inc(s_outD, 1)
                        dve.wait_ge(s_hhi, h0 + j + 1)
                        nc.vector.tensor_tensor(a_lo[:, 4 * slot + j], zt[:, j % 2], a_hi[:, 4 * slot + j].bitcast(F32),
                                                ALU.subtract).then_inc(s_hlo, 1)

                def down(u, t, tp, n=None):
                    for j in range(4):
                        for o in range(2):
                            m = 2 * j + o
                            if o == 1 and not (isinstance(u, int) and u + j + 2 >= N_UNITS):
                                split_lo(dve, u + j + 2, j % 2, t + 2 * j + 2)
                            dve.wait_ge(s_mm, t + m + 1)
                            nc.vector.tensor_tensor(res[:, m], pair_flat(tp + m), res[:, m], ALU.add
                                                    ).then_inc(s_outD, 1)
                            if n is not None:
                                add_square(n, m)
                                if b == 1 and m:
                                    dve.wait_ge(sem("s_sqg"), m + 1)
                                    if m > 1:
                                        dve.wait_ge(sem("s_sqgs"), m - 1)
                                    nc.vector.tensor_tensor(sqsum_g[:], sqsum_g[:], sq_g[:], ALU.add
                                                            ).then_inc(sem("s_sqgs"), 1)

                rms(1 if b == 1 else 3)
                dve.wait_ge(sem("s_rb"), b + 1)
                hidden(st.u, st.t, st.t, 0, 0)
                with dve.Fori(0, 3) as i:
                    for e in range(2):
                        hidden(st.u + 4 + 8 * e + 16 * i, st.t + 4 + 12 * e + 24 * i, st.t,
                               4 + 4 * e + 8 * i, 1 - e)
                        down(st.u + 8 + 8 * e + 16 * i, st.t + 8 + 12 * e + 24 * i, st.t)
                hidden(st.u + 52, st.t + 76, st.t, 28, 1)
                down(st.u + 56, st.t + 80, st.t)
                down(st.u + 60, st.t + 88, st.t, 2 if b == 1 else 4)

            mlp(1)
            two_norms()
            attention(2)

            st = STAGES["gat0"]
            for n in range(5):
                if n % 2 or n == 4:
                    split_lo(dve, st.u + n // 2 + 2, (st.u + n // 2) % 2, st.t + n + 1)
                dve.wait_ge(s_mm, st.t + n + 1)
                if n == 4:
                    dve.wait_ge(s_outA, st.a)
                tanh_ = zt[:, 0] if n == 4 else (tg01 if n < 2 else tg23)[:, n % 2]
                nc.vector.scalar_tensor_tensor(out=res[:, n], in0=tanh_, scalar=1.0,
                                               in1=pair_flat(st.t + n), op0=ALU.add, op1=ALU.mult
                                               ).then_inc(s_outD, 1)
            st = STAGES["gatt"]
            with dve.Fori(0, KT - 5) as n:
                for o in range(2):
                    split_lo(dve, st.u + 2 * n + o + 2, (st.u + o) % 2, st.t + 2 * n + o + 1)
                dve.wait_ge(s_outA, st.a + n + 1)
                nc.vector.scalar_tensor_tensor(out=res[:, bass.ds(5 + n, 1)].rearrange("p a b -> p (a b)"),
                                               in0=zt[:, 0], scalar=1.0,
                                               in1=pair_flat(st.t + 1), op0=ALU.add, op1=ALU.mult
                                               ).then_inc(s_outD, 1)

            st = STAGES["rec"]

            def conv(c):
                dve.wait_ge(s_outA, st.a + (1 if c == 0 else 3 + 6 * (c - 1)))
                if c >= 2:
                    dve.wait_ge(sem("s_rec"), c - 1)
                dst = uc[:, c % 2]
                w = [V("conv_w", 8 * j + c) for j in range(4)]
                link(nc.vector.tensor_scalar(dst, ur[c % 2][:, 0:S], w[0], V("conv_b", c), ALU.mult, ALU.add))
                for j in (1, 2, 3):
                    ins = nc.vector.scalar_tensor_tensor(out=dst, in0=ur[c % 2][:, j:j + S], scalar=w[j], in1=dst,
                                                         op0=ALU.mult, op1=ALU.add)
                    if j < 3:
                        link(ins)
                ins.then_inc(sem("s_conv"), 1)

            def direction(c, d):
                a, i = th[:, 2 * d], th[:, 2 * d + 1]
                dve.wait_ge(sem("s_dec"), 2 * c + d + 1)
                link(nc.vector.scalar_tensor_tensor(out=i, in0=i, scalar=1.0, in1=uc[:, c % 2],
                                                    op0=ALU.add, op1=ALU.mult))
                dve.wait_ge(sem("s_root"), 2 * c + d + 1)
                link(nc.vector.scalar_tensor_tensor(out=tm[:, d], in0=a, scalar=1.0, in1=tm[:, d],
                                                    op0=ALU.add, op1=ALU.mult))
                link(nc.vector.scalar_tensor_tensor(out=i, in0=i, scalar=0.5, in1=tm[:, d],
                                                    op0=ALU.mult, op1=ALU.mult))
                if d == 0:
                    ins = nc.vector.tensor_tensor_scan(tm[:, 0], a, i, 0.0, ALU.mult, ALU.add)
                else:
                    ins = nc.vector.tensor_tensor_scan(tm[:, 1, ::-1], a[:, ::-1], i[:, ::-1], 0.0, ALU.mult, ALU.add)
                ins.then_inc(sem("s_scan"), 1)

            def guards(c):
                dve.wait_ge(sem("s_gsq"), c + 1)
                nc.vector.tensor_scalar(gt[:], gt[:], 0.044715, 1.0, ALU.mult, ALU.add).then_inc(sem("s_gpoly"), 1)
                for d in range(2):
                    dve.wait_ge(sem("s_thr"), 3 * c + d + 1)
                    nc.vector.tensor_scalar(tm[:, d], tm[:, d], -1.0, 0.0, ALU.mult, ALU.max).then_inc(sem("s_neg"), 1)

            def gelu(c):
                dve.wait_ge(sem("s_thr"), 3 * c + 3)
                nc.vector.scalar_tensor_tensor(out=gt[:], in0=gt[:], scalar=1.0, in1=y_in[:, c % 2],
                                               op0=ALU.add, op1=ALU.mult).then_inc(sem("s_gelu"), 1)

            def output(c):
                dve.wait_ge(sem("s_dirs"), c + 1)
                dve.wait_ge(sem("s_gelu"), c + 1)
                nc.vector.scalar_tensor_tensor(out=rec[:, c], in0=gt[:], scalar=0.5, in1=tm[:, 0],
                                               op0=ALU.mult, op1=ALU.mult).then_inc(sem("s_rec"), 1)

            def unit_y(c):
                split_lo(dve, st.u + 3 + 3 * c, (st.u + 1 + 3 * c) % 2, st.t + 2 + 6 * c)

            def unit_u(c):
                split_lo(dve, st.u + 1 + 3 * c, (st.u - 1 + 3 * c) % 2, st.t + 3 + 6 * (c - 1))

            def unit_gates(c):
                split_lo(dve, st.u + 5 + 3 * c, (st.u + 1 + 3 * c) % 2, st.t + 7 + 6 * c)

            for i in range(2):
                nc.vector.memset(ur[i][:], 0.0).then_inc(sem("s_urpad"), 1)
            split_lo(dve, st.u + 2, st.u % 2, st.t + 1)
            conv(0)
            unit_y(0)
            unit_u(1)
            conv(1)
            unit_gates(0)
            for c in range(KT):
                guards(c)
                direction(c, 0)
                if c < KT - 1:
                    unit_y(c + 1)
                direction(c, 1)
                gelu(c)
                if c < KT - 1:
                    unit_u(c + 2)
                output(c)
                if c < KT - 2:
                    conv(c + 2)
                if c < KT - 1:
                    unit_gates(c + 1)
            st = STAGES["mrg2"]

            def rec_lo(n, k):
                dve.wait_ge(sem("s_rhi"), n + 1)
                nc.vector.tensor_tensor(r_lo[:, k], rec[:, k], r_hi[:, k].bitcast(F32), ALU.subtract
                                        ).then_inc(sem("s_rlo"), 1)

            def gated(t1, n, z):
                dve.wait_ge(s_outA, st.a + n)
                dve.wait_ge(s_mm, t1)
                nc.vector.scalar_tensor_tensor(out=zt[:, z], in0=zt[:, z], scalar=1.0,
                                               in1=pa[:, 2 * z:2 * z + 2].rearrange("p c n -> p (c n)"),
                                               op0=ALU.add, op1=ALU.mult).then_inc(sem("s_gz"), 1)
                dve.wait_ge(sem("s_gz"), n + 1)
                r = res[:, bass.ds(n, 1)].rearrange("p a b -> p (a b)")
                nc.vector.tensor_tensor(r, r, zt[:, z], ALU.add).then_inc(s_outD, 1)

            for n in range(3):
                rec_lo(n, REC_ORDER[n])
            split_lo(dve, st.u + 2, st.u % 2, st.t + 1)
            for n in range(3, KT):
                rec_lo(n, REC_ORDER[n])
            with dve.Fori(0, KT // 2 - 1) as i:
                for o in range(4):
                    t1 = st.t + 4 * i + o + 2
                    split_lo(dve, st.u + 4 * i + o + 3, (st.u + o + 1) % 2, t1)
                    if o >= 2:
                        gated(t1, 2 * i + o - 2, o - 2)
            for o in range(2):
                split_lo(dve, st.u + 15 + o, (st.u + 13 + o) % 2, st.t + 14 + o)
                gated(st.t + 14 + o, 6 + o, o)
            out_stage(2)
            mlp(2)
            rms(4)
            scale_tiles(4, V("g_lnf", 0, 8), "s_nrm2")

        @block.tensor
        def _(pe):
            def stats(n):
                if n == 0:
                    pe.wait_ge(sem("s_pc"), 1)
                    pe.wait_ge(sem("s_cst"), 16)
                pe.wait_ge(sem("s_sqs"), 7 * (n + 1))
                for i in range(8):
                    mm = nc.tensor.matmul(pa[:, 0, i:i + 1], sqsum[:, i * P:(i + 1) * P], ones[:, 0:1],
                                          start=True, stop=True)
                mm.then_inc(sem("s_stat"), 1)
                if n == 2:
                    pe.wait_ge(sem("s_sqgs"), 7)
                    for i in range(8):
                        mm = nc.tensor.matmul(pa[:, 1, i:i + 1], sqsum_g[:, i * P:(i + 1) * P], ones[:, 0:1],
                                              start=True, stop=True)
                    mm.then_inc(sem("s_statg"), 1)

            def broadcast(i, src=diag, bank=2):
                pe.wait_ge(sem("s_diag"), i + 1)
                for c in range(2):
                    mm = nc.tensor.matmul(pa[:, bank + c], ones[:],
                                          src[:, 4 * c:4 * c + 4].rearrange("p a n -> p (a n)"),
                                          start=True, stop=True)
                mm.then_inc(sem("s_bc"), 1)

            def enter(name):
                st = STAGES[name]
                if st.a:
                    pe.wait_ge(s_outA, st.a)
                if st.d:
                    pe.wait_ge(s_outD, st.d)
                return st

            def attention(b):
                st = STAGES[f"att{b}"]
                s_in, in0 = (sem("s_scaled"), 0) if b == 1 else (s_outA, st.a)
                vtok = vtok1 if b == 1 else vtok2
                sm, pt = (sm1, pt1) if b == 1 else (sm2, pt2)
                s_S, s_add, s_pn, s_T, s_pt, s_pv, s_oev, s_vt, s_vev = [sem(f"s_{x}{b}") for x in (
                    "S", "add", "pn", "T", "pt", "pv", "oev", "vt", "vev")]
                npair = NP_[b]
                nt = npair * UNITS_PER_PAIR
                batches = [0]

                def fill(m0, m1):
                    for i in range(m0, m1):
                        m, r = divmod(i, 48)
                        k, r = divmod(r, 6)
                        n, c = divmod(r, 2)
                        u, t = st.u + m, st.t + m
                        if k == 0 and r == 0:
                            pe.wait_ge(s_wlo, u + 1)
                            if m >= 2:
                                pe.wait_ge(s_outA, st.a + m - 1)
                        if m == 0 and r == 0:
                            if b == 1:
                                pe.wait_ge(sem("s_xl"), k + 1)
                            else:
                                pe.wait_ge(sem("s_nlo" if k % 2 else "s_nle"), k // 2 + 1)
                        w, x = ((w_hi, a_hi), (w_hi, a_lo), (w_lo, a_hi))[n]
                        mm = nc.tensor.matmul(pair(t)[:, c], w[:, u % 2, k * P:(k + 1) * P],
                                              x[:, k, c * HC:(c + 1) * HC], start=(k == 0 and n == 0),
                                              stop=(k == KT - 1 and n == 2))
                        if r == 5 and k == KT - 1:
                            mm.then_inc(s_mm, 1)

                def v_batch(n):
                    p, bt = divmod(n, VB[b])
                    pe.wait_ge(s_in, in0 + 3 * p + 1)
                    if n:
                        pe.wait_ge(s_vev, n)
                    for a in range(4):
                        if b == 1:
                            src = qkv1[:, p % 2, 0, (4 * bt + a) * P:(4 * bt + a + 1) * P]
                        else:
                            src = v2[:, bt, a * P:(a + 1) * P]
                        mm = nc.tensor.transpose(pa[:, 2, a * P:(a + 1) * P], src, ident)
                    mm.then_inc(s_vt, 1)
                    batches[0] = n + 1

                def scores(j):
                    p, idx = divmod(j, UNITS_PER_PAIR)
                    _, hh, i = tile_of(idx)
                    w = width(b, j)
                    rows = slice(64 * hh, 64 * hh + 64)
                    if idx == 0:
                        pe.wait_ge(s_in, in0 + 3 * p + 3)
                    if j >= 2:
                        pe.wait_ge(s_add, j - 1)
                    elif b == 2:
                        pe.wait_ge(sem("s_nrm1"), KT)
                    q, k = (qkv1[rows, p % 2, 1], qkv1[rows, p % 2, 2]) if b == 1 else (
                        qk2[rows, p % 2, 0], qk2[rows, p % 2, 1])
                    if b == 1:
                        lhsT = q[:, i * P:(i + 1) * P]
                        rhs = k[:, (i + 1) * P - w:(i + 1) * P]
                        out = pa[:, j % 2, 0:w]
                    else:
                        hf, n = divmod(i, 4)
                        lhsT = q[:, n * 256 + hf * 128:n * 256 + hf * 128 + 128]
                        c0 = COL_START[n]
                        rhs = k.rearrange("p (r c) -> p r c", c=64)[:, 4 * hf:4 * hf + 12, c0:c0 + 32]
                        out = pa[:, j % 2, 0:w].rearrange("p (r c) -> p r c", c=32)
                    nc.tensor.matmul(out, lhsT, rhs, start=True, stop=True).then_inc(s_S, 1)

                def transpose_probs(j):
                    w = width(b, j)
                    pe.wait_ge(s_pn, j + 1)
                    if j:
                        pe.wait_ge(s_pt, j)
                    pe.wait_ge(s_vev, batches[0])
                    for a in range(w // P):
                        mm = nc.tensor.transpose(pa[:, 2, a * P:(a + 1) * P], sm[:, j % 3, a * P:(a + 1) * P], ident)
                    mm.then_inc(s_T, 1)

                def values(j):
                    p, idx = divmod(j, UNITS_PER_PAIR)
                    _, hh, i = tile_of(idx)
                    nb = width(b, j) // P
                    pe.wait_ge(s_pt, j + 1)
                    if idx == 0:
                        pe.wait_ge(s_vev, VB[b] * (p + 1))
                    if idx % 4 == 0 and j >= 8:
                        pe.wait_ge(s_oev, j // 4 - 1)
                    for a in range(nb):
                        if b == 1:
                            blk = i - nb + 1 + a
                        else:
                            hf, n = divmod(i, 4)
                            blk = 4 * n + hf + a
                        mm = nc.tensor.matmul(pa[64 * hh:64 * hh + 64, 3, (i % 4) * P:(i % 4 + 1) * P],
                                              vtok[:, p % 2, blk, 64 * hh:64 * hh + 64],
                                              pt[:, j % 2, a * P:(a + 1) * P], start=(a == 0), stop=(a == nb - 1))
                    mm.then_inc(s_pv, 1)

                fill(0, 48)
                if b == 1:
                    stats(0)
                    fill(48, 78)
                    broadcast(0)
                    fill(78, 48 * 3)
                    pe.wait_ge(sem("s_rb"), 1)
                else:
                    fill(48, 48 * 3)
                    pe.wait_ge(sem("s_nd"), KT)
                for n in range(VB[b]):
                    v_batch(n)
                    fill(48 * 3 + 48 // VB[b] * n, 48 * 3 + 48 // VB[b] * (n + 1))
                for t in range(nt + 2):
                    p, idx = divmod(t, UNITS_PER_PAIR)
                    if t < nt:
                        scores(t)
                    if p + 1 < npair and V_STEP <= idx < V_STEP + VB[b]:
                        if t >= 2:
                            pe.wait_ge(s_pt, t - 1)
                        v_batch(VB[b] * (p + 1) + idx - V_STEP)
                    if t < nt:
                        fill(48 * AHEAD + FILL * t, 48 * AHEAD + FILL * (t + 1))
                    else:
                        fill(48 * AHEAD + FILL * nt + 24 * (t - nt), 48 * AHEAD + FILL * nt + 24 * (t - nt + 1))
                    if 1 <= t <= nt:
                        transpose_probs(t - 1)
                    if t >= 2:
                        values(t - 2)

            attention(1)
            pe.wait_ge(sem("s_oev1"), 4 * N_PAIR1)
            st = STAGES["pool"]

            def rows(n):
                st_, g = divmod(n, 3)
                if n >= 2:
                    pe.wait_ge(sem("s_rowc"), n - 1)
                src = negm if st_ == 0 else lsum
                for i in range(8):
                    mm = nc.tensor.matmul(pa[0:4, 2 * (n % 2) + i // 4, (i % 4) * P:(i % 4 + 1) * P],
                                          src[:, 32 * g + 4 * i:32 * g + 4 * i + 4], ident, start=True, stop=True)
                mm.then_inc(sem("s_row"), 1)

            def channels(z):
                i = z - 4
                if i >= 2:
                    pe.wait_ge(s_outD, st.d + i - 1)
                else:
                    pe.wait_ge(s_outA, st.a + i - 1)
                pe.wait_ge(s_wlo, st.u + i + 1)
                for k in range(KT):
                    mm = product((st.u + i) % 2, pair(st.t + i), a_hi, a_lo, k, k == 0, k == KT - 1, m=PW, wofs=k * P)
                    if k == KT - 1:
                        mm.then_inc(s_mm, 1)
                    if z == 7:
                        spread(4 + k)

            def spread(nb):
                a, r = divmod(nb, 6)
                c, g = divmod(r, 3)
                pe.wait_ge(sem("s_wts"), 3)
                if nb >= 4:
                    pe.wait_ge(sem("s_bcu"), nb - 3)
                nc.tensor.matmul(pa[:, nb % 4], sel[:, a], lrow[:, g, c * HC:(c + 1) * HC],
                                 start=True, stop=True).then_inc(sem("s_bcm"), 1)

            for n in range(6):
                rows(n)
            channels(5)
            channels(6)
            for nb in range(4):
                spread(nb)
            channels(7)
            for g in range(4):
                u, t = st.u + 4 + g, st.t + 4 + 2 * g
                pe.wait_ge(s_wlo, u + 1)
                for o in range(2):
                    if g >= 2:
                        pe.wait_ge(s_outD, st.d + 4 + 2 * (g - 2) + o + 1)
                    elif g == 0:
                        pe.wait_ge(s_outD, st.d + 3 + o)
                    out = pa[:, 2 * o:2 * o + 2] if g % 2 else pair(t + o)
                    for k in range(2):
                        pe.wait_ge(sem("s_pllo"), 2 * g + k + 1)
                        mm = product(u % 2, out, b_hi, b_lo, 2 * g + k, k == 0, k == 1, m=PW, kp=PW,
                                     wofs=(2 * k + o) * PW)
                    mm.then_inc(s_mm, 1)
            st = enter("mrg1")
            with pe.Fori(0, KT) as n:
                for o, (xh, xl, kw) in enumerate(((a_hi, a_lo, {}),
                                                  (att1_hi, att1_lo, {"nk": 2}),
                                                  (a_hi, a_lo, {}),
                                                  (b_hi, b_lo, {"kp": PW}))):
                    pe.wait_ge(s_outD, st.d + 4 * n + o - 1)
                    unit8(pe, st.u + 4 * n + o, (st.u + o) % 2, o % 2, xh, xl, **kw)

            def out_stage(b):
                st = enter(f"out{b}")
                for m in range(KT):
                    if m >= 2:
                        pe.wait_ge(s_outD, st.d + m - 1)
                    pe.wait_ge(s_wlo, st.u + m + 1)
                    for k in range(KT):
                        if m == 0:
                            pe.wait_ge(sem(f"s_msplit{b}"), k + 1)
                        mm = product(m % 2, pair(m), a_hi, a_lo, k, k == 0, k == KT - 1)
                    mm.then_inc(s_mm, 1)

            out_stage(1)

            def mlp(b):
                st = enter(f"mlp{b}")
                n_norm = 1 if b == 1 else 3
                s_hlo = sem(f"s_hlo{b}")

                def hidden(u, d, first=False):
                    for j in range(4):
                        if not first or j >= 2:
                            pe.wait_ge(s_outD, d + j - 1)
                        pe.wait_ge(s_wlo, u + j + 1)
                        for k in range(KT):
                            if first and j == 0:
                                pe.wait_ge(sem(f"s_blo{b}"), k + 1)
                            mm = product(j % 2, pair(j), b_hi, b_lo, k, k == 0, k == KT - 1)
                            if k == KT - 1:
                                mm.then_inc(s_mm, 1)
                            if first and j == 1 and k == 4:
                                broadcast(SPREADS[n_norm] - 1)
                        if first and j == 0:
                            stats(n_norm)

                def down(u, d, h, slot):
                    pe.wait_ge(s_hlo, h)
                    for j in range(4):
                        pe.wait_ge(s_wlo, u + j + 1)
                        for o in range(2):
                            m = 2 * j + o
                            pe.wait_ge(s_outD, d + m - 1)
                            for k in range(4):
                                mm = product(j % 2, pair(m), a_hi, a_lo, 4 * slot + k, k == 0, k == 3,
                                             wofs=(2 * k + o) * P)
                            mm.then_inc(s_mm, 1)

                hidden(st.u, st.d, True)
                with pe.Fori(0, 3) as i:
                    for e in range(2):
                        hidden(st.u + 4 + 8 * e + 16 * i, st.d + 4 + 12 * e + 24 * i)
                        down(st.u + 8 + 8 * e + 16 * i, st.d + 8 + 12 * e + 24 * i, 4 + 4 * e + 8 * i, e)
                hidden(st.u + 52, st.d + 76)
                down(st.u + 56, st.d + 80, 28, 0)
                down(st.u + 60, st.d + 88, 32, 1)

            mlp(1)
            stats(2)
            broadcast(2)
            broadcast(3, diag_r, 0)
            attention(2)
            st = enter("gat0")
            pe.wait_ge(sem("s_a2lo"), N_PAIR2)
            for j in range(2):
                pe.wait_ge(s_wlo, st.u + j + 1)
                for o in range(2):
                    if j:
                        pe.wait_ge(s_outD, st.d + o + 1)
                    for k in range(4):
                        mm = product((st.u + j) % 2, pair(st.t + 2 * j + o), att2_hi, att2_lo, k, k == 0, k == 3,
                                     wofs=(2 * k + o) * P)
                    mm.then_inc(s_mm, 1)
            pe.wait_ge(s_outD, st.d + 3)
            unit8(pe, st.u + 2, st.u % 2, st.t + 4, att2_hi, att2_lo, nk=4)
            st = STAGES["gatt"]
            with pe.Fori(0, KT - 5) as n:
                pe.wait_ge(s_outD, st.d + n - 1)
                pe.wait_ge(s_outA, st.a + n)
                unit8(pe, st.u + 2 * n, st.u % 2, st.t, a_hi, a_lo)
                pe.wait_ge(s_outD, st.d + n)
                unit8(pe, st.u + 2 * n + 1, (st.u + 1) % 2, st.t + 1, att2_hi, att2_lo, nk=4)
            st = enter("rec")

            def proj(c_out, u, t):
                if t - st.t >= 2:
                    pe.wait_ge(s_outA, st.a + t - st.t - 1)
                unit8(pe, u, u % 2, t, a_hi, a_lo)

            def gates(c, u, t):
                pe.wait_ge(s_wlo, u + 1)
                pe.wait_ge(sem("s_ul"), c + 1)
                for o in range(4):
                    pe.wait_ge(s_outA, st.a + t + o - st.t - 1)
                    mm = product(u % 2, pair(t + o), uh3, ul3, 0, True, True, wofs=o * P)
                    mm.then_inc(s_mm, 1)

            uh3 = uh[:].unsqueeze(1)
            ul3 = ul[:].unsqueeze(1)
            proj(0, st.u, st.t)
            for c in range(KT):
                proj(c, st.u + 1 + 3 * c, st.t + 1 + 6 * c)
                proj(c + 1, st.u + 2 + 3 * c, st.t + 2 + 6 * c)
                gates(c, st.u + 3 + 3 * c, st.t + 3 + 6 * c)
            st = STAGES["mrg2"]
            pe.wait_ge(s_outA, st.a - 1)
            unit8(pe, st.u, st.u % 2, st.t, a_hi, a_lo)

            def projected(u, slot, n, o):
                pe.wait_ge(s_outD, st.d + n - 1)
                pe.wait_ge(s_wlo, u + 1)
                for k in range(KT):
                    mm = product(slot, pa[:, 2 * o:2 * o + 2], r_hi, r_lo, k, k == 0, k == KT - 1)
                mm.then_inc(s_mm, 1)

            with pe.Fori(0, KT // 2 - 1) as i:
                for o in range(2):
                    pe.wait_ge(s_outA, st.a + 2 * i + o)
                    unit8(pe, st.u + 4 * i + o + 1, (st.u + o + 1) % 2, st.t + o + 1, a_hi, a_lo)
                pe.wait_ge(sem("s_rlo"), KT)
                for o in range(2):
                    projected(st.u + 4 * i + 3 + o, (st.u + 1 + o) % 2, 2 * i + o, o)
            for o in range(2):
                projected(st.u + 13 + o, (st.u + 1 + o) % 2, 6 + o, o)
            out_stage(2)
            mlp(2)
            stats(4)
            broadcast(5)


def tiles(w, n, width=P, rows=P):
    k = w.shape[0] // rows
    return w.reshape(k, rows, w.shape[1])[:, :, n * width:(n + 1) * width].transpose(1, 0, 2)


def weight_stream(i):
    out = np.zeros((P, N_UNITS, KT, P), np.float32)
    flat = out.reshape(P, N_UNITS, S)
    u = 0
    w = i["w_in"][0]
    for p in range(N_PAIR1):
        for c in (12, 0, 6):
            out[:, u] = tiles(w, c + p)
            u += 1
    for z in range(8):
        out[:, u, :, 0:PW] = tiles(w[:, 2304:3072], z, PW)
        u += 1
    for g in range(4):
        for k in range(2):
            for o in range(2):
                flat[0:PW, u, (2 * k + o) * PW:(2 * k + o + 1) * PW] = (
                    i["w_pool_grp"][0, g, k * PW:(k + 1) * PW, o * PW:(o + 1) * PW])
        u += 1
    for n in range(KT):
        out[:, u] = tiles(w, 24 + n)
        out[:, u + 1, 0:2] = tiles(i["w_att_out"][0], n)
        out[:, u + 2] = tiles(w, 32 + n)
        out[0:PW, u + 3] = tiles(i["w_pool_out"][0], n, rows=PW)
        u += 4
    u = mlp_units(out, u, i["w_out"][0], i["w_mlp_in"][0], i["w_mlp_out"][0])
    w = i["w_in_2"][0]
    for p in range(N_PAIR2):
        for c in (8, 0, 4):
            out[:, u] = tiles(w, c + p)
            u += 1
    for n in range(EXTRA + 1):
        out[:, u] = tiles(w, 28 + n)
        u += 1
    for j in range(2):
        out[:, u] = tiles(i["w_att_o_2"][0], j, 2 * P).reshape(P, KT, P)
        u += 1
    for n in range(EXTRA, KT):
        if n > EXTRA:
            out[:, u] = tiles(w, 28 + n)
            u += 1
        out[:, u, 0:4] = tiles(i["w_att_o_2"][0], n)
        u += 1
    out[:, u] = tiles(w, 12)
    u += 1
    for c in range(KT):
        out[:, u] = tiles(w, 20 + c)
        u += 1
        out[:, u] = tiles(w, 13 + c if c < KT - 1 else 36)
        u += 1
        for d in range(2):
            for g, name in enumerate(("w_rg_a_2", "w_rg_i_2")):
                for h in range(2):
                    r = slice(64 * h, 64 * h + 64)
                    out[r, u, 2 * d + g, r] = i[name][0, d, 2 * c + h]
        u += 1
    out[:, u] = tiles(w, 37)
    u += 1
    for n in range(0, KT, 2):
        if n < KT - 2:
            for o in range(2):
                out[:, u] = tiles(w, 38 + n + o)
                u += 1
        for o in range(2):
            out[:, u] = tiles(i["w_rec_o_2"][0], n + o)
            u += 1
    u = mlp_units(out, u, i["w_out_2"][0], i["w_ff1_2"][0], i["w_ff2_2"][0])
    return flat


def mlp_units(out, u, w_out, w1, w2):
    for n in range(KT):
        out[:, u] = tiles(w_out, n)
        u += 1

    def hidden(g, u):
        for j in range(4):
            out[:, u + j] = tiles(w1, 4 * g + j)
        return u + 4

    def down(g, u):
        for j in range(4):
            out[:, u + j] = tiles(w2[4 * g * P:4 * (g + 1) * P], j, 2 * P).reshape(P, KT, P)
        return u + 4

    u = hidden(0, u)
    for g in range(8):
        if g < 7:
            u = hidden(g + 1, u)
        u = down(g, u)
    return u


def columns(v):
    return v.reshape(-1, P).T


def packed_vectors(i):
    out = np.zeros((P, NVEC), np.float32)

    def put(name, a):
        out[0:a.shape[0], VEC[name]:VEC[name] + a.shape[1]] = a

    for name, key in (("g_mix", "norm_mix_g"), ("g_mlp", "norm_mlp_g"), ("g_ln1", "ln1_g_2"), ("g_ln2", "ln2_g_2"),
                      ("b_in", "b_in_2"), ("conv_b", "conv_b_2")):
        put(name, columns(i[key][0]))
    put("g_fin", columns(i["norm_final_g"]))
    put("g_lnf", columns(i["lnf_g_2"]))
    put("conv_w", columns(i["conv_w_2"][0].reshape(-1)))
    put("lam", columns(i["lru_lambda_2"][0].reshape(-1)))
    put("b_rg", columns(np.stack([i["b_rg_a_2"][0], i["b_rg_i_2"][0]], 1).reshape(-1)))
    put("p_scale", i["pool_scale"][0].reshape(8, PW).T)
    return out


def shape_constants():
    q = np.arange(P)[:, None]
    c = np.zeros((P, 832), np.float32)
    c[:, 0:128] = np.eye(P)
    step = P + q - np.arange(256)[None, :]
    c[:, 128:384] = np.where((step >= 0) & (step <= P), step, BIG)
    k = np.arange(P)[None, :]
    c[:, 384:512] = np.where((q // 64 == k // 64) & (q >= k), q - k, BIG)
    for h in range(4):
        c[h, 512 + 128 * (h // 2) + 64 * (h % 2):512 + 128 * (h // 2) + 64 * (h % 2) + 64] = 1.0
    for g, w in enumerate(WINDOWS):
        c[:, 768 + 16 * g:784 + 16 * g] = 1.0 / np.minimum(np.arange(16) + 1, w)
    return c


def neighbourhood_mask():
    out = np.full((P, 6, 12, 32), NEG, np.float32)
    for o, n in enumerate((0, 1, 3)):
        cs = (0, 8, 24, 32)[n]
        for hf in range(2):
            for r in range(8):
                row = 8 * hf + r
                rs = min(max(row - 4, 0), 8)
                for a in range(16):
                    qc = 16 * n + a
                    ws = min(max(qc - 8, 0), 48)
                    r0, c0 = rs - 4 * hf, ws - cs
                    out[16 * r + a, 2 * o + hf, r0:r0 + 8, max(c0, 0):c0 + 16] = 0.0
    return out.reshape(P, 6, 384)


def relative_bias(rpb):
    h = rpb.shape[0]
    pad = np.zeros((h, 15 + 8, 31 + 32), np.float32)
    pad[:, 4:19, 16:47] = rpb
    out = np.zeros((h // 2, 8, 16, 3, 2, 16, 32), np.float32)
    for r in range(8):
        for a in range(16):
            for o, s in enumerate((0, -8, -16)):
                c0 = s - a + 31
                out[:, r, a, o] = pad[:, 7 - r:23 - r, c0:c0 + 32].reshape(h // 2, 2, 16, 32)
    return out.reshape(h // 2, P, 6, HC)


def kernel(**inputs):
    import concourse.bacc as bacc
    from concourse.bass_utils import run_bass_kernel_spmd

    i = {k: np.ascontiguousarray(v) for k, v in inputs.items()}
    arrays = {
        "xT": np.ascontiguousarray(i["x"][0].T),
        "wstream": weight_stream(i),
        "vecs": packed_vectors(i),
        "consts": shape_constants(),
        "mask2": neighbourhood_mask(),
        "bias2": relative_bias(i["rpb_2"][0]),
    }
    nc = bacc.Bacc("TRN2", target_bir_lowering=False, num_devices=1, dynamic_dma_scratch_size=4096)
    args = [nc.dram_tensor(n, a.shape, F32, kind="ExternalInput").ap() for n, a in arrays.items()]
    args.append(nc.dram_tensor("outT", (D, S), F32, kind="ExternalOutput").ap())
    args.append(nc.dram_tensor("x2", (D, S), F32, kind="Internal").ap())
    build(nc, *args)
    r = run_bass_kernel_spmd(nc, [arrays], core_ids=[0])
    return np.ascontiguousarray(np.asarray(r.results[0]["outT"]).T).reshape(1, S, D)
```
